# Optimizing a Trainium2 kernel written in Bass

```python
import jax, jax.numpy as jnp
from jax import lax
import numpy as np

D_MODEL = 1024
BATCH = 1
SEQ = 1024
DEPTH = 1

MEM_LEN = 256
EPS = 1e-6

SB_HEADS = 16
SB_HEAD_DIM = 64
SB_WIDTH = SB_HEADS * SB_HEAD_DIM
SB_BLOCK = 128

SSD_EXPAND = 2
SSD_INNER = SSD_EXPAND * D_MODEL
SSD_HEAD_DIM = 64
SSD_HEADS = SSD_INNER // SSD_HEAD_DIM
SSD_GROUPS = 4
SSD_HEADS_PER_GROUP = SSD_HEADS // SSD_GROUPS
SSD_STATE = 128
SSD_CONV = 4
SSD_CHUNK = 128
SSD_CONV_DIM = SSD_INNER + 2 * SSD_GROUPS * SSD_STATE

MEM_HEADS = 4
MEM_HEAD_DIM = 256
MEM_WIDTH = MEM_HEADS * MEM_HEAD_DIM

N_BRANCHES = 3
D_FF = 4 * D_MODEL

IN_SIZES = (3 * SB_WIDTH, SSD_INNER, SSD_CONV_DIM, SSD_HEADS, MEM_WIDTH, N_BRANCHES * D_MODEL)
D_IN_PROJ = int(sum(IN_SIZES))
SPLIT_POINTS = tuple(int(v) for v in np.cumsum(IN_SIZES)[:-1])

kernel_name = "hybrid_gated_stickbreak_ssd_memxattn_block"

def rms_norm(x, gain):
    xf = x.astype(jnp.float32)
    y = xf * lax.rsqrt(jnp.mean(xf * xf, axis=-1, keepdims=True) + EPS)
    return (y * gain.astype(jnp.float32)).astype(x.dtype)

def stick_breaking_attention(q, k, v):
    b, h, s, dh = q.shape
    nb = s // SB_BLOCK
    scale = dh ** -0.5
    qb = q.reshape(b, h, nb, SB_BLOCK, dh).transpose(2, 0, 1, 3, 4)
    key_pos = jnp.arange(s)

    def block(args):
        q_blk, blk_idx = args
        q_pos = blk_idx * SB_BLOCK + jnp.arange(SB_BLOCK)
        z = jnp.einsum("bhqd,bhkd->bhqk", q_blk, k).astype(jnp.float32) * scale
        causal = key_pos[None, :] < q_pos[:, None]
        log_beta = jax.nn.log_sigmoid(z)
        log_keep = jnp.where(causal, jax.nn.log_sigmoid(-z), 0.0)
        suffix = lax.cumsum(log_keep, axis=3, reverse=True) - log_keep
        w = jnp.where(causal, jnp.exp(log_beta + suffix), 0.0)
        return jnp.einsum("bhqk,bhkd->bhqd", w.astype(v.dtype), v)

    out = lax.map(block, (qb, jnp.arange(nb)))
    return out.transpose(1, 2, 0, 3, 4).reshape(b, h, s, dh)

def causal_depthwise_conv(x, w, bias):
    kw, c = w.shape
    y = lax.conv_general_dilated(
        x, w[:, None, :].astype(x.dtype), window_strides=(1,), padding=((kw - 1, 0),),
        dimension_numbers=("NWC", "WIO", "NWC"), feature_group_count=c)
    return y + bias.astype(x.dtype)

def ssd_chunked(xh, dt, a, bmat, cmat):
    b, s, g, r, p = xh.shape
    n = bmat.shape[-1]
    l = SSD_CHUNK
    c = s // l
    x = (xh * dt[..., None]).reshape(b, c, l, g, r, p)
    da = (dt.astype(jnp.float32) * a.astype(jnp.float32)).reshape(b, c, l, g, r)
    bm = bmat.reshape(b, c, l, g, n)
    cm = cmat.reshape(b, c, l, g, n)
    a_cs = jnp.cumsum(da, axis=2).transpose(0, 1, 3, 4, 2)

    tri = jnp.tril(jnp.ones((l, l), dtype=bool))
    seg = a_cs[..., :, None] - a_cs[..., None, :]
    decay = jnp.exp(jnp.where(tri, seg, -jnp.inf))
    cb = jnp.einsum("bclgn,bcsgn->bcgls", cm, bm).astype(jnp.float32)
    w_intra = cb[:, :, :, None] * decay
    y_diag = jnp.einsum("bcgrls,bcsgrp->bclgrp", w_intra, x.astype(jnp.float32))

    decay_to_end = jnp.exp(a_cs[..., -1:] - a_cs)
    states = jnp.einsum("bcsgn,bcgrs,bcsgrp->bcgrpn", bm.astype(jnp.float32), decay_to_end,
                        x.astype(jnp.float32))
    chunk_decay = jnp.exp(a_cs[..., -1])

    def step(hstate, inp):
        st, dec = inp
        return hstate * dec[..., None, None] + st, hstate

    h0 = jnp.zeros((b, g, r, p, n), jnp.float32)
    _, prev = lax.scan(step, h0, (states.transpose(1, 0, 2, 3, 4, 5), chunk_decay.transpose(1, 0, 2, 3)))
    prev = prev.transpose(1, 0, 2, 3, 4, 5)
    y_off = jnp.einsum("bclgn,bcgrpn,bcgrl->bclgrp", cm.astype(jnp.float32), prev, jnp.exp(a_cs))
    return (y_diag + y_off).reshape(b, s, g, r, p).astype(xh.dtype)

def ssd_branch(z, xbc_raw, dt_raw, conv_w, conv_b, dt_bias, a_log, d_skip, ssd_norm):
    b, s, _ = z.shape
    xbc = jax.nn.silu(causal_depthwise_conv(xbc_raw, conv_w, conv_b))
    xs, bmat, cmat = jnp.split(xbc, (SSD_INNER, SSD_INNER + SSD_GROUPS * SSD_STATE), axis=-1)
    xh = xs.reshape(b, s, SSD_GROUPS, SSD_HEADS_PER_GROUP, SSD_HEAD_DIM)
    bmat = bmat.reshape(b, s, SSD_GROUPS, SSD_STATE)
    cmat = cmat.reshape(b, s, SSD_GROUPS, SSD_STATE)
    dt = jax.nn.softplus((dt_raw + dt_bias).astype(jnp.float32)).astype(xs.dtype)
    dt = dt.reshape(b, s, SSD_GROUPS, SSD_HEADS_PER_GROUP)
    a = -jnp.exp(a_log.astype(jnp.float32)).reshape(SSD_GROUPS, SSD_HEADS_PER_GROUP)
    d = d_skip.reshape(SSD_GROUPS, SSD_HEADS_PER_GROUP)
    y = ssd_chunked(xh, dt, a, bmat, cmat) + d[..., None] * xh
    y = y.reshape(b, s, SSD_INNER) * jax.nn.silu(z)
    yg = y.reshape(b, s, SSD_GROUPS, SSD_INNER // SSD_GROUPS).astype(jnp.float32)
    yg = yg * lax.rsqrt(jnp.mean(yg * yg, axis=-1, keepdims=True) + EPS)
    return (yg.reshape(b, s, SSD_INNER) * ssd_norm.astype(jnp.float32)).astype(z.dtype)

def mem_cross_attention(q, mem, norm_mem, w_mem_kv):
    b, s, _ = q.shape
    m = mem.shape[1]
    kv = rms_norm(mem, norm_mem) @ w_mem_kv
    k, v = jnp.split(kv, 2, axis=-1)
    qh = q.reshape(b, s, MEM_HEADS, MEM_HEAD_DIM)
    kh = k.reshape(b, m, MEM_HEADS, MEM_HEAD_DIM)
    vh = v.reshape(b, m, MEM_HEADS, MEM_HEAD_DIM)
    scores = jnp.einsum("bshd,bmhd->bhsm", qh, kh).astype(jnp.float32) * (MEM_HEAD_DIM ** -0.5)
    probs = jax.nn.softmax(scores, axis=-1).astype(v.dtype)
    return jnp.einsum("bhsm,bmhd->bshd", probs, vh).reshape(b, s, MEM_WIDTH)

def setup_inputs(seed: int = 0) -> dict:
    key = jax.random.key(seed)
    ks = jax.random.split(key, 24)
    nrm = jax.random.normal
    f32 = jnp.float32

    def gain(k, n):
        return 1.0 + 0.05 * nrm(k, (DEPTH, n), f32)

    dt0 = jnp.exp(jax.random.uniform(ks[6], (DEPTH, SSD_HEADS), f32, minval=np.log(1e-3), maxval=np.log(1e-1)))
    dt_bias = dt0 + jnp.log(-jnp.expm1(-dt0))
    return {
        "x": nrm(ks[0], (BATCH, SEQ, D_MODEL), f32),
        "mem": nrm(ks[1], (BATCH, MEM_LEN, D_MODEL), f32),
        "norm_mix_pre": gain(ks[2], D_MODEL),
        "w_in": nrm(ks[3], (DEPTH, D_MODEL, D_IN_PROJ), f32) * D_MODEL ** -0.5,
        "conv_w": nrm(ks[4], (DEPTH, SSD_CONV, SSD_CONV_DIM), f32) * SSD_CONV ** -0.5,
        "conv_b": 0.02 * nrm(ks[5], (DEPTH, SSD_CONV_DIM), f32),
        "dt_bias": dt_bias,
        "a_log": jnp.log(jax.random.uniform(ks[7], (DEPTH, SSD_HEADS), f32, minval=1.0, maxval=16.0)),
        "d_skip": 1.0 + 0.1 * nrm(ks[8], (DEPTH, SSD_HEADS), f32),
        "ssd_norm": gain(ks[9], SSD_INNER),
        "norm_mem": gain(ks[10], D_MODEL),
        "w_mem_kv": nrm(ks[11], (DEPTH, D_MODEL, 2 * MEM_WIDTH), f32) * D_MODEL ** -0.5,
        "w_sb_out": nrm(ks[12], (DEPTH, SB_WIDTH, D_MODEL), f32) * SB_WIDTH ** -0.5,
        "w_ssd_out": nrm(ks[13], (DEPTH, SSD_INNER, D_MODEL), f32) * SSD_INNER ** -0.5,
        "w_mem_out": nrm(ks[14], (DEPTH, MEM_WIDTH, D_MODEL), f32) * MEM_WIDTH ** -0.5,
        "w_o": nrm(ks[15], (DEPTH, D_MODEL, D_MODEL), f32) * D_MODEL ** -0.5,
        "norm_mix_post": gain(ks[16], D_MODEL),
        "norm_mlp_pre": gain(ks[17], D_MODEL),
        "w_up": nrm(ks[18], (DEPTH, D_MODEL, D_FF), f32) * D_MODEL ** -0.5,
        "w_down": nrm(ks[19], (DEPTH, D_FF, D_MODEL), f32) * D_FF ** -0.5,
        "norm_mlp_post": gain(ks[20], D_MODEL),
    }

def reference(x, mem, norm_mix_pre, w_in, conv_w, conv_b, dt_bias, a_log, d_skip, ssd_norm,
              norm_mem, w_mem_kv, w_sb_out, w_ssd_out, w_mem_out, w_o, norm_mix_post,
              norm_mlp_pre, w_up, w_down, norm_mlp_post):
    b, s, _ = x.shape
    h = x
    for layer in range(DEPTH):
        u = rms_norm(h, norm_mix_pre[layer])
        proj = u @ w_in[layer]
        sb_qkv, z, xbc_raw, dt_raw, mem_q, gate_logits = jnp.split(proj, SPLIT_POINTS, axis=-1)

        q, k, v = jnp.split(sb_qkv, 3, axis=-1)
        to_heads = lambda t: t.reshape(b, s, SB_HEADS, SB_HEAD_DIM).transpose(0, 2, 1, 3)
        y_sb = stick_breaking_attention(to_heads(q), to_heads(k), to_heads(v))
        y_sb = y_sb.transpose(0, 2, 1, 3).reshape(b, s, SB_WIDTH)

        y_ssd = ssd_branch(z, xbc_raw, dt_raw, conv_w[layer], conv_b[layer], dt_bias[layer],
                           a_log[layer], d_skip[layer], ssd_norm[layer])

        y_mem = mem_cross_attention(mem_q, mem, norm_mem[layer], w_mem_kv[layer])

        gates = jax.nn.sigmoid(gate_logits.astype(jnp.float32)).astype(h.dtype)
        gates = gates.reshape(b, s, N_BRANCHES, D_MODEL)
        merged = (gates[:, :, 0] * (y_sb @ w_sb_out[layer])
                  + gates[:, :, 1] * (y_ssd @ w_ssd_out[layer])
                  + gates[:, :, 2] * (y_mem @ w_mem_out[layer]))
        mix = merged @ w_o[layer]
        h = h + rms_norm(mix, norm_mix_post[layer])

        u = rms_norm(h, norm_mlp_pre[layer])
        ff = jnp.square(jax.nn.relu(u @ w_up[layer])) @ w_down[layer]
        h = h + rms_norm(ff, norm_mlp_post[layer])
    return h


_drawn_inputs = setup_inputs


def setup_inputs(seed=0):
    import zlib

    import numpy as np

    out = dict(_drawn_inputs(seed))
    spreads = {}
    factors = {'conv_b': 16.615, 'norm_mem': 8.0, 'd_skip': 7.632, 'ssd_norm': 8.0}
    for name, (base, spread) in spreads.items():
        noise = np.random.default_rng([zlib.crc32(name.encode()), seed]).standard_normal(out[name].shape)
        drawn = base * np.exp(spread * noise) if base else spread * noise
        out[name] = __import__('jax').numpy.asarray(drawn.astype(out[name].dtype))
    for name, factor in factors.items():
        out[name] = (out[name] * factor).astype(out[name].dtype)
    return out
```

```python
from contextlib import ExitStack, contextmanager

import concourse.bass as bass
from concourse import mybir

F32 = mybir.dt.float32
F32R = mybir.dt.float32r
ALU = mybir.AluOpType
ACT = mybir.ActivationFunctionType
AX_X = mybir.AxisListType.X

P = 128
D = 1024
KB = D // P
S = 1024
TB = S // P
HALF = 512
M = 256
MB = M // P
EPS = 1e-6

SB_PAIRS = 8
SSD_HEADS, GROUPS, HPG = 32, 4, 8
GB = 4
MEM_HEADS = 4
MEM_SCALE = 256.0 ** -0.5
CONV = 4

Q0, K0, V0, Z0, X0, B0, C0, MQ0, G0, N_IN = 0, 8, 16, 24, 40, 56, 60, 64, 72, 96
Y_SB, Y_SSD, Y_MEM, N_Y = 0, 8, 24, 32
FF_CHUNKS = 4


@contextmanager
def stage(nc):
    with nc.cleanup_on_exit(), ExitStack() as ctx:
        yield ctx


def split3(hi, lo):
    (ah, bh), (al, bl) = hi, lo
    return ((ah, bh), (ah, bl), (al, bh))


def norm_to_feature_major(nc, name, src, tokens, gain, xh, xl, consts):
    n_pairs = tokens // P // 2
    with stage(nc) as ctx:
        def sb(n, shape, dt=F32):
            return ctx.enter_context(nc.sbuf_tensor(f"{name}_{n}", shape, dt))

        def sem(n):
            return nc.alloc_semaphore(f"{name}_{n}")

        x_tile, u, square = sb("x", [P, 2, D]), sb("u", [P, 2, D]), sb("sq", [P, D])
        scaled = sb("scaled", [P, 2, D])
        sums, root, rstd = sb("sums", [P, 2]), sb("root", [P, 2]), sb("rstd", [P, 2])
        gains = sb("gain", [P, KB])
        turned = ctx.enter_context(nc.psum_tensor(f"{name}_ps", [P, 2, D], F32))
        gain_loaded = sem("gain_loaded")
        loaded = [sem(f"loaded{s}") for s in range(2)]
        summed, rooted, inverted = sem("summed"), sem("rooted"), sem("inverted")
        normed = [sem(f"normed{s}") for s in range(2)]
        turned_done = [sem(f"turned{s}") for s in range(2)]
        gained = [sem(f"gained{s}") for s in range(2)]
        hi_done = [sem(f"hi{s}") for s in range(2)]
        lo_done = [sem(f"lo{s}") for s in range(2)]

        block = ctx.enter_context(nc.Block())

        @block.sync
        def _(sp):
            sp.dma_start(gains[:], gain).then_inc(gain_loaded, 16)
            with sp.Fori(0, n_pairs) as i:
                for s in range(2):
                    sp.wait_ge(normed[s], i)
                    sp.dma_start(x_tile[:, s], src[bass.ds(i * 256 + s * P, P), :]).then_inc(loaded[s], 16)

        @block.scalar
        def _(act):
            with act.Fori(0, n_pairs) as i:
                for s in range(2):
                    act.wait_ge(loaded[s], i * 16 + 16)
                    nc.scalar.activation(square[:], x_tile[:, s], ACT.Square,
                                         accum_out=sums[:, s:s + 1]).then_inc(summed, 1)
                    act.wait_ge(summed, i * 2 + s + 1)
                    act.wait_ge(normed[s], i)
                    nc.scalar.activation(root[:, s:s + 1], sums[:, s:s + 1], ACT.Sqrt, scale=1.0 / D,
                                         bias=consts["eps"][:]).then_inc(rooted, 1)
                for s in range(2):
                    act.wait_ge(gained[s], i + 1)
                    act.wait_ge(lo_done[s], i)
                    nc.scalar.activation(xh[:, :, bass.ds(i * 256 + s * P, P)],
                                         scaled[:, s].rearrange("p (k t) -> p k t", k=KB),
                                         ACT.Copy).then_inc(hi_done[s], 1)

        @block.vector
        def _(dve):
            dve.wait_ge(gain_loaded, 16)
            with dve.Fori(0, n_pairs) as i:
                for s in range(2):
                    dve.wait_ge(rooted, i * 2 + s + 1)
                    nc.vector.reciprocal(rstd[:, s:s + 1], root[:, s:s + 1]).then_inc(inverted, 1)
                    dve.wait_ge(inverted, i * 2 + s + 1)
                    dve.wait_ge(turned_done[s], i)
                    nc.vector.tensor_scalar(u[:, s], x_tile[:, s], rstd[:, s:s + 1], None,
                                            ALU.mult).then_inc(normed[s], 1)
                for s in range(2):
                    dve.wait_ge(turned_done[s], i + 1)
                    dve.wait_ge(lo_done[s], i)
                    nc.vector.tensor_tensor(
                        scaled[:, s].rearrange("p (k t) -> p k t", k=KB),
                        turned[:, s].rearrange("p (k t) -> p k t", k=KB),
                        gains[:, :, None].broadcast_to([P, KB, P]), ALU.mult).then_inc(gained[s], 1)
                for s in range(2):
                    dve.wait_ge(hi_done[s], i + 1)
                    dve.wait_ge(gained[s], i + 1)
                    hi = xh[:, :, bass.ds(i * 256 + s * P, P)].bitcast(F32)
                    nc.vector.tensor_tensor(xl[:, :, bass.ds(i * 256 + s * P, P)],
                                            scaled[:, s].rearrange("p (k t) -> p k t", k=KB), hi,
                                            ALU.subtract).then_inc(lo_done[s], 1)

        @block.tensor
        def _(pe):
            with pe.Fori(0, n_pairs) as i:
                for s in range(2):
                    pe.wait_ge(normed[s], i + 1)
                    pe.wait_ge(gained[s], i)
                    for k in range(KB):
                        last = nc.tensor.transpose(turned[:, s, k * P:(k + 1) * P], u[:, s, k * P:(k + 1) * P],
                                                   consts["ident"][:])
                    last.then_inc(turned_done[s], 1)


class Ring:

    def __init__(self, nc, ctx, name, consts):
        self.ones = consts["one"]
        self.raw = ctx.enter_context(nc.sbuf_tensor(f"{name}_w", [P, 2, D], F32))
        self.hi = ctx.enter_context(nc.sbuf_tensor(f"{name}_wh", [P, 2, KB, P], F32R))
        self.lo = ctx.enter_context(nc.sbuf_tensor(f"{name}_wl", [P, 2, KB, P], F32R))
        s = [nc.alloc_semaphore(f"{name}_{n}{i}") for n in ("loaded", "hi", "split", "used")
             for i in range(2)]
        self.loaded, self.hi_done, self.split, self.used = s[0:2], s[2:4], s[4:6], s[6:8]


def load_weights(sp, ring, w, i, s, row):
    sp.wait_ge(ring.split[s], i)
    sp.dma_start(ring.raw[:, s], w[bass.ds(row, 1)].rearrange("a p n -> (a p) n")).then_inc(ring.loaded[s], 16)


def split_weights(nc, pool, ring, i, s):
    pool.wait_ge(ring.loaded[s], i * 16 + 16)
    pool.wait_ge(ring.used[s], i)
    flat = "p k n -> p (k n)"
    nc.gpsimd.tensor_tensor(ring.hi[:, s].rearrange(flat), ring.raw[:, s], ring.ones[:].broadcast_to([P, D]),
                            ALU.mult).then_inc(ring.hi_done[s], 1)
    pool.wait_ge(ring.hi_done[s], i + 1)
    nc.gpsimd.tensor_tensor(ring.lo[:, s].rearrange(flat), ring.raw[:, s],
                            ring.hi[:, s].rearrange(flat).bitcast(F32), ALU.subtract).then_inc(ring.split[s], 1)


def product(nc, ring, s, xh, xl, out, tokens):
    n = min(tokens, HALF)
    for h in range(tokens // n):
        for k in range(KB):
            for j, (w, x) in enumerate(split3((ring.hi, xh), (ring.lo, xl))):
                last = nc.tensor.matmul(out[:, h * n:(h + 1) * n], w[:, s, k], x[:, k, h * n:(h + 1) * n],
                                        start=(k == 0 and j == 0), stop=(k == KB - 1 and j == 2))
    return last


def input_projection(nc, w_in, w_dt, conv_w, conv_b, proj, dt_bias, a_log, dt_out, da_out, xh, xl, consts):
    with stage(nc) as ctx:
        def sb(n, shape, dt=F32):
            return ctx.enter_context(nc.sbuf_tensor(f"in_{n}", shape, dt))

        def sem(n):
            return nc.alloc_semaphore(f"in_{n}")

        ring = Ring(nc, ctx, "in", consts)
        n_conv = C0 + GROUPS - X0
        out_tile = sb("out", [P, 2, S])
        padded = sb("padded", [P, 2, CONV - 1 + S])
        conv = sb("conv", [P, 2, S])
        cw, cb = sb("cw", [P, n_conv, CONV]), sb("cb", [P, n_conv])
        wd, wdh, wdl = sb("wd", [P, KB, 32]), sb("wdh", [P, KB, 32], F32R), sb("wdl", [P, KB, 32], F32R)
        bias_row, a_row = sb("bias", [P, 32]), sb("a", [P, 32])
        raw, capped, soft = (sb(n, [P, TB, 32]) for n in ("dtraw", "dtcap", "dtsoft"))
        ps = ctx.enter_context(nc.psum_tensor("in_ps", [P, 2, S], F32))
        ps_dt = ctx.enter_context(nc.psum_tensor("in_psdt", [P, TB, 32], F32))
        small_loaded, wd_hi, wd_split, dt_done = sem("small"), sem("wdhi"), sem("wdsplit"), sem("dtdone")
        dt_dve, dt_act = sem("dtdve"), sem("dtact")
        evacuated = [sem(f"evac{s}") for s in range(2)]
        stored = [sem(f"stored{s}") for s in range(2)]
        padded_done = [sem(f"padded{s}") for s in range(2)]
        conv_step = [sem(f"convstep{s}") for s in range(2)]
        zeroed = sem("zeroed")

        block = ctx.enter_context(nc.Block())

        @block.sync
        def _(sp):
            for dst, src in ((cw, conv_w), (cb, conv_b), (wd, w_dt), (bias_row, dt_bias), (a_row, a_log)):
                sp.dma_start(dst[:], src).then_inc(small_loaded, 16)
            for s in range(2):
                load_weights(sp, ring, w_in, 0, s, s)
            with sp.Fori(0, N_IN // 2 - 1) as i:
                for s in range(2):
                    load_weights(sp, ring, w_in, i + 1, s, i * 2 + s + 2)
                    sp.wait_ge(evacuated[s], i + 1)
                    sp.dma_start(proj[bass.ds(i * 2 + s, 1)].rearrange("a p n -> (a p) n"),
                                 out_tile[:, s]).then_inc(stored[s], 16)
            for s in range(2):
                sp.wait_ge(evacuated[s], N_IN // 2)
                sp.dma_start(proj[N_IN - 2 + s], out_tile[:, s]).then_inc(stored[s], 16)
            for s in range(2):
                sp.wait_ge(stored[s], 16 * N_IN // 2)

        @block.gpsimd
        def _(pool):
            pool.wait_ge(small_loaded, 80)
            nc.gpsimd.tensor_copy(wdh[:], wd[:]).then_inc(wd_hi, 1)
            pool.wait_ge(wd_hi, 1)
            nc.gpsimd.tensor_tensor(wdl[:], wd[:], wdh[:].bitcast(F32), ALU.subtract).then_inc(wd_split, 1)
            with pool.Fori(0, N_IN // 2) as i:
                for s in range(2):
                    split_weights(nc, pool, ring, i, s)

        @block.tensor
        def _(pe):
            pe.wait_ge(wd_split, 1)
            for t in range(TB):
                for k in range(KB):
                    for j, (x, w) in enumerate(split3((xh, wdh), (xl, wdl))):
                        last = nc.tensor.matmul(ps_dt[:, t], x[:, k, t * P:(t + 1) * P], w[:, k],
                                                start=(k == 0 and j == 0), stop=(k == KB - 1 and j == 2))
            last.then_inc(dt_done, 1)
            with pe.Fori(0, N_IN // 2) as i:
                for s in range(2):
                    pe.wait_ge(ring.split[s], i + 1)
                    pe.wait_ge(evacuated[s], i)
                    product(nc, ring, s, xh, xl, ps[:, s], S).then_inc(ring.used[s], 1)

        def evacuate(act, first, end, func):
            with act.Fori(first, end) as i:
                for s in range(2):
                    act.wait_ge(ring.used[s], i + 1)
                    act.wait_ge(stored[s], i * 16)
                    nc.scalar.activation(out_tile[:, s], ps[:, s], func).then_inc(evacuated[s], 1)

        @block.scalar
        def _(act):
            act.wait_ge(dt_dve, 2)
            nc.scalar.activation(soft[:], capped[:], ACT.Exp).then_inc(dt_act, 1)
            act.wait_ge(dt_act, 1)
            nc.scalar.activation(soft[:], soft[:], ACT.Ln, bias=consts["one"][:]).then_inc(dt_act, 1)
            nc.scalar.activation(a_row[:], a_row[:], ACT.Exp).then_inc(dt_act, 1)
            evacuate(act, 0, Z0 // 2, ACT.Copy)
            evacuate(act, Z0 // 2, X0 // 2, ACT.Silu)
            act.wait_ge(zeroed, 1)
            with act.Fori(X0 // 2, MQ0 // 2) as i:
                for s in range(2):
                    act.wait_ge(ring.used[s], i + 1)
                    act.wait_ge(conv_step[s], (i - X0 // 2) * CONV)
                    nc.scalar.activation(padded[:, s, CONV - 1:], ps[:, s], ACT.Copy).then_inc(padded_done[s], 1)
                    act.wait_ge(conv_step[s], (i - X0 // 2) * CONV + CONV)
                    act.wait_ge(stored[s], i * 16)
                    nc.scalar.activation(out_tile[:, s], conv[:, s], ACT.Silu).then_inc(evacuated[s], 1)
            evacuate(act, MQ0 // 2, G0 // 2, ACT.Copy)
            evacuate(act, G0 // 2, N_IN // 2, ACT.Sigmoid)

        @block.vector
        def _(dve):
            nc.vector.memset(padded[:, :, 0:CONV - 1], 0.0).then_inc(zeroed, 1)
            dve.wait_ge(small_loaded, 80)
            dve.wait_ge(dt_done, 1)
            nc.vector.tensor_tensor(raw[:], ps_dt[:], bias_row[:, None, :].broadcast_to([P, TB, 32]),
                                    ALU.add).then_inc(dt_dve, 1)
            dve.wait_ge(dt_dve, 1)
            nc.vector.tensor_scalar(capped[:], raw[:], 40.0, None, ALU.min).then_inc(dt_dve, 1)
            dve.wait_ge(dt_act, 3)
            nc.vector.tensor_tensor(dt_out[:], soft[:], raw[:], ALU.max).then_inc(dt_dve, 1)
            nc.vector.tensor_scalar(a_row[:], a_row[:], -1.0, None, ALU.mult).then_inc(dt_dve, 1)
            dve.wait_ge(dt_dve, 4)
            nc.vector.tensor_tensor(da_out[:], dt_out[:], a_row[:, None, :].broadcast_to([P, TB, 32]),
                                    ALU.mult).then_inc(dt_dve, 1)
            with dve.Fori(0, n_conv // 2) as j:
                for s in range(2):
                    dve.wait_ge(padded_done[s], j + 1)
                    dve.wait_ge(evacuated[s], j + X0 // 2)
                    c = j * 2 + s
                    nc.vector.tensor_scalar(conv[:, s], padded[:, s, 0:S], cw[:, bass.ds(c, 1), 0],
                                            cb[:, bass.ds(c, 1)], ALU.mult, ALU.add).then_inc(conv_step[s], 1)
                    for tap in range(1, CONV):
                        dve.wait_ge(conv_step[s], j * CONV + tap)
                        nc.vector.scalar_tensor_tensor(
                            conv[:, s], padded[:, s, tap:tap + S], cw[:, bass.ds(c, 1), tap], conv[:, s],
                            ALU.mult, ALU.add).then_inc(conv_step[s], 1)


def stick_breaking(nc, proj, y, consts):
    with stage(nc) as ctx:
        def sb(n, shape, dt=F32):
            return ctx.enter_context(nc.sbuf_tensor(f"sb_{n}", shape, dt))

        def sem(n):
            return nc.alloc_semaphore(f"sb_{n}")

        qkv = sb("qkv", [P, 3, S])
        qkh, qkl = sb("qkh", [P, 2, S], F32R), sb("qkl", [P, 2, S], F32R)
        vh, vl = sb("vh", [P, TB, P], F32R), sb("vl", [P, TB, P], F32R)
        beta, keep = sb("beta", [P, 2, S]), sb("keep", [P, 2, S])
        rest = sb("rest", [P, 2, S + 1])
        w = sb("w", [P, 2, S])
        wth, wtl = sb("wth", [P, 2, TB, HALF], F32R), sb("wtl", [P, 2, TB, HALF], F32R)
        y_tile = sb("y", [P, S])
        ps_z = ctx.enter_context(nc.psum_tensor("sb_psz", [P, 2, S], F32))
        ps_t = ctx.enter_context(nc.psum_tensor("sb_pst", [P, 2, HALF], F32))
        ps_y = ctx.enter_context(nc.psum_tensor("sb_psy", [P, HALF], F32))

        loaded, v_loaded, qk_hi, qk_split = (sem(n) for n in ("ld", "vld", "qkhi", "qksplit"))
        ones_set = sem("ones")
        scores, beta_done, masked, keep_done, scanned, weighted = (
            sem(n) for n in ("scores", "beta", "masked", "keep", "scanned", "weighted"))
        turned, hi_done, lo_done = sem("turned"), sem("hi"), sem("lo")
        y_done, y_out, stored = sem("ydone"), sem("yout"), sem("stored")

        steps = [(a, t) for a in range(2) for t in range(TB)]
        N = len(steps)
        units = [("v", 0, 4 * u, 4) for u in range(2)]
        for n, (a, t) in enumerate(steps):
            units += [("w", n, j, min(4, t + 1 - j)) for j in range(0, t + 1, 4)]
        U = len(units)
        LAG = 2

        block = ctx.enter_context(nc.Block())

        @block.sync
        def _(sp):
            with sp.Fori(0, SB_PAIRS) as p:
                sp.wait_ge(qk_split, p * 2)
                for n, b in enumerate((Q0, K0)):
                    sp.dma_start(qkv[:, n], proj[bass.ds(p + b, 1)].rearrange("a p n -> (a p) n")
                                 ).then_inc(loaded, 16)
                sp.wait_ge(turned, p * U)
                sp.dma_start(qkv[:, 2], proj[bass.ds(p + V0, 1)].rearrange("a p n -> (a p) n")
                             ).then_inc(v_loaded, 16)
                sp.wait_ge(y_out, p * 4 + 4)
                sp.dma_start(y[bass.ds(p + Y_SB, 1)].rearrange("a p n -> (a p) n"), y_tile[:]).then_inc(stored, 16)
            sp.wait_ge(stored, 16 * SB_PAIRS)

        def unit_of(n):
            return max(u for u, x in enumerate(units) if x[:2] == ("w", n)) + 1

        @block.tensor
        def _(pe):
            with pe.Fori(0, SB_PAIRS) as p:
                def turn(u):
                    kind, n, j0, cnt = units[u]
                    if u >= 2:
                        pe.wait_ge(lo_done, p * U + u - 1)
                        pe.wait_ge(hi_done, p * U + u - 1)
                    for j in range(j0, j0 + cnt):
                        src = qkv[:, 2, j * P:(j + 1) * P] if kind == "v" else w[:, n % 2, j * P:(j + 1) * P]
                        last = nc.tensor.transpose(ps_t[:, u % 2, (j - j0) * P:(j - j0 + 1) * P], src,
                                                   consts["ident"][:])
                    last.then_inc(turned, 1)

                pe.wait_ge(v_loaded, p * 16 + 16)
                turn(0)
                turn(1)
                u = 2
                for i in range(N + LAG):
                    if i < N:
                        a, t = steps[i]
                        rows = slice(64 * a, 64 * a + 64)
                        if i == 0:
                            pe.wait_ge(qk_split, p * 2 + 2)
                        pe.wait_ge(beta_done, p * N + i - 1) if i >= 2 else pe.wait_ge(beta_done, p * N)
                        cols = (t + 1) * P
                        for c in range(0, cols, HALF):
                            e = min(cols, c + HALF)
                            for j, (l, r) in enumerate(split3((qkh, qkh), (qkl, qkl))):
                                last = nc.tensor.matmul(ps_z[:, i % 2, c:e], l[rows, 0, t * P:(t + 1) * P],
                                                        r[rows, 1, c:e], start=(j == 0), stop=(j == 2))
                        last.then_inc(scores, 1)
                    n = i - LAG
                    if n < 0:
                        continue
                    a, t = steps[n]
                    pe.wait_ge(weighted, p * N + n + 1)
                    while u < U and units[u][1] == n:
                        turn(u)
                        u += 1
                    if t % 4 == 3:
                        g = n // 4
                        pe.wait_ge(lo_done, p * U + unit_of(n))
                        pe.wait_ge(y_out, p * 4 + g)
                        for j in range(t + 1):
                            lo_col = max(0, j - (t - 3)) * P
                            for m, (l, r) in enumerate(split3((vh, wth), (vl, wtl))):
                                last = nc.tensor.matmul(ps_y[:, lo_col:], l[:, j], r[:, g % 2, j, lo_col:],
                                                        start=(j == 0 and m == 0), stop=(j == t and m == 2))
                        last.then_inc(y_done, 1)

        def moved(u, dst, src):
            kind, n, j0, cnt = units[u]
            ps = ps_t[:, u % 2, 0:cnt * P].rearrange("p (j t) -> p j t", j=cnt)
            if kind == "v":
                return src[:, j0:j0 + cnt], ps
            a, t = steps[n]
            return dst[:, (n // 4) % 2, j0:j0 + cnt, (t % 4) * P:(t % 4 + 1) * P], ps

        @block.scalar
        def _(act):
            with act.Fori(0, SB_PAIRS) as p:
                def hi(u):
                    kind, n, _, _ = units[u]
                    act.wait_ge(turned, p * U + u + 1)
                    if kind == "v" and u == 0:
                        act.wait_ge(y_done, p * 4)
                    if kind == "w" and n % 4 == 0 and n >= 8 and units[u][2] == 0:
                        act.wait_ge(y_done, p * 4 + n // 4 - 1)
                    out, src = moved(u, wth, vh)
                    nc.scalar.activation(out, src, ACT.Copy).then_inc(hi_done, 1)

                hi(0)
                hi(1)
                u = 2
                for i in range(N + LAG):
                    if i < N:
                        t = steps[i][1]
                        act.wait_ge(scores, p * N + i + 1)
                        act.wait_ge(weighted, p * N + (i - 1 if i >= 2 else 0))
                        nc.scalar.activation(beta[:, i % 2, 0:(t + 1) * P], ps_z[:, i % 2, 0:(t + 1) * P],
                                             ACT.Sigmoid, scale=0.125).then_inc(beta_done, 1)
                    n = i - LAG
                    if n < 0:
                        continue
                    while u < U and units[u][1] == n:
                        hi(u)
                        u += 1
                    if n % 4 == 3:
                        g = n // 4
                        rows = slice(64 * (g // 2), 64 * (g // 2) + 64)
                        act.wait_ge(y_done, p * 4 + g + 1)
                        if g == 0:
                            act.wait_ge(stored, p * 16)
                        nc.scalar.activation(y_tile[rows, (g % 2) * HALF:(g % 2 + 1) * HALF], ps_y[rows, :],
                                             ACT.Copy).then_inc(y_out, 1)

        @block.gpsimd
        def _(pool):
            with pool.Fori(0, SB_PAIRS) as p:
                def weigh(n):
                    t = steps[n][1]
                    cols = (t + 1) * P
                    pool.wait_ge(scanned, p * N + n + 1)
                    pool.wait_ge(turned, p * U + (unit_of(n - 2) if n >= 2 else 0))
                    nc.gpsimd.tensor_tensor(w[:, n % 2, 0:cols], beta[:, n % 2, 0:cols],
                                            rest[:, n % 2, S - cols + 1:S + 1], ALU.mult).then_inc(weighted, 1)

                for i in range(N):
                    t = steps[i][1]
                    diag = beta[:, i % 2, t * P:(t + 1) * P]
                    pool.wait_ge(beta_done, p * N + i + 1)
                    nc.gpsimd.tensor_tensor(diag, diag, consts["before"][:], ALU.mult).then_inc(masked, 1)
                    if i:
                        weigh(i - 1)
                weigh(N - 1)

        @block.vector
        def _(dve):
            nc.vector.memset(rest[:, :, S:S + 1], 1.0).then_inc(ones_set, 1)
            dve.wait_ge(ones_set, 1)
            with dve.Fori(0, SB_PAIRS) as p:
                def lo(u):
                    dve.wait_ge(hi_done, p * U + u + 1)
                    out, src = moved(u, wtl, vl)
                    hi = moved(u, wth, vh)[0].bitcast(F32)
                    nc.vector.tensor_tensor(out, src, hi, ALU.subtract).then_inc(lo_done, 1)

                dve.wait_ge(loaded, p * 32 + 32)
                dve.wait_ge(scores, p * N)
                for n in range(2):
                    nc.vector.tensor_copy(qkh[:, n], qkv[:, n]).then_inc(qk_hi, 1)
                for n in range(2):
                    dve.wait_ge(qk_hi, p * 2 + n + 1)
                    nc.vector.tensor_tensor(qkl[:, n], qkv[:, n], qkh[:, n].bitcast(F32),
                                            ALU.subtract).then_inc(qk_split, 1)
                lo(0)
                lo(1)
                u = 2
                for i in range(N + LAG):
                    if i < N:
                        t = steps[i][1]
                        cols = (t + 1) * P
                        dve.wait_ge(masked, p * N + i + 1)
                        nc.vector.tensor_scalar(keep[:, i % 2, 0:cols], beta[:, i % 2, 0:cols], -1.0, 1.0,
                                                ALU.mult, ALU.add).then_inc(keep_done, 1)
                        dve.wait_ge(keep_done, p * N + i + 1)
                        dve.wait_ge(weighted, p * N + (i - 1 if i >= 2 else 0))
                        down = keep[:, i % 2, 0:cols][:, ::-1]
                        nc.vector.tensor_tensor_scan(rest[:, i % 2, S - cols:S][:, ::-1], down, down, 1.0,
                                                     ALU.mult, ALU.bypass).then_inc(scanned, 1)
                    n = i - LAG
                    while n >= 0 and u < U and units[u][1] == n:
                        lo(u)
                        u += 1


def ssd(nc, proj, y, dt, da, d_rows, ssd_gain, consts):
    with stage(nc) as ctx:
        def sb(n, shape, dt_=F32):
            return ctx.enter_context(nc.sbuf_tensor(f"ssd_{n}", shape, dt_))

        def ps(n, shape):
            return ctx.enter_context(nc.psum_tensor(f"ssd_{n}", shape, F32))

        def sem(n):
            return nc.alloc_semaphore(f"ssd_{n}")

        R = HPG
        xT, zT, yT = sb("xT", [P, GB, S]), sb("zT", [P, GB, S]), sb("yT", [P, GB, S])
        bcT = sb("bcT", [P, 2, S])
        bch, bcl = sb("bch", [P, 2, S], F32R), sb("bcl", [P, 2, S], F32R)
        drow, gain = sb("drow", [P, GROUPS * GB]), sb("gain", [P, GROUPS * GB])
        a_cs, to_end = (sb(n, [P, TB, SSD_HEADS]) for n in ("acs", "toend"))
        bth, btl = sb("bth", [P, 2, P], F32R), sb("btl", [P, 2, P], F32R)
        xd = sb("xd", [P, R, 64])
        xe = sb("xe", [P, R, 64])
        xdh, xdl, xeh, xel = (sb(n, [P, 2, R * 64], F32R) for n in ("xdh", "xdl", "xeh", "xel"))
        cb = sb("cb", [P, P])
        tri_da = sb("trida", [P, R, P])
        w = sb("w", [P, R, P])
        grown = sb("grown", [P, R, P])
        ce = sb("ce", [P, R, P])
        wh, wl, ceh, cel = (sb(n, [P, 2, R, P], F32R) for n in ("wh", "wl", "ceh", "cel"))
        whole = sb("whole", [P, 2, R])
        state = sb("state", [P, R, 64])
        sth, stl = sb("sth", [P, R * 64], F32R), sb("stl", [P, R * 64], F32R)
        rstd = sb("rstd", [P, S])
        ps_bc, ps_x, ps_a = ps("psbc", [P, 2, P]), ps("psx", [P, R, 64]), ps("psa", [P, R, P])
        ps_y, ps_s, ps_cs = ps("psy", [P, GB, 2, P]), ps("pss", [P, R, 64]), ps("pscs", [P, 2, TB * SSD_HEADS])

        small_loaded, cs_done, cs_exp, cs_read, cs_diff = (sem(n) for n in ("small", "cs", "csexp", "csread", "csdiff"))
        loaded, z_loaded, stored = sem("loaded"), sem("zloaded"), sem("stored")
        bc_hi, bc_split, skip_done = sem("bchi"), sem("bcsplit"), sem("skip")
        tri_done, bc_turned, x_turned, a_done = (sem(n) for n in ("tri", "bcturned", "xturned", "adone"))
        xd_done, xe_done, cb_done, seg_raw, seg_done = (sem(n) for n in ("xd", "xe", "cb", "segraw", "seg"))
        bt_hi, bt_split, xd_hi, xd_split, xe_hi, xe_split = (
            sem(n) for n in ("bthi", "btsplit", "xdhi", "xdsplit", "xehi", "xesplit"))
        decayed, w_done, w_hi, w_split = (sem(n) for n in ("decayed", "wdone", "whi", "wsplit"))
        grown_done, ce_done, ce_hi, ce_split = (sem(n) for n in ("grown", "cedone", "cehi", "cesplit"))
        y_mm, s_mm, y_done, state_scaled, state_done, st_hi, st_split = (
            sem(n) for n in ("ymm", "smm", "ydone", "scaled", "state", "sthi", "stsplit"))
        whole_kept = sem("whole")
        gated, squared, norm_mm, rooted, inverted, normed = (
            sem(n) for n in ("gated", "squared", "normmm", "rooted", "inverted", "normed"))

        block = ctx.enter_context(nc.Block())

        @block.sync
        def _(sp):
            sp.dma_start(drow[:], d_rows).then_inc(small_loaded, 16)
            sp.dma_start(gain[:], ssd_gain).then_inc(small_loaded, 16)
            with sp.Fori(0, GROUPS) as g:
                sp.wait_ge(ce_done, g * TB)
                sp.wait_ge(x_turned, g * TB)
                sp.wait_ge(bc_turned, g * TB)
                for n, b in enumerate((B0, C0)):
                    sp.dma_start(bcT[:, n], proj[bass.ds(g + b, 1)].rearrange("a p n -> (a p) n")).then_inc(loaded, 16)
                sp.wait_ge(skip_done, g * GB)
                sp.dma_start(xT[:], proj[bass.ds(g * GB + X0, GB)].rearrange("k p n -> p k n")).then_inc(loaded, 16)
                sp.wait_ge(norm_mm, g)
                sp.dma_start(zT[:], proj[bass.ds(g * GB + Z0, GB)].rearrange("k p n -> p k n")).then_inc(z_loaded, 16)
                sp.wait_ge(normed, g * GB + GB)
                sp.dma_start(y[bass.ds(g * GB + Y_SSD, GB)].rearrange("k p n -> p k n"), yT[:]).then_inc(stored, 16)
            sp.wait_ge(stored, 16 * GROUPS)

        @block.tensor
        def _(pe):
            da_all = da[:].rearrange("p c h -> p (c h)")
            nc.tensor.matmul(ps_cs[:, 0], consts["tri"][:], da_all, start=True, stop=True)
            nc.tensor.matmul(ps_cs[:, 1], consts["ones"][:], da_all, start=True, stop=True).then_inc(cs_done, 1)

            with pe.Fori(0, GROUPS) as g:
                def front(c):
                    n = g * TB + c
                    cols = slice(c * P, (c + 1) * P)
                    if c == 0:
                        pe.wait_ge(bc_split, g * 2 + 2)
                        pe.wait_ge(loaded, g * 48 + 48)
                    pe.wait_ge(bt_split, n)
                    pe.wait_ge(cb_done, n)
                    nc.tensor.transpose(ps_bc[:, 0], bcT[:, 0, cols], consts["ident"][:])
                    for j, (l, r) in enumerate(split3((bch, bch), (bcl, bcl))):
                        last = nc.tensor.matmul(ps_bc[:, 1], l[:, 0, cols], r[:, 1, cols], start=(j == 0), stop=(j == 2))
                    last.then_inc(bc_turned, 1)
                    pe.wait_ge(xd_done, n)
                    for b in range(GB):
                        last = nc.tensor.transpose(ps_x[:, 2 * b:2 * b + 2].rearrange("p r d -> p (r d)"),
                                                   xT[:, b, cols], consts["ident"][:])
                    last.then_inc(x_turned, 1)
                    pe.wait_ge(tri_done, n + 1)
                    pe.wait_ge(seg_raw, n)
                    pe.wait_ge(grown_done, n)
                    if c == 0:
                        pe.wait_ge(rooted, g)
                    for h in range(2):
                        last = nc.tensor.matmul(ps_a[:, 4 * h:4 * h + 4], consts["ones"][:],
                                                tri_da[:, 4 * h:4 * h + 4], start=True, stop=True)
                    last.then_inc(a_done, 1)

                def back(c):
                    n = g * TB + c
                    b = c % 2
                    pe.wait_ge(xd_split, n + 1)
                    pe.wait_ge(w_split, n + 1)
                    if c:
                        pe.wait_ge(ce_split, n + 1)
                        pe.wait_ge(st_split, n)
                    pe.wait_ge(y_done, n * 2)
                    for q in range(GB):
                        heads = slice(q * P, (q + 1) * P)
                        for j, (l, r) in enumerate(split3((xdh, wh), (xdl, wl))):
                            last = nc.tensor.matmul(ps_y[:, q], l[:, b, heads], r[:, b, 2 * q:2 * q + 2],
                                                    start=(j == 0), stop=(c == 0 and j == 2))
                        for j, (l, r) in enumerate(split3((sth, ceh), (stl, cel)) if c else ()):
                            last = nc.tensor.matmul(ps_y[:, q], l[:, heads], r[:, b, 2 * q:2 * q + 2],
                                                    start=False, stop=(j == 2))
                    last.then_inc(y_mm, 1)
                    pe.wait_ge(xe_split, n + 1)
                    pe.wait_ge(bt_split, n + 1)
                    pe.wait_ge(state_done, n)
                    for j, (l, r) in enumerate(split3((bth, xeh), (btl, xel))):
                        last = nc.tensor.matmul(ps_s[:], l[:, b], r[:, b], start=(j == 0), stop=(j == 2))
                    last.then_inc(s_mm, 1)

                for c in range(TB + 1):
                    if c < TB:
                        front(c)
                    if c:
                        back(c - 1)
                pe.wait_ge(squared, g + 1)
                for h in range(2):
                    for b in range(GB):
                        last = nc.tensor.matmul(ps_a[:, 4 * h:4 * h + 4], consts["ones"][:],
                                                zT[:, b, h * HALF:(h + 1) * HALF], start=(b == 0), stop=(b == GB - 1))
                last.then_inc(norm_mm, 1)

        @block.scalar
        def _(act):
            act.wait_ge(cs_diff, 1)
            nc.scalar.activation(to_end[:], to_end[:], ACT.Exp).then_inc(cs_exp, 1)
            with act.Fori(0, GROUPS) as g:
                act.wait_ge(loaded, g * 48 + 48)
                act.wait_ge(s_mm, g * TB)
                act.wait_ge(bc_split, g * 2)
                for i in range(2):
                    nc.scalar.activation(bch[:, i], bcT[:, i], ACT.Copy).then_inc(bc_hi, 1)
                for c in range(TB + 1):
                    n = g * TB + c
                    b = c % 2
                    if c < TB:
                        if c >= 2:
                            act.wait_ge(s_mm, n - 1)
                        act.wait_ge(bc_turned, n + 1)
                        nc.scalar.activation(bth[:, b], ps_bc[:, 0], ACT.Copy).then_inc(bt_hi, 1)
                        act.wait_ge(xd_done, n + 1)
                        nc.scalar.activation(xdh[:, b], xd[:].rearrange("p r d -> p (r d)"), ACT.Copy).then_inc(xd_hi, 1)
                        act.wait_ge(a_done, n + 1)
                        act.wait_ge(ce_done, n)
                        act.wait_ge(whole_kept, n)
                        nc.scalar.activation(grown[:], ps_a[:], ACT.Exp).then_inc(grown_done, 1)
                        act.wait_ge(seg_done, n + 1)
                        nc.scalar.activation(w[:], w[:], ACT.Exp).then_inc(decayed, 1)
                        act.wait_ge(xe_done, n + 1)
                        nc.scalar.activation(xeh[:, b], xe[:].rearrange("p r d -> p (r d)"), ACT.Copy).then_inc(xe_hi, 1)
                        act.wait_ge(w_done, n + 1)
                        nc.scalar.activation(wh[:, b], w[:], ACT.Copy).then_inc(w_hi, 1)
                        act.wait_ge(ce_done, n + 1)
                        nc.scalar.activation(ceh[:, b], ce[:], ACT.Copy).then_inc(ce_hi, 1)
                    if c:
                        act.wait_ge(state_done, n)
                        act.wait_ge(y_mm, n)
                        nc.scalar.activation(sth[:], state[:].rearrange("p r d -> p (r d)"), ACT.Copy).then_inc(st_hi, 1)
                act.wait_ge(gated, g + 1)
                nc.scalar.activation(zT[:], yT[:], ACT.Square).then_inc(squared, 1)
                act.wait_ge(norm_mm, g + 1)
                act.wait_ge(normed, g * GB)
                nc.scalar.activation(rstd[:], ps_a[:].rearrange("p r l -> p (r l)"), ACT.Sqrt,
                                     scale=1.0 / (GB * P), bias=consts["eps"][:]).then_inc(rooted, 1)

        @block.gpsimd
        def _(pool):
            with pool.Fori(0, GROUPS) as g:
                def decays(c):
                    pool.wait_ge(a_done, g * TB + c)
                    nc.gpsimd.tensor_tensor(
                        tri_da[:], consts["tri"][:, None, :].broadcast_to([P, R, P]),
                        da[:, c, bass.ds(g * R, R)][:, :, None].broadcast_to([P, R, P]), ALU.mult).then_inc(tri_done, 1)

                decays(0)
                for c in range(TB):
                    n = g * TB + c
                    pool.wait_ge(xd_done, n + 1)
                    pool.wait_ge(xe_split, n)
                    if c == 0:
                        pool.wait_ge(cs_exp, 1)
                    nc.gpsimd.tensor_tensor(
                        xe[:], xd[:], to_end[:, c, bass.ds(g * R, R)][:, :, None].broadcast_to([P, R, 64]),
                        ALU.mult).then_inc(xe_done, 1)
                    if c < TB - 1:
                        decays(c + 1)
                    pool.wait_ge(decayed, n + 1)
                    pool.wait_ge(cb_done, n + 1)
                    nc.gpsimd.tensor_tensor(w[:], w[:], cb[:, None, :].broadcast_to([P, R, P]),
                                            ALU.mult).then_inc(w_done, 1)
                    pool.wait_ge(grown_done, n + 1)
                    pool.wait_ge(ce_split, n)
                    nc.gpsimd.tensor_tensor(
                        ce[:], grown[:], bcT[:, 1, c * P:(c + 1) * P][:, None, :].broadcast_to([P, R, P]),
                        ALU.mult).then_inc(ce_done, 1)

        @block.vector
        def _(dve):
            dve.wait_ge(small_loaded, 32)
            dve.wait_ge(cs_done, 1)
            flat = "p c h -> p (c h)"
            nc.vector.tensor_copy(a_cs[:].rearrange(flat), ps_cs[:, 0]).then_inc(cs_read, 1)
            dve.wait_ge(cs_read, 1)
            nc.vector.tensor_tensor(to_end[:].rearrange(flat), ps_cs[:, 1], a_cs[:].rearrange(flat),
                                    ALU.subtract).then_inc(cs_diff, 1)
            with dve.Fori(0, GROUPS) as g:
                dve.wait_ge(loaded, g * 48 + 48)
                for i in range(2):
                    dve.wait_ge(bc_hi, g * 2 + i + 1)
                    nc.vector.tensor_tensor(bcl[:, i], bcT[:, i], bch[:, i].bitcast(F32), ALU.subtract).then_inc(bc_split, 1)
                dve.wait_ge(stored, g * 16)
                for b in range(GB):
                    nc.vector.tensor_scalar(yT[:, b], xT[:, b], drow[:, bass.ds(g * GB + b, 1)], None,
                                            ALU.mult).then_inc(skip_done, 1)
                for c in range(TB + 1):
                    n = g * TB + c
                    b = c % 2
                    if c < TB:
                        heads = bass.ds(g * R, R)
                        if c >= 2:
                            dve.wait_ge(s_mm, n - 1)
                        dve.wait_ge(x_turned, n + 1)
                        dve.wait_ge(xd_hi, n)
                        dve.wait_ge(xe_done, n)
                        dve.wait_ge(xd_split, n)
                        nc.vector.tensor_tensor(xd[:], ps_x[:], dt[:, c, heads][:, :, None].broadcast_to([P, R, 64]),
                                                ALU.mult).then_inc(xd_done, 1)
                        dve.wait_ge(bc_turned, n + 1)
                        dve.wait_ge(bt_hi, n + 1)
                        dve.wait_ge(w_done, n)
                        nc.vector.tensor_tensor(cb[:], ps_bc[:, 1], consts["tri"][:], ALU.mult).then_inc(cb_done, 1)
                        dve.wait_ge(bt_hi, n + 1)
                        nc.vector.tensor_tensor(btl[:, b], ps_bc[:, 0], bth[:, b].bitcast(F32),
                                                ALU.subtract).then_inc(bt_split, 1)
                        dve.wait_ge(grown_done, n + 1)
                        nc.vector.tensor_copy(whole[:, b], grown[:, :, P - 1]).then_inc(whole_kept, 1)
                        dve.wait_ge(w_split, n)
                        nc.vector.tensor_tensor(w[:], ps_a[:], a_cs[:, c, heads][:, :, None].broadcast_to([P, R, P]),
                                                ALU.subtract).then_inc(seg_raw, 1)
                        dve.wait_ge(seg_raw, n + 1)
                        nc.vector.tensor_scalar(w[:], w[:], 0.0, None, ALU.min).then_inc(seg_done, 1)
                        dve.wait_ge(xd_hi, n + 1)
                        nc.vector.tensor_tensor(xdl[:, b], xd[:].rearrange("p r d -> p (r d)"), xdh[:, b].bitcast(F32),
                                                ALU.subtract).then_inc(xd_split, 1)
                        dve.wait_ge(xe_hi, n + 1)
                        nc.vector.tensor_tensor(xel[:, b], xe[:].rearrange("p r d -> p (r d)"), xeh[:, b].bitcast(F32),
                                                ALU.subtract).then_inc(xe_split, 1)
                        dve.wait_ge(w_hi, n + 1)
                        nc.vector.tensor_tensor(wl[:, b], w[:], wh[:, b].bitcast(F32), ALU.subtract).then_inc(w_split, 1)
                        dve.wait_ge(ce_hi, n + 1)
                        nc.vector.tensor_tensor(cel[:, b], ce[:], ceh[:, b].bitcast(F32),
                                                ALU.subtract).then_inc(ce_split, 1)
                    if c:
                        m = n - 1
                        dve.wait_ge(y_mm, m + 1)
                        cols = slice((c - 1) * P, c * P)
                        for h in range(2):
                            rows = slice(64 * h, 64 * h + 64)
                            nc.vector.tensor_tensor(yT[rows, :, cols], ps_y[rows, :, h], yT[rows, :, cols],
                                                    ALU.add).then_inc(y_done, 1)
                        dve.wait_ge(s_mm, m + 1)
                        if c > 1:
                            nc.vector.tensor_tensor(state[:], state[:],
                                                    whole[:, 1 - b, :, None].broadcast_to([P, R, 64]),
                                                    ALU.mult).then_inc(state_scaled, 1)
                            dve.wait_ge(state_scaled, g * (TB - 1) + c - 1)
                            nc.vector.tensor_tensor(state[:], ps_s[:], state[:], ALU.add).then_inc(state_done, 1)
                        else:
                            nc.vector.tensor_copy(state[:], ps_s[:]).then_inc(state_done, 1)
                        dve.wait_ge(st_hi, m + 1)
                        nc.vector.tensor_tensor(stl[:], state[:].rearrange("p r d -> p (r d)"), sth[:].bitcast(F32),
                                                ALU.subtract).then_inc(st_split, 1)
                dve.wait_ge(z_loaded, g * 16 + 16)
                dve.wait_ge(y_done, (g * TB + TB) * 2)
                nc.vector.tensor_tensor(yT[:], yT[:], zT[:], ALU.mult).then_inc(gated, 1)
                dve.wait_ge(rooted, g + 1)
                nc.vector.reciprocal(rstd[:], rstd[:]).then_inc(inverted, 1)
                dve.wait_ge(inverted, g + 1)
                for b in range(GB):
                    nc.vector.scalar_tensor_tensor(yT[:, b], yT[:, b], gain[:, bass.ds(g * GB + b, 1)], rstd[:],
                                                   ALU.mult, ALU.mult).then_inc(normed, 1)


def memory_keys_values(nc, w_kv, kv, xh, xl, consts):
    with stage(nc) as ctx:
        ring = Ring(nc, ctx, "kv", consts)
        n_blocks = 2 * KB
        out_tile = ctx.enter_context(nc.sbuf_tensor("kv_out", [P, 2, M], F32))
        ps = ctx.enter_context(nc.psum_tensor("kv_ps", [P, 2, HALF], F32))
        evacuated = [nc.alloc_semaphore(f"kv_evac{s}") for s in range(2)]
        stored = [nc.alloc_semaphore(f"kv_stored{s}") for s in range(2)]
        block = ctx.enter_context(nc.Block())

        @block.sync
        def _(sp):
            for s in range(2):
                load_weights(sp, ring, w_kv, 0, s, s)
            with sp.Fori(0, n_blocks // 2 - 1) as i:
                for s in range(2):
                    load_weights(sp, ring, w_kv, i + 1, s, i * 2 + s + 2)
                    sp.wait_ge(evacuated[s], i + 1)
                    sp.dma_start(kv[bass.ds(i * 2 + s, 1)].rearrange("a p n -> (a p) n"),
                                 out_tile[:, s]).then_inc(stored[s], 16)
            for s in range(2):
                sp.wait_ge(evacuated[s], n_blocks // 2)
                sp.dma_start(kv[n_blocks - 2 + s], out_tile[:, s]).then_inc(stored[s], 16)
            for s in range(2):
                sp.wait_ge(stored[s], 16 * n_blocks // 2)

        @block.gpsimd
        def _(pool):
            with pool.Fori(0, n_blocks // 2) as i:
                for s in range(2):
                    split_weights(nc, pool, ring, i, s)

        @block.tensor
        def _(pe):
            with pe.Fori(0, n_blocks // 2) as i:
                for s in range(2):
                    pe.wait_ge(ring.split[s], i + 1)
                    pe.wait_ge(evacuated[s], i)
                    product(nc, ring, s, xh, xl, ps[:, s], M).then_inc(ring.used[s], 1)

        @block.scalar
        def _(act):
            with act.Fori(0, n_blocks // 2) as i:
                for s in range(2):
                    act.wait_ge(ring.used[s], i + 1)
                    act.wait_ge(stored[s], i * 16)
                    nc.scalar.activation(out_tile[:, s], ps[:, s, 0:M], ACT.Copy).then_inc(evacuated[s], 1)


def memory_attention(nc, proj, kv, y, consts):
    with stage(nc) as ctx:
        def sb(n, shape, dt=F32):
            return ctx.enter_context(nc.sbuf_tensor(f"ma_{n}", shape, dt))

        def sem(n):
            return nc.alloc_semaphore(f"ma_{n}")

        DB = 2
        qT, kT, vT = sb("qT", [P, DB, S]), sb("kT", [P, DB, M]), sb("vT", [P, DB, M])
        qh, ql = sb("qh", [P, DB, S], F32R), sb("ql", [P, DB, S], F32R)
        kh, kl = sb("kh", [P, DB, M], F32R), sb("kl", [P, DB, M], F32R)
        vh, vl = sb("vh", [P, MB, M], F32R), sb("vl", [P, MB, M], F32R)
        top, less, total, share = (sb(n, [P, 2]) for n in ("top", "less", "total", "share"))
        e, prob = sb("e", [P, 2, M]), sb("prob", [P, 2, M])
        pth, ptl = sb("pth", [P, MB, S], F32R), sb("ptl", [P, MB, S], F32R)
        y_tile = sb("y", [P, DB, S])
        ps_s = ctx.enter_context(nc.psum_tensor("ma_pss", [P, 2, HALF], F32))
        ps_t = ctx.enter_context(nc.psum_tensor("ma_pst", [P, 2, HALF], F32))
        ps_v = ctx.enter_context(nc.psum_tensor("ma_psv", [P, MB, M], F32))
        ps_y = ctx.enter_context(nc.psum_tensor("ma_psy", [P, 2, HALF], F32))
        loaded, k_hi, q_hi, k_split, q_split = (sem(n) for n in ("ld", "khi", "qhi", "ksplit", "qsplit"))
        v_turned, v_hi, v_split = sem("vturned"), sem("vhi"), sem("vsplit")
        scores, topped, lessened, e_done, inverted, prob_done = (
            sem(n) for n in ("scores", "topped", "less", "e", "inverted", "prob"))
        turned, pt_hi, pt_split, y_mm, y_out, stored = (
            sem(n) for n in ("turned", "pthi", "ptsplit", "ymm", "yout", "stored"))
        block = ctx.enter_context(nc.Block())

        @block.sync
        def _(sp):
            with sp.Fori(0, MEM_HEADS) as h:
                sp.wait_ge(q_split, h)
                sp.wait_ge(k_split, h)
                sp.wait_ge(v_turned, h)
                for dst, src, b in ((kT, kv, 0), (vT, kv, KB), (qT, proj, MQ0)):
                    sp.dma_start(dst[:], src[bass.ds(h * DB + b, DB)].rearrange("k p n -> p k n")).then_inc(loaded, 16)
                sp.wait_ge(y_out, h * 4 + 4)
                sp.dma_start(y[bass.ds(h * DB + Y_MEM, DB)].rearrange("k p n -> p k n"), y_tile[:]).then_inc(stored, 16)
            sp.wait_ge(stored, 16 * MEM_HEADS)

        @block.tensor
        def _(pe):
            with pe.Fori(0, MEM_HEADS) as h:
                pe.wait_ge(loaded, h * 48 + 48)
                for m in range(MB):
                    for d in range(DB):
                        last = nc.tensor.transpose(ps_v[:, m, d * P:(d + 1) * P], vT[:, d, m * P:(m + 1) * P],
                                                   consts["ident"][:])
                last.then_inc(v_turned, 1)
                pe.wait_ge(q_split, h + 1)
                pe.wait_ge(k_split, h + 1)
                for t in range(TB + 1):
                    n = h * TB + t
                    if t < TB:
                        pe.wait_ge(e_done, n - 1 if t >= 2 else h * TB)
                        for d in range(DB):
                            for j, (l, r) in enumerate(split3((qh, kh), (ql, kl))):
                                last = nc.tensor.matmul(ps_s[:, t % 2, 0:M], l[:, d, t * P:(t + 1) * P], r[:, d],
                                                        start=(d == 0 and j == 0), stop=(d == DB - 1 and j == 2))
                        last.then_inc(scores, 1)
                    if t:
                        pe.wait_ge(prob_done, n)
                        pe.wait_ge(pt_split, n - 2 if t >= 3 else h * TB)
                        for m in range(MB):
                            last = nc.tensor.transpose(ps_t[:, (t - 1) % 2, m * P:(m + 1) * P],
                                                       prob[:, (t - 1) % 2, m * P:(m + 1) * P], consts["ident"][:])
                        last.then_inc(turned, 1)
                pe.wait_ge(pt_split, h * TB + TB)
                pe.wait_ge(v_split, h + 1)
                for u in range(4):
                    d, half = u // 2, u % 2
                    pe.wait_ge(y_out, h * 4 + (u - 1 if u >= 2 else 0))
                    for m in range(MB):
                        for j, (l, r) in enumerate(split3((vh, pth), (vl, ptl))):
                            last = nc.tensor.matmul(ps_y[:, u % 2], l[:, m, d * P:(d + 1) * P],
                                                    r[:, m, half * HALF:(half + 1) * HALF],
                                                    start=(m == 0 and j == 0), stop=(m == MB - 1 and j == 2))
                    last.then_inc(y_mm, 1)

        @block.scalar
        def _(act):
            with act.Fori(0, MEM_HEADS) as h:
                act.wait_ge(loaded, h * 48 + 48)
                act.wait_ge(y_mm, h * 4)
                act.wait_ge(scores, h * TB)
                nc.scalar.activation(qh[:], qT[:], ACT.Copy).then_inc(q_hi, 1)
                nc.scalar.activation(kh[:], kT[:], ACT.Copy).then_inc(k_hi, 1)
                act.wait_ge(v_turned, h + 1)
                nc.scalar.activation(vh[:], ps_v[:], ACT.Copy).then_inc(v_hi, 1)
                for t in range(TB + 1):
                    n = h * TB + t
                    if t < TB:
                        act.wait_ge(lessened, n + 1)
                        act.wait_ge(prob_done, n - 1 if t >= 2 else h * TB)
                        nc.scalar.activation(e[:, t % 2], ps_s[:, t % 2, 0:M], ACT.Exp, scale=MEM_SCALE,
                                             bias=less[:, t % 2:t % 2 + 1],
                                             accum_out=total[:, t % 2:t % 2 + 1]).then_inc(e_done, 1)
                    if t:
                        act.wait_ge(turned, n)
                        nc.scalar.activation(pth[:, :, (t - 1) * P:t * P],
                                             ps_t[:, (t - 1) % 2, 0:M].rearrange("p (m t) -> p m t", m=MB),
                                             ACT.Copy).then_inc(pt_hi, 1)
                for u in range(4):
                    d, half = u // 2, u % 2
                    act.wait_ge(y_mm, h * 4 + u + 1)
                    act.wait_ge(stored, h * 16)
                    nc.scalar.activation(y_tile[:, d, half * HALF:(half + 1) * HALF], ps_y[:, u % 2],
                                         ACT.Copy).then_inc(y_out, 1)

        @block.vector
        def _(dve):
            with dve.Fori(0, MEM_HEADS) as h:
                dve.wait_ge(q_hi, h + 1)
                nc.vector.tensor_tensor(ql[:], qT[:], qh[:].bitcast(F32), ALU.subtract).then_inc(q_split, 1)
                dve.wait_ge(k_hi, h + 1)
                nc.vector.tensor_tensor(kl[:], kT[:], kh[:].bitcast(F32), ALU.subtract).then_inc(k_split, 1)
                dve.wait_ge(v_hi, h + 1)
                nc.vector.tensor_tensor(vl[:], ps_v[:], vh[:].bitcast(F32), ALU.subtract).then_inc(v_split, 1)
                for t in range(TB + 1):
                    n = h * TB + t
                    s = slice(t % 2, t % 2 + 1)
                    if t < TB:
                        dve.wait_ge(scores, n + 1)
                        nc.vector.tensor_reduce(top[:, s], ps_s[:, t % 2, 0:M], AX_X, ALU.max).then_inc(topped, 1)
                        dve.wait_ge(topped, n + 1)
                        dve.wait_ge(e_done, n - 1 if t >= 2 else h * TB)
                        nc.vector.tensor_scalar(less[:, s], top[:, s], -MEM_SCALE, None, ALU.mult).then_inc(lessened, 1)
                        dve.wait_ge(e_done, n + 1)
                        nc.vector.reciprocal(share[:, s], total[:, s]).then_inc(inverted, 1)
                        dve.wait_ge(inverted, n + 1)
                        dve.wait_ge(turned, n - 1 if t >= 2 else h * TB)
                        nc.vector.tensor_scalar(prob[:, t % 2], e[:, t % 2], share[:, s], None,
                                                ALU.mult).then_inc(prob_done, 1)
                    if t:
                        dve.wait_ge(pt_hi, n)
                        cols = slice((t - 1) * P, t * P)
                        nc.vector.tensor_tensor(ptl[:, :, cols],
                                                ps_t[:, (t - 1) % 2, 0:M].rearrange("p (m t) -> p m t", m=MB),
                                                pth[:, :, cols].bitcast(F32), ALU.subtract).then_inc(pt_split, 1)


def merge_branches(nc, w_out, proj, y, merged, consts):
    gates_of = (0, 1, 1, 2)
    with stage(nc) as ctx:
        def sb(n, shape, dt=F32):
            return ctx.enter_context(nc.sbuf_tensor(f"mg_{n}", shape, dt))

        def sem(n):
            return nc.alloc_semaphore(f"mg_{n}")

        ring = Ring(nc, ctx, "mg", consts)
        raw = sb("raw", [P, 2, S])
        yh, yl = sb("yh", [P, KB, S], F32R), sb("yl", [P, KB, S], F32R)
        gate, gated = sb("gate", [P, 2, S]), sb("gated", [P, 2, S])
        ps = ctx.enter_context(nc.psum_tensor("mg_ps", [P, 2, S], F32))
        y_loaded = [sem(f"yld{s}") for s in range(2)]
        gate_loaded = [sem(f"gld{s}") for s in range(2)]
        y_hi, y_split, gated_done, summed = sem("yhi"), sem("ysplit"), sem("gated"), sem("summed")
        multiplied = [sem(f"mult{s}") for s in range(2)]
        cleared = sem("cleared")
        block = ctx.enter_context(nc.Block())
        NP = KB // 2

        @block.sync
        def _(sp):
            for part in range(4):
                for k in range(KB):
                    sp.wait_ge(y_split, part * KB + (k - 1 if k >= 2 else 0))
                    sp.dma_start(raw[:, k % 2], y[part * KB + k]).then_inc(y_loaded[k % 2], 16)
                with sp.Fori(0, NP) as i:
                    for s in range(2):
                        load_weights(sp, ring, w_out, i + part * NP, s, i * 2 + s + part * KB)
                        sp.wait_ge(multiplied[s], i + part * NP)
                        sp.dma_start(gate[:, s], proj[bass.ds(i * 2 + s + G0 + gates_of[part] * KB, 1)]
                                     .rearrange("a p n -> (a p) n")).then_inc(gate_loaded[s], 16)

        @block.gpsimd
        def _(pool):
            with pool.Fori(0, 4 * NP) as i:
                for s in range(2):
                    split_weights(nc, pool, ring, i, s)

        @block.scalar
        def _(act):
            for part in range(4):
                for k in range(KB):
                    act.wait_ge(y_loaded[k % 2], 16 * (part * NP + k // 2 + 1))
                    if k == 0 and part:
                        for s in range(2):
                            act.wait_ge(ring.used[s], part * NP)
                    nc.scalar.activation(yh[:, k], raw[:, k % 2], ACT.Copy).then_inc(y_hi, 1)

        @block.tensor
        def _(pe):
            for part in range(4):
                pe.wait_ge(y_split, part * KB + KB)
                with pe.Fori(part * NP, part * NP + NP) as i:
                    for s in range(2):
                        pe.wait_ge(ring.split[s], i + 1)
                        pe.wait_ge(multiplied[s], i)
                        product(nc, ring, s, yh, yl, ps[:, s], S).then_inc(ring.used[s], 1)

        @block.vector
        def _(dve):
            nc.vector.memset(merged[:], 0.0).then_inc(cleared, 1)
            dve.wait_ge(cleared, 1)
            for part in range(4):
                for k in range(KB):
                    n = part * KB + k
                    dve.wait_ge(y_hi, n + 1)
                    nc.vector.tensor_tensor(yl[:, k], raw[:, k % 2], yh[:, k].bitcast(F32),
                                            ALU.subtract).then_inc(y_split, 1)
                with dve.Fori(part * NP, part * NP + NP) as i:
                    for s in range(2):
                        dve.wait_ge(ring.used[s], i + 1)
                        dve.wait_ge(gate_loaded[s], i * 16 + 16)
                        dve.wait_ge(summed, i * 2 + s)
                        nc.vector.tensor_tensor(gated[:, s], ps[:, s], gate[:, s], ALU.mult).then_inc(multiplied[s], 1)
                        dve.wait_ge(multiplied[s], i + 1)
                        row = merged[:, bass.ds(i * 2 + s - part * KB, 1)].rearrange("p a n -> p (a n)")
                        nc.vector.tensor_tensor(row, row, gated[:, s], ALU.add).then_inc(summed, 1)


def split_blocks(nc, name, x, xh, xl):
    with stage(nc) as ctx:
        hi_done = nc.alloc_semaphore(f"{name}_hi")
        block = ctx.enter_context(nc.Block())

        @block.scalar
        def _(act):
            for k in range(KB):
                nc.scalar.activation(xh[:, k], x[:, k], ACT.Copy).then_inc(hi_done, 1)

        @block.vector
        def _(dve):
            for k in range(KB):
                dve.wait_ge(hi_done, k + 1)
                nc.vector.tensor_tensor(xl[:, k], x[:, k], xh[:, k].bitcast(F32), ALU.subtract)


def output_projection(nc, w_o, xh, xl, mix, consts):
    with stage(nc) as ctx:
        ring = Ring(nc, ctx, "wo", consts)
        ps = ctx.enter_context(nc.psum_tensor("wo_ps", [P, 2, S], F32))
        evacuated = [nc.alloc_semaphore(f"wo_evac{s}") for s in range(2)]
        block = ctx.enter_context(nc.Block())

        @block.sync
        def _(sp):
            with sp.Fori(0, KB // 2) as i:
                for s in range(2):
                    load_weights(sp, ring, w_o, i, s, i * 2 + s)

        @block.gpsimd
        def _(pool):
            with pool.Fori(0, KB // 2) as i:
                for s in range(2):
                    split_weights(nc, pool, ring, i, s)

        @block.tensor
        def _(pe):
            with pe.Fori(0, KB // 2) as i:
                for s in range(2):
                    pe.wait_ge(ring.split[s], i + 1)
                    pe.wait_ge(evacuated[s], i)
                    product(nc, ring, s, xh, xl, ps[:, s], S).then_inc(ring.used[s], 1)

        @block.scalar
        def _(act):
            with act.Fori(0, KB // 2) as i:
                for s in range(2):
                    act.wait_ge(ring.used[s], i + 1)
                    nc.scalar.activation(mix[:, bass.ds(i * 2 + s, 1)].rearrange("p a n -> p (a n)"), ps[:, s],
                                         ACT.Copy).then_inc(evacuated[s], 1)


def add_normed(nc, name, xT, gain_row, base, dst, consts):
    with stage(nc) as ctx:
        def sb(n, shape, dt=F32):
            return ctx.enter_context(nc.sbuf_tensor(f"{name}_{n}", shape, dt))

        def sem(n):
            return nc.alloc_semaphore(f"{name}_{n}")

        gain, tile, square, scaled = sb("gain", [P, D]), sb("tile", [P, 2, D]), sb("sq", [P, D]), sb("scaled", [P, 2, D])
        sums, root, rstd = sb("sums", [P, TB]), sb("root", [P, TB]), sb("rstd", [P, TB])
        ps = ctx.enter_context(nc.psum_tensor(f"{name}_ps", [P, 2, D], F32))
        gain_loaded = sem("gain")
        loaded, stored = [sem(f"ld{s}") for s in range(2)], [sem(f"st{s}") for s in range(2)]
        turned, summed, rooted, inverted, scaled_done, added = (
            sem(n) for n in ("turned", "summed", "rooted", "inverted", "scaled_done", "added"))
        block = ctx.enter_context(nc.Block())

        @block.sync
        def _(sp):
            sp.dma_start(gain[:], gain_row).then_inc(gain_loaded, 16)
            for t in range(TB + 1):
                if t < TB:
                    if t >= 2:
                        sp.wait_ge(stored[t % 2], 16 * (t // 2))
                    sp.dma_start(tile[:, t % 2], base[t * P:(t + 1) * P, :]).then_inc(loaded[t % 2], 16)
                if t:
                    sp.wait_ge(added, t)
                    sp.dma_start(dst[(t - 1) * P:t * P, :], tile[:, (t - 1) % 2]).then_inc(stored[(t - 1) % 2], 16)
            for s in range(2):
                sp.wait_ge(stored[s], 16 * TB // 2)

        @block.tensor
        def _(pe):
            for t in range(TB):
                if t >= 2:
                    pe.wait_ge(scaled_done, t - 1)
                for k in range(KB):
                    last = nc.tensor.transpose(ps[:, t % 2, k * P:(k + 1) * P], xT[:, k, t * P:(t + 1) * P],
                                               consts["ident"][:])
                last.then_inc(turned, 1)

        @block.scalar
        def _(act):
            for t in range(TB):
                act.wait_ge(turned, t + 1)
                nc.scalar.activation(square[:], ps[:, t % 2], ACT.Square, accum_out=sums[:, t:t + 1]).then_inc(summed, 1)
                act.wait_ge(summed, t + 1)
                nc.scalar.activation(root[:, t:t + 1], sums[:, t:t + 1], ACT.Sqrt, scale=1.0 / D,
                                     bias=consts["eps"][:]).then_inc(rooted, 1)

        @block.vector
        def _(dve):
            dve.wait_ge(gain_loaded, 16)
            for t in range(TB):
                dve.wait_ge(rooted, t + 1)
                nc.vector.reciprocal(rstd[:, t:t + 1], root[:, t:t + 1]).then_inc(inverted, 1)
                dve.wait_ge(inverted, t + 1)
                nc.vector.scalar_tensor_tensor(scaled[:, t % 2], ps[:, t % 2], rstd[:, t:t + 1], gain[:],
                                               ALU.mult, ALU.mult).then_inc(scaled_done, 1)
                dve.wait_ge(scaled_done, t + 1)
                dve.wait_ge(loaded[t % 2], 16 * (t // 2 + 1))
                nc.vector.tensor_tensor(tile[:, t % 2], tile[:, t % 2], scaled[:, t % 2], ALU.add).then_inc(added, 1)


def mlp(nc, w_up, w_down, xh, xl, out, consts):
    with stage(nc) as ctx:
        def sb(n, shape, dt=F32):
            return ctx.enter_context(nc.sbuf_tensor(f"ff_{n}", shape, dt))

        def sem(n):
            return nc.alloc_semaphore(f"ff_{n}")

        ring = Ring(nc, ctx, "ff", consts)
        fh, fl = sb("fh", [P, KB, S], F32R), sb("fl", [P, KB, S], F32R)
        positive, square = sb("pos", [P, 2, S]), sb("sq", [P, 2, S])
        ps = ctx.enter_context(nc.psum_tensor("ff_ps", [P, 2, S], F32))
        pos_done, sq_done, f_hi, f_split = ([sem(f"{n}{s}") for s in range(2)] for n in ("posdone", "sqdone", "fhi", "fsplit"))
        added = [sem(f"added{s}") for s in range(2)]
        cleared = sem("cleared")
        NP = KB // 2
        block = ctx.enter_context(nc.Block())

        @block.sync
        def _(sp):
            with sp.Fori(0, FF_CHUNKS) as f:
                with sp.Fori(0, NP) as i:
                    for s in range(2):
                        load_weights(sp, ring, w_up, f * 2 * NP + i, s, f * KB + i * 2 + s)
                with sp.Fori(0, NP) as i:
                    for s in range(2):
                        load_weights(sp, ring, w_down, f * 2 * NP + NP + i, s, f * KB + i * 2 + s)

        @block.gpsimd
        def _(pool):
            with pool.Fori(0, FF_CHUNKS * 2 * NP) as i:
                for s in range(2):
                    split_weights(nc, pool, ring, i, s)

        @block.tensor
        def _(pe):
            with pe.Fori(0, FF_CHUNKS) as f:
                with pe.Fori(0, NP) as i:
                    for s in range(2):
                        pe.wait_ge(ring.split[s], f * 2 * NP + i + 1)
                        pe.wait_ge(pos_done[s], f * NP + i)
                        pe.wait_ge(added[s], f * NP)
                        product(nc, ring, s, xh, xl, ps[:, s], S).then_inc(ring.used[s], 1)
                with pe.Fori(0, NP) as i:
                    for s in range(2):
                        for r in range(2):
                            pe.wait_ge(f_split[r], f * NP + NP)
                        pe.wait_ge(ring.split[s], f * 2 * NP + NP + i + 1)
                        pe.wait_ge(added[s], f * NP + i)
                        product(nc, ring, s, fh, fl, ps[:, s], S).then_inc(ring.used[s], 1)

        @block.scalar
        def _(act):
            with act.Fori(0, FF_CHUNKS) as f:
                with act.Fori(0, NP) as i:
                    for s in range(2):
                        act.wait_ge(ring.used[s], f * 2 * NP + i + 1)
                        act.wait_ge(sq_done[s], f * NP + i)
                        nc.scalar.activation(positive[:, s], ps[:, s], ACT.Relu).then_inc(pos_done[s], 1)
                        act.wait_ge(sq_done[s], f * NP + i + 1)
                        nc.scalar.activation(fh[:, bass.ds(i * 2 + s, 1)].rearrange("p a n -> p (a n)"),
                                             square[:, s], ACT.Copy).then_inc(f_hi[s], 1)

        @block.vector
        def _(dve):
            nc.vector.memset(out[:], 0.0).then_inc(cleared, 1)
            dve.wait_ge(cleared, 1)
            with dve.Fori(0, FF_CHUNKS) as f:
                with dve.Fori(0, NP) as i:
                    for s in range(2):
                        dve.wait_ge(pos_done[s], f * NP + i + 1)
                        dve.wait_ge(f_split[s], f * NP + i)
                        nc.vector.tensor_tensor(square[:, s], positive[:, s], positive[:, s],
                                                ALU.mult).then_inc(sq_done[s], 1)
                        dve.wait_ge(f_hi[s], f * NP + i + 1)
                        one = bass.ds(i * 2 + s, 1)
                        nc.vector.tensor_tensor(fl[:, one].rearrange("p a n -> p (a n)"), square[:, s],
                                                fh[:, one].rearrange("p a n -> p (a n)").bitcast(F32),
                                                ALU.subtract).then_inc(f_split[s], 1)
                with dve.Fori(0, NP) as i:
                    for s in range(2):
                        dve.wait_ge(ring.used[s], f * 2 * NP + NP + i + 1)
                        row = out[:, bass.ds(i * 2 + s, 1)].rearrange("p a n -> p (a n)")
                        nc.vector.tensor_tensor(row, ps[:, s], row, ALU.add).then_inc(added[s], 1)


def set_constants(nc, consts):
    with stage(nc) as ctx:
        set_, shaped = (nc.alloc_semaphore("const_set")), (nc.alloc_semaphore("const_shaped"))
        block = ctx.enter_context(nc.Block())

        @block.gpsimd
        def _(pool):
            for name, value in (("ident", 0.0), ("tri", 1.0), ("before", 1.0), ("ones", 1.0), ("one", 1.0), ("eps", EPS)):
                nc.gpsimd.memset(consts[name][:], value).then_inc(set_, 1)
            pool.wait_ge(set_, 6)
            ident, tri, before = consts["ident"][:], consts["tri"][:], consts["before"][:]
            nc.gpsimd.affine_select(out=ident, in_=ident, pattern=[[-1, P]], compare_op=ALU.not_equal, fill=1.0,
                                    base=0, channel_multiplier=1).then_inc(shaped, 1)
            nc.gpsimd.affine_select(out=tri, in_=tri, pattern=[[1, P]], compare_op=ALU.is_ge, fill=0.0,
                                    base=0, channel_multiplier=-1).then_inc(shaped, 1)
            nc.gpsimd.affine_select(out=before, in_=before, pattern=[[-1, P]], compare_op=ALU.is_gt, fill=0.0,
                                    base=0, channel_multiplier=1).then_inc(shaped, 1)


def layer(nc, a, out, scratch):
    proj, y, kv, h = (scratch[n] for n in ("proj", "y", "kv", "h"))
    with ExitStack() as ctx:
        def sb(c, n, shape, dt=F32):
            return c.enter_context(nc.sbuf_tensor(n, shape, dt))

        consts = {n: sb(ctx, n, [P, P]) for n in ("ident", "tri", "before", "ones")}
        consts |= {n: sb(ctx, n, [P, 1]) for n in ("one", "eps")}
        set_constants(nc, consts)
        dt, da = sb(ctx, "dt", [P, TB, SSD_HEADS]), sb(ctx, "da", [P, TB, SSD_HEADS])
        with ExitStack() as c:
            xh, xl = sb(c, "memh", [P, KB, M], F32R), sb(c, "meml", [P, KB, M], F32R)
            norm_to_feature_major(nc, "nm", a["mem"], M, a["norm_mem"], xh, xl, consts)
            memory_keys_values(nc, a["w_mem_kv"], kv, xh, xl, consts)
        with ExitStack() as c:
            xh, xl = sb(c, "uh", [P, KB, S], F32R), sb(c, "ul", [P, KB, S], F32R)
            norm_to_feature_major(nc, "nu", a["x"], S, a["norm_mix_pre"], xh, xl, consts)
            input_projection(nc, a["w_in"], a["w_dt"], a["conv_w"], a["conv_b"], proj,
                             a["dt_bias"].broadcast_to([P, 32]), a["a_log"].broadcast_to([P, 32]), dt, da, xh, xl, consts)
        stick_breaking(nc, proj, y, consts)
        ssd(nc, proj, y, dt, da, a["d_skip"], a["ssd_norm"], consts)
        memory_attention(nc, proj, kv, y, consts)
        with ExitStack() as c:
            merged = sb(c, "merged", [P, KB, S])
            merge_branches(nc, a["w_branch"], proj, y, merged, consts)
            xh, xl = sb(c, "mh", [P, KB, S], F32R), sb(c, "ml", [P, KB, S], F32R)
            split_blocks(nc, "ms", merged, xh, xl)
            output_projection(nc, a["w_o"], xh, xl, merged, consts)
            add_normed(nc, "h1", merged, a["norm_mix_post"].broadcast_to([P, D]), a["x"], h, consts)
        with ExitStack() as c:
            xh, xl = sb(c, "vh", [P, KB, S], F32R), sb(c, "vl", [P, KB, S], F32R)
            norm_to_feature_major(nc, "nh", h, S, a["norm_mlp_pre"], xh, xl, consts)
            ff = sb(c, "ff", [P, KB, S])
            mlp(nc, a["w_up"], a["w_down"], xh, xl, ff, consts)
            add_normed(nc, "h2", ff, a["norm_mlp_post"].broadcast_to([P, D]), h, out, consts)


def lay_out(inputs):
    import numpy as np
    x = {k: np.asarray(v) for k, v in inputs.items()}
    n_qkv_z_xbc, n_dt = Q0 * P + MQ0 * P, SSD_HEADS
    w_in = x["w_in"][0]

    def tiles(w):
        r, c = w.shape[0] // D, w.shape[1] // P
        return np.ascontiguousarray(w.reshape(r, KB, P, c, P).transpose(0, 3, 2, 1, 4).reshape(r * c, P, D))

    def columns(v):
        return np.ascontiguousarray(v.reshape(-1, P).T)

    return {
        "x": x["x"][0], "mem": x["mem"][0],
        "w_in": tiles(np.concatenate([w_in[:, :n_qkv_z_xbc], w_in[:, n_qkv_z_xbc + n_dt:]], axis=1)),
        "w_dt": np.ascontiguousarray(w_in[:, n_qkv_z_xbc:n_qkv_z_xbc + n_dt].reshape(KB, P, n_dt).transpose(1, 0, 2)),
        "conv_w": np.ascontiguousarray(x["conv_w"][0].reshape(CONV, -1, P).transpose(2, 1, 0)),
        "conv_b": columns(x["conv_b"][0]),
        "dt_bias": x["dt_bias"], "a_log": x["a_log"],
        "d_skip": np.ascontiguousarray(np.repeat(x["d_skip"][0], 64).reshape(-1, P).T),
        "ssd_norm": columns(x["ssd_norm"][0]),
        "norm_mix_pre": columns(x["norm_mix_pre"][0]), "norm_mem": columns(x["norm_mem"][0]),
        "norm_mlp_pre": columns(x["norm_mlp_pre"][0]),
        "norm_mix_post": x["norm_mix_post"], "norm_mlp_post": x["norm_mlp_post"],
        "w_mem_kv": tiles(x["w_mem_kv"][0]),
        "w_branch": tiles(np.concatenate([x["w_sb_out"][0], x["w_ssd_out"][0], x["w_mem_out"][0]], axis=0)),
        "w_o": tiles(x["w_o"][0]), "w_up": tiles(x["w_up"][0]), "w_down": tiles(x["w_down"][0]),
    }


def kernel(**inputs):
    import numpy as np
    import concourse.bacc as bacc
    from concourse.bass_utils import run_bass_kernel_spmd

    nc = bacc.Bacc("TRN2", target_bir_lowering=False, num_devices=1)
    arrays = {f"in_{k}": v for k, v in lay_out(inputs).items()}
    a = {k[3:]: nc.dram_tensor(k, v.shape, mybir.dt.from_np(v.dtype), kind="ExternalInput").ap()
         for k, v in arrays.items()}
    out = nc.dram_tensor("out", (S, D), F32, kind="ExternalOutput").ap()
    scratch = {n: nc.dram_tensor(f"scratch_{n}", shape, F32, kind=KIND).ap()
               for n, shape in (("proj", (N_IN, P, S)), ("y", (N_Y, P, S)), ("kv", (2 * KB, P, M)), ("h", (S, D)))}
    layer(nc, a, out, scratch)
    r = run_bass_kernel_spmd(nc, [arrays], core_ids=[0])
    return r.results[0]["out"].reshape(1, S, D)


KIND = "Internal"
```

```python
from contextlib import ExitStack, contextmanager

import concourse.bass as bass
from concourse import mybir

F32 = mybir.dt.float32
F32R = mybir.dt.float32r
ALU = mybir.AluOpType
ACT = mybir.ActivationFunctionType
AX_X = mybir.AxisListType.X

P = 128
D = 1024
KB = D // P
S = 1024
TB = S // P
HALF = 512
M = 256
MB = M // P
EPS = 1e-6

SB_PAIRS = 8
SSD_HEADS, GROUPS, HPG = 32, 4, 8
GB = 4
MEM_HEADS = 4
MEM_SCALE = 256.0 ** -0.5
CONV = 4

Q0, K0, V0, Z0, X0, B0, C0, MQ0, G0, N_IN = 0, 8, 16, 24, 40, 56, 60, 64, 72, 96
Y_SB, Y_SSD, Y_MEM, N_Y = 0, 8, 24, 32
FF_CHUNKS = 4


@contextmanager
def stage(nc):
    with nc.cleanup_on_exit(), ExitStack() as ctx:
        yield ctx


def split3(hi, lo):
    (ah, bh), (al, bl) = hi, lo
    return ((ah, bh), (ah, bl), (al, bh))


def norm_to_feature_major(nc, name, src, tokens, gain, xh, xl, consts):
    n_pairs = tokens // P // 2
    with stage(nc) as ctx:
        def sb(n, shape, dt=F32):
            return ctx.enter_context(nc.sbuf_tensor(f"{name}_{n}", shape, dt))

        def sem(n):
            return nc.alloc_semaphore(f"{name}_{n}")

        x_tile, u, square = sb("x", [P, 2, D]), sb("u", [P, 2, D]), sb("sq", [P, D])
        scaled = sb("scaled", [P, 2, D])
        sums, root, rstd = sb("sums", [P, 2]), sb("root", [P, 2]), sb("rstd", [P, 2])
        gains = sb("gain", [P, KB])
        turned = ctx.enter_context(nc.psum_tensor(f"{name}_ps", [P, 2, D], F32))
        gain_loaded = sem("gain_loaded")
        loaded = [sem(f"loaded{s}") for s in range(2)]
        summed, rooted, inverted = sem("summed"), sem("rooted"), sem("inverted")
        normed = [sem(f"normed{s}") for s in range(2)]
        turned_done = [sem(f"turned{s}") for s in range(2)]
        gained = [sem(f"gained{s}") for s in range(2)]
        hi_done = [sem(f"hi{s}") for s in range(2)]
        lo_done = [sem(f"lo{s}") for s in range(2)]

        block = ctx.enter_context(nc.Block())

        @block.sync
        def _(sp):
            sp.dma_start(gains[:], gain).then_inc(gain_loaded, 16)
            with sp.Fori(0, n_pairs) as i:
                for s in range(2):
                    sp.wait_ge(normed[s], i)
                    sp.dma_start(x_tile[:, s], src[bass.ds(i * 256 + s * P, P), :]).then_inc(loaded[s], 16)

        @block.scalar
        def _(act):
            with act.Fori(0, n_pairs) as i:
                for s in range(2):
                    act.wait_ge(loaded[s], i * 16 + 16)
                    nc.scalar.activation(square[:], x_tile[:, s], ACT.Square,
                                         accum_out=sums[:, s:s + 1]).then_inc(summed, 1)
                    act.wait_ge(summed, i * 2 + s + 1)
                    act.wait_ge(normed[s], i)
                    nc.scalar.activation(root[:, s:s + 1], sums[:, s:s + 1], ACT.Sqrt, scale=1.0 / D,
                                         bias=consts["eps"][:]).then_inc(rooted, 1)
                for s in range(2):
                    act.wait_ge(gained[s], i + 1)
                    act.wait_ge(lo_done[s], i)
                    nc.scalar.activation(xh[:, :, bass.ds(i * 256 + s * P, P)],
                                         scaled[:, s].rearrange("p (k t) -> p k t", k=KB),
                                         ACT.Copy).then_inc(hi_done[s], 1)

        @block.vector
        def _(dve):
            dve.wait_ge(gain_loaded, 16)
            with dve.Fori(0, n_pairs) as i:
                for s in range(2):
                    dve.wait_ge(rooted, i * 2 + s + 1)
                    nc.vector.reciprocal(rstd[:, s:s + 1], root[:, s:s + 1]).then_inc(inverted, 1)
                    dve.wait_ge(inverted, i * 2 + s + 1)
                    dve.wait_ge(turned_done[s], i)
                    nc.vector.tensor_scalar(u[:, s], x_tile[:, s], rstd[:, s:s + 1], None,
                                            ALU.mult).then_inc(normed[s], 1)
                for s in range(2):
                    dve.wait_ge(turned_done[s], i + 1)
                    dve.wait_ge(lo_done[s], i)
                    nc.vector.tensor_tensor(
                        scaled[:, s].rearrange("p (k t) -> p k t", k=KB),
                        turned[:, s].rearrange("p (k t) -> p k t", k=KB),
                        gains[:, :, None].broadcast_to([P, KB, P]), ALU.mult).then_inc(gained[s], 1)
                for s in range(2):
                    dve.wait_ge(hi_done[s], i + 1)
                    dve.wait_ge(gained[s], i + 1)
                    hi = xh[:, :, bass.ds(i * 256 + s * P, P)].bitcast(F32)
                    nc.vector.tensor_tensor(xl[:, :, bass.ds(i * 256 + s * P, P)],
                                            scaled[:, s].rearrange("p (k t) -> p k t", k=KB), hi,
                                            ALU.subtract).then_inc(lo_done[s], 1)

        @block.tensor
        def _(pe):
            with pe.Fori(0, n_pairs) as i:
                for s in range(2):
                    pe.wait_ge(normed[s], i + 1)
                    pe.wait_ge(gained[s], i)
                    for k in range(KB):
                        last = nc.tensor.transpose(turned[:, s, k * P:(k + 1) * P], u[:, s, k * P:(k + 1) * P],
                                                   consts["ident"][:])
                    last.then_inc(turned_done[s], 1)


class Ring:

    def __init__(self, nc, ctx, name, consts):
        self.ones = consts["one"]
        self.raw = ctx.enter_context(nc.sbuf_tensor(f"{name}_w", [P, 2, D], F32))
        self.hi = ctx.enter_context(nc.sbuf_tensor(f"{name}_wh", [P, 2, KB, P], F32R))
        self.lo = ctx.enter_context(nc.sbuf_tensor(f"{name}_wl", [P, 2, KB, P], F32R))
        s = [nc.alloc_semaphore(f"{name}_{n}{i}") for n in ("loaded", "hi", "split", "used")
             for i in range(2)]
        self.loaded, self.hi_done, self.split, self.used = s[0:2], s[2:4], s[4:6], s[6:8]


def load_weights(sp, ring, w, i, s, row):
    sp.wait_ge(ring.split[s], i)
    sp.dma_start(ring.raw[:, s], w[bass.ds(row, 1)].rearrange("a p n -> (a p) n")).then_inc(ring.loaded[s], 16)


def round_weights(nc, pool, ring, i, s):
    pool.wait_ge(ring.loaded[s], i * 16 + 16)
    pool.wait_ge(ring.used[s], i)
    nc.gpsimd.tensor_tensor(ring.hi[:, s].rearrange("p k n -> p (k n)"), ring.raw[:, s],
                            ring.ones[:].broadcast_to([P, D]), ALU.mult).then_inc(ring.hi_done[s], 1)


def rest_of_weights(nc, pool, ring, i, s):
    flat = "p k n -> p (k n)"
    pool.wait_ge(ring.hi_done[s], i + 1)
    nc.gpsimd.tensor_tensor(ring.lo[:, s].rearrange(flat), ring.raw[:, s],
                            ring.hi[:, s].rearrange(flat).bitcast(F32), ALU.subtract).then_inc(ring.split[s], 1)


def split_weights(nc, pool, ring, i, s):
    round_weights(nc, pool, ring, i, s)
    rest_of_weights(nc, pool, ring, i, s)


def product(nc, ring, s, xh, xl, out, tokens):
    n = min(tokens, HALF)
    for h in range(tokens // n):
        for k in range(KB):
            for j, (w, x) in enumerate(split3((ring.hi, xh), (ring.lo, xl))):
                last = nc.tensor.matmul(out[:, h * n:(h + 1) * n], w[:, s, k], x[:, k, h * n:(h + 1) * n],
                                        start=(k == 0 and j == 0), stop=(k == KB - 1 and j == 2))
    return last


def input_projection(nc, w_in, w_dt, proj, dt_bias, a_log, dt_out, da_out, xh, xl, consts):
    with stage(nc) as ctx:
        def sb(n, shape, dt=F32):
            return ctx.enter_context(nc.sbuf_tensor(f"in_{n}", shape, dt))

        def sem(n):
            return nc.alloc_semaphore(f"in_{n}")

        ring = Ring(nc, ctx, "in", consts)
        out_tile = sb("out", [P, 2, S])
        wd, wdh, wdl = sb("wd", [P, KB, 32]), sb("wdh", [P, KB, 32], F32R), sb("wdl", [P, KB, 32], F32R)
        bias_row, a_row = sb("bias", [P, 32]), sb("a", [P, 32])
        raw, capped, soft = (sb(n, [P, TB, 32]) for n in ("dtraw", "dtcap", "dtsoft"))
        ps = ctx.enter_context(nc.psum_tensor("in_ps", [P, 2, S], F32))
        ps_dt = ctx.enter_context(nc.psum_tensor("in_psdt", [P, TB, 32], F32))
        small_loaded, wd_hi, wd_split, dt_done = sem("small"), sem("wdhi"), sem("wdsplit"), sem("dtdone")
        dt_dve, dt_act = sem("dtdve"), sem("dtact")
        evacuated = [sem(f"evac{s}") for s in range(2)]
        stored = [sem(f"stored{s}") for s in range(2)]
        N_QKV = Z0

        block = ctx.enter_context(nc.Block())

        @block.sync
        def _(sp):
            for dst, src in ((wd, w_dt), (bias_row, dt_bias), (a_row, a_log)):
                sp.dma_start(dst[:], src).then_inc(small_loaded, 16)
            for s in range(2):
                load_weights(sp, ring, w_in, 0, s, s)
            with sp.Fori(0, N_QKV // 2 - 1) as i:
                for s in range(2):
                    load_weights(sp, ring, w_in, i + 1, s, i * 2 + s + 2)
                    sp.wait_ge(evacuated[s], i + 1)
                    sp.dma_start(proj[bass.ds(i * 2 + s, 1)].rearrange("a p n -> (a p) n"),
                                 out_tile[:, s]).then_inc(stored[s], 16)
            for s in range(2):
                sp.wait_ge(evacuated[s], N_QKV // 2)
                sp.dma_start(proj[N_QKV - 2 + s], out_tile[:, s]).then_inc(stored[s], 16)
            for s in range(2):
                sp.wait_ge(stored[s], 16 * N_QKV // 2)

        @block.gpsimd
        def _(pool):
            pool.wait_ge(small_loaded, 48)
            nc.gpsimd.tensor_copy(wdh[:], wd[:]).then_inc(wd_hi, 1)
            pool.wait_ge(wd_hi, 1)
            nc.gpsimd.tensor_tensor(wdl[:], wd[:], wdh[:].bitcast(F32), ALU.subtract).then_inc(wd_split, 1)
            with pool.Fori(0, N_QKV // 2) as i:
                for s in range(2):
                    split_weights(nc, pool, ring, i, s)

        @block.tensor
        def _(pe):
            pe.wait_ge(wd_split, 1)
            for t in range(TB):
                for k in range(KB):
                    for j, (x, w) in enumerate(split3((xh, wdh), (xl, wdl))):
                        last = nc.tensor.matmul(ps_dt[:, t], x[:, k, t * P:(t + 1) * P], w[:, k],
                                                start=(k == 0 and j == 0), stop=(k == KB - 1 and j == 2))
            last.then_inc(dt_done, 1)
            with pe.Fori(0, N_QKV // 2) as i:
                for s in range(2):
                    pe.wait_ge(ring.split[s], i + 1)
                    pe.wait_ge(evacuated[s], i)
                    product(nc, ring, s, xh, xl, ps[:, s], S).then_inc(ring.used[s], 1)

        @block.scalar
        def _(act):
            act.wait_ge(dt_dve, 2)
            nc.scalar.activation(soft[:], capped[:], ACT.Exp).then_inc(dt_act, 1)
            act.wait_ge(dt_act, 1)
            nc.scalar.activation(soft[:], soft[:], ACT.Ln, bias=consts["one"][:]).then_inc(dt_act, 1)
            nc.scalar.activation(a_row[:], a_row[:], ACT.Exp).then_inc(dt_act, 1)
            with act.Fori(0, N_QKV // 2) as i:
                for s in range(2):
                    act.wait_ge(ring.used[s], i + 1)
                    act.wait_ge(stored[s], i * 16)
                    nc.scalar.activation(out_tile[:, s], ps[:, s], ACT.Copy).then_inc(evacuated[s], 1)

        @block.vector
        def _(dve):
            dve.wait_ge(small_loaded, 48)
            dve.wait_ge(dt_done, 1)
            nc.vector.tensor_tensor(raw[:], ps_dt[:], bias_row[:, None, :].broadcast_to([P, TB, 32]),
                                    ALU.add).then_inc(dt_dve, 1)
            dve.wait_ge(dt_dve, 1)
            nc.vector.tensor_scalar(capped[:], raw[:], 40.0, None, ALU.min).then_inc(dt_dve, 1)
            dve.wait_ge(dt_act, 3)
            nc.vector.tensor_tensor(dt_out[:], soft[:], raw[:], ALU.max).then_inc(dt_dve, 1)
            nc.vector.tensor_scalar(a_row[:], a_row[:], -1.0, None, ALU.mult).then_inc(dt_dve, 1)
            dve.wait_ge(dt_dve, 4)
            nc.vector.tensor_tensor(da_out[:], dt_out[:], a_row[:, None, :].broadcast_to([P, TB, 32]),
                                    ALU.mult).then_inc(dt_dve, 1)


def stick_breaking(nc, w_in, conv_w, conv_b, proj, y, uh, ul, consts):
    with stage(nc) as ctx:
        def sb(n, shape, dt=F32):
            return ctx.enter_context(nc.sbuf_tensor(f"sb_{n}", shape, dt))

        def sem(n):
            return nc.alloc_semaphore(f"sb_{n}")

        qkv = sb("qkv", [P, 3, S])
        qkh, qkl = sb("qkh", [P, 2, S], F32R), sb("qkl", [P, 2, S], F32R)
        vh, vl = sb("vh", [P, TB, P], F32R), sb("vl", [P, TB, P], F32R)
        beta, keep = sb("beta", [P, 2, S]), sb("keep", [P, S])
        rest = sb("rest", [P, 2, S + 1])
        wth, wtl = sb("wth", [P, TB, HALF], F32R), sb("wtl", [P, TB, HALF], F32R)
        y_tile = sb("y", [P, S])
        ps_z = ctx.enter_context(nc.psum_tensor("sb_psz", [P, S], F32))
        ps_t = ctx.enter_context(nc.psum_tensor("sb_pst", [P, 2, HALF], F32))
        ps_y = ctx.enter_context(nc.psum_tensor("sb_psy", [P, HALF], F32))

        loaded, v_loaded, qk_hi, qk_split = (sem(n) for n in ("ld", "vld", "qkhi", "qksplit"))
        ones_set = sem("ones")
        scores, beta_done, masked, keep_done, scanned, weighted = (
            sem(n) for n in ("scores", "beta", "masked", "keep", "scanned", "weighted"))
        turned, hi_done, lo_done = sem("turned"), sem("hi"), sem("lo")
        y_done, y_out, stored = sem("ydone"), sem("yout"), sem("stored")

        ring = Ring(nc, ctx, "sb", consts)
        kinds = "xzxzxq"
        PER = len(kinds)
        n_conv = MQ0 - X0
        out_tile = sb("out", [P, 2, S])
        padded = sb("padded", [P, CONV - 1 + S])
        sigm = sb("sigm", [P, 2, S])
        cw, cb = sb("cw", [P, n_conv, CONV]), sb("cb", [P, n_conv])
        ps_g = ctx.enter_context(nc.psum_tensor("sb_psg", [P, 2, HALF], F32))
        small_loaded, zeroed = sem("small"), sem("zeroed")
        half_done, half_out = sem("halfdone"), [sem(f"halfout{h}") for h in range(2)]
        conv_step, sigm_done = sem("convstep"), sem("sigm")
        silu_done = [sem(f"silu{s}") for s in range(2)]
        g_stored = [sem(f"gstored{s}") for s in range(2)]

        steps = [(a, t) for a in range(2) for t in range(TB)]
        N = len(steps)
        units = [("v", 0, 4 * u, 4) for u in range(2)]
        for n, (a, t) in enumerate(steps):
            units += [("w", n, j, min(4, t + 1 - j)) for j in range(0, t + 1, 4)]
        U = len(units)
        LAG = 2
        EVENTS = N + LAG
        PASSES = KB * 3
        PER_EVENT = PER * 2 * PASSES // (EVENTS - 2)

        def event_of(m, h):
            return 2 + (m * 2 * PASSES + h * PASSES + PASSES - 1) // PER_EVENT

        def units_of(n):
            return [u for u, x in enumerate(units) if x[:2] == ("w", n)]

        def turned_by(n):
            return units_of(n)[-1] + 1

        def row_of(p, m):
            return {"x": p * 3 + X0 + m // 2, "z": p * 2 + Z0 + m // 2, "q": p + MQ0}[kinds[m]]

        block = ctx.enter_context(nc.Block())

        @block.sync
        def _(sp):
            def load_qk(p):
                for n, b in enumerate((Q0, K0)):
                    sp.dma_start(qkv[:, n], proj[bass.ds(p + b, 1)].rearrange("a p n -> (a p) n")).then_inc(loaded, 16)

            def load_v(p):
                sp.dma_start(qkv[:, 2], proj[bass.ds(p + V0, 1)].rearrange("a p n -> (a p) n")).then_inc(v_loaded, 16)

            load_qk(0)
            load_v(0)
            load_weights(sp, ring, w_in, 0, 0, row_of(0, 0))
            for dst, src in ((cw, conv_w), (cb, conv_b)):
                sp.dma_start(dst[:], src).then_inc(small_loaded, 16)
            with sp.Fori(0, SB_PAIRS) as p:
                after = p + 1

                def load(m):
                    load_weights(sp, ring, w_in, p * 3 + m // 2, m % 2, row_of(p, m))

                def store(m):
                    if kinds[m] == "q":
                        sp.wait_ge(half_out[1], p * PER + m + 1)
                    else:
                        sp.wait_ge(silu_done[m % 2], p * (3 if kinds[m] == "x" else 2) + m // 2 + 1)
                    sp.dma_start(proj[bass.ds(row_of(p, m), 1)].rearrange("a p n -> (a p) n"),
                                 out_tile[:, m % 2]).then_inc(g_stored[m % 2], 16)

                load(1)
                sp.wait_ge(qk_split, p * 2 + 2)
                load_qk(after)
                sp.wait_ge(turned, p * U + 2)
                load_v(after)
                load(2)
                load(3)
                load(4)
                store(0)
                store(1)
                load(5)
                store(2)
                load_weights(sp, ring, w_in, p * 3 + 3, 0, row_of(after, 0))
                store(3)
                store(4)
                store(5)
                sp.wait_ge(y_out, p * 4 + 4)
                sp.dma_start(y[bass.ds(p + Y_SB, 1)].rearrange("a p n -> (a p) n"), y_tile[:]).then_inc(stored, 16)
            sp.wait_ge(stored, 16 * SB_PAIRS)
            for s in range(2):
                sp.wait_ge(g_stored[s], 16 * 3 * SB_PAIRS)
            sp.wait_ge(loaded, 32 * (SB_PAIRS + 1))
            sp.wait_ge(v_loaded, 16 * (SB_PAIRS + 1))
            sp.wait_ge(ring.loaded[0], 16 * (3 * SB_PAIRS + 1))

        @block.tensor
        def _(pe):
            with pe.Fori(0, SB_PAIRS) as p:
                def turn(u):
                    kind, n, j0, cnt = units[u]
                    if u >= 2:
                        pe.wait_ge(lo_done, p * U + u - 1)
                    for j in range(j0, j0 + cnt):
                        src = qkv[:, 2, j * P:(j + 1) * P] if kind == "v" else beta[:, n % 2, j * P:(j + 1) * P]
                        last = nc.tensor.transpose(ps_t[:, u % 2, (j - j0) * P:(j - j0 + 1) * P], src,
                                                   consts["ident"][:])
                    last.then_inc(turned, 1)

                def project(first, end):
                    for x in range(first, end):
                        m, h, k, j = x // (2 * PASSES), x // PASSES % 2, x % PASSES // 3, x % 3
                        s = m % 2
                        if k == 0 and j == 0:
                            if h == 0:
                                pe.wait_ge(ring.split[s], p * 3 + m // 2 + 1)
                            pe.wait_ge(half_out[h], p * PER + m)
                        l, r = split3((ring.hi, uh), (ring.lo, ul))[j]
                        last = nc.tensor.matmul(ps_g[:, h], l[:, s, k], r[:, k, h * HALF:(h + 1) * HALF],
                                                start=(k == 0 and j == 0), stop=(k == KB - 1 and j == 2))
                        if k == KB - 1 and j == 2:
                            last.then_inc(ring.used[s] if h else half_done, 1)

                pe.wait_ge(v_loaded, p * 16 + 16)
                turn(0)
                turn(1)
                for i in range(EVENTS):
                    if i < N:
                        a, t = steps[i]
                        rows = slice(64 * a, 64 * a + 64)
                        if i == 0:
                            pe.wait_ge(qk_split, p * 2 + 2)
                        pe.wait_ge(beta_done, p * N + i)
                        cols = (t + 1) * P
                        for c in range(0, cols, HALF):
                            e = min(cols, c + HALF)
                            for j, (l, r) in enumerate(split3((qkh, qkh), (qkl, qkl))):
                                last = nc.tensor.matmul(ps_z[:, c:e], l[rows, 0, t * P:(t + 1) * P],
                                                        r[rows, 1, c:e], start=(j == 0), stop=(j == 2))
                        last.then_inc(scores, 1)
                    n = i - LAG
                    if n >= 0:
                        a, t = steps[n]
                        pe.wait_ge(weighted, p * N + n + 1)
                        for u in units_of(n):
                            turn(u)
                    if i >= 2:
                        project((i - 2) * PER_EVENT, (i - 1) * PER_EVENT)
                    if n >= 0 and t % 4 == 3:
                        pe.wait_ge(lo_done, p * U + turned_by(n))
                        pe.wait_ge(y_out, p * 4 + n // 4)
                        for j in range(t + 1):
                            lo_col = max(0, j - (t - 3)) * P
                            for m, (l, r) in enumerate(split3((vh, wth), (vl, wtl))):
                                last = nc.tensor.matmul(ps_y[:, lo_col:], l[:, j], r[:, j, lo_col:],
                                                        start=(j == 0 and m == 0), stop=(j == t and m == 2))
                        last.then_inc(y_done, 1)

        def moved(u, dst, v_dst):
            kind, n, j0, cnt = units[u]
            ps = ps_t[:, u % 2, 0:cnt * P].rearrange("p (j t) -> p j t", j=cnt)
            if kind == "v":
                return v_dst[:, j0:j0 + cnt], ps
            t = steps[n][1]
            return dst[:, j0:j0 + cnt, (t % 4) * P:(t % 4 + 1) * P], ps

        @block.scalar
        def _(act):
            act.wait_ge(zeroed, 1)
            with act.Fori(0, SB_PAIRS) as p:
                def hi(u):
                    kind, n, j0, _ = units[u]
                    act.wait_ge(turned, p * U + u + 1)
                    if u == 0:
                        act.wait_ge(y_done, p * 4)
                    if kind == "w" and n % 4 == 0 and j0 == 0:
                        act.wait_ge(y_done, p * 4 + n // 4)
                    out, src = moved(u, wth, vh)
                    nc.scalar.activation(out, src, ACT.Copy).then_inc(hi_done, 1)

                def evacuate(m, h):
                    s, cols = m % 2, slice(h * HALF, (h + 1) * HALF)
                    if h:
                        act.wait_ge(ring.used[s], p * 3 + m // 2 + 1)
                    else:
                        act.wait_ge(half_done, p * PER + m + 1)
                        if kinds[m] != "x":
                            act.wait_ge(g_stored[s], (p * 3 + m // 2) * 16)
                        if kinds[m] == "x":
                            act.wait_ge(conv_step, (p * 3 + m // 2) * CONV)
                        if kinds[m] == "z":
                            act.wait_ge(silu_done[1], p * 2 + m // 2)
                    if kinds[m] == "x":
                        nc.scalar.activation(padded[:, CONV - 1 + h * HALF:CONV - 1 + (h + 1) * HALF], ps_g[:, h],
                                             ACT.Copy).then_inc(half_out[h], 1)
                    elif kinds[m] == "q":
                        nc.scalar.activation(out_tile[:, s, cols], ps_g[:, h], ACT.Copy).then_inc(half_out[h], 1)
                    else:
                        nc.scalar.activation(out_tile[:, s, cols], ps_g[:, h], ACT.Copy)
                        nc.scalar.activation(sigm[:, 1, cols], ps_g[:, h], ACT.Sigmoid).then_inc(half_out[h], 1)

                def sigmoid_of_conv(m):
                    act.wait_ge(conv_step, (p * 3 + m // 2 + 1) * CONV)
                    act.wait_ge(silu_done[0], p * 3 + m // 2)
                    nc.scalar.activation(sigm[:, 0], out_tile[:, 0], ACT.Sigmoid).then_inc(sigm_done, 1)

                hi(0)
                hi(1)
                for i in range(EVENTS):
                    if i < N:
                        t = steps[i][1]
                        act.wait_ge(scores, p * N + i + 1)
                        act.wait_ge(turned, p * U + (turned_by(i - 2) if i >= 2 else 0))
                        nc.scalar.activation(beta[:, i % 2, 0:(t + 1) * P], ps_z[:, 0:(t + 1) * P],
                                             ACT.Sigmoid, scale=0.125).then_inc(beta_done, 1)
                    n = i - LAG
                    if n >= 0:
                        for u in units_of(n):
                            hi(u)
                    for m in (0, 2, 4):
                        if i == min(event_of(m, 1) + 3, EVENTS - 1):
                            sigmoid_of_conv(m)
                    for m in range(PER):
                        for h in range(2):
                            if event_of(m, h) == i:
                                evacuate(m, h)
                    if n >= 0 and n % 4 == 3:
                        g = n // 4
                        rows = slice(64 * (g // 2), 64 * (g // 2) + 64)
                        act.wait_ge(y_done, p * 4 + g + 1)
                        if g == 0:
                            act.wait_ge(stored, p * 16)
                        nc.scalar.activation(y_tile[rows, (g % 2) * HALF:(g % 2 + 1) * HALF], ps_y[rows, :],
                                             ACT.Copy).then_inc(y_out, 1)

        @block.gpsimd
        def _(pool):
            with pool.Fori(0, SB_PAIRS) as p:
                def weigh(n):
                    cols = (steps[n][1] + 1) * P
                    pool.wait_ge(scanned, p * N + n + 1)
                    nc.gpsimd.tensor_tensor(beta[:, n % 2, 0:cols], beta[:, n % 2, 0:cols],
                                            rest[:, n % 2, S - cols + 1:S + 1], ALU.mult).then_inc(weighted, 1)

                for i in range(N + 1):
                    if i < N:
                        t = steps[i][1]
                        diag = beta[:, i % 2, t * P:(t + 1) * P]
                        pool.wait_ge(beta_done, p * N + i + 1)
                        nc.gpsimd.tensor_tensor(diag, diag, consts["before"][:], ALU.mult).then_inc(masked, 1)
                    if i:
                        weigh(i - 1)
                    for m in range(PER):
                        at = 2 + m * 2 * PASSES // PER_EVENT
                        if i == max(0, at - 2):
                            round_weights(nc, pool, ring, p * 3 + m // 2, m % 2)
                        if i == max(0, at - 2) + 1:
                            rest_of_weights(nc, pool, ring, p * 3 + m // 2, m % 2)

        @block.vector
        def _(dve):
            def split_qk(p, n_pairs):
                dve.wait_ge(loaded, n_pairs * 32)
                for n in range(2):
                    nc.vector.tensor_copy(qkh[:, n], qkv[:, n]).then_inc(qk_hi, 1)
                for n in range(2):
                    dve.wait_ge(qk_hi, n_pairs * 2 - 1 + n)
                    nc.vector.tensor_tensor(qkl[:, n], qkv[:, n], qkh[:, n].bitcast(F32),
                                            ALU.subtract).then_inc(qk_split, 1)

            nc.vector.memset(rest[:, :, S:S + 1], 1.0).then_inc(ones_set, 1)
            nc.vector.memset(padded[:, 0:CONV - 1], 0.0).then_inc(zeroed, 1)
            dve.wait_ge(ones_set, 1)
            dve.wait_ge(small_loaded, 32)
            split_qk(None, 1)
            with dve.Fori(0, SB_PAIRS) as p:
                def lo(u):
                    dve.wait_ge(hi_done, p * U + u + 1)
                    out, src = moved(u, wtl, vl)
                    hi = moved(u, wth, vh)[0].bitcast(F32)
                    nc.vector.tensor_tensor(out, src, hi, ALU.subtract).then_inc(lo_done, 1)

                def convolve(m, taps):
                    n = p * 3 + m // 2
                    for tap in taps:
                        if tap == 0:
                            dve.wait_ge(half_out[1], p * PER + m + 1)
                            dve.wait_ge(g_stored[0], n * 16)
                            nc.vector.tensor_scalar(out_tile[:, 0], padded[:, 0:S], cw[:, bass.ds(n, 1), 0],
                                                    cb[:, bass.ds(n, 1)], ALU.mult, ALU.add).then_inc(conv_step, 1)
                        else:
                            dve.wait_ge(conv_step, n * CONV + tap)
                            nc.vector.scalar_tensor_tensor(
                                out_tile[:, 0], padded[:, tap:tap + S], cw[:, bass.ds(n, 1), tap],
                                out_tile[:, 0], ALU.mult, ALU.add).then_inc(conv_step, 1)

                def silu(m):
                    s = m % 2
                    if kinds[m] == "x":
                        dve.wait_ge(sigm_done, p * 3 + m // 2 + 1)
                    else:
                        dve.wait_ge(half_out[1], p * PER + m + 1)
                    nc.vector.tensor_tensor(out_tile[:, s], out_tile[:, s], sigm[:, s], ALU.mult).then_inc(silu_done[s], 1)

                lo(0)
                lo(1)
                for i in range(EVENTS):
                    if i < N:
                        t = steps[i][1]
                        cols = (t + 1) * P
                        dve.wait_ge(masked, p * N + i + 1)
                        dve.wait_ge(scanned, p * N + i)
                        nc.vector.tensor_scalar(keep[:, 0:cols], beta[:, i % 2, 0:cols], -1.0, 1.0,
                                                ALU.mult, ALU.add).then_inc(keep_done, 1)
                        dve.wait_ge(keep_done, p * N + i + 1)
                        dve.wait_ge(weighted, p * N + (i - 1 if i >= 2 else 0))
                        down = keep[:, 0:cols][:, ::-1]
                        nc.vector.tensor_tensor_scan(rest[:, i % 2, S - cols:S][:, ::-1], down, down, 1.0,
                                                     ALU.mult, ALU.bypass).then_inc(scanned, 1)
                    n = i - LAG
                    if n >= 0:
                        for u in units_of(n):
                            lo(u)
                    for m in range(PER):
                        end = event_of(m, 1)
                        if kinds[m] == "x" and i == end + 1:
                            convolve(m, range(2) if end + 2 < EVENTS else range(CONV))
                        if kinds[m] == "x" and i == end + 2:
                            convolve(m, range(2, CONV))
                        if kinds[m] == "x" and i == min(end + 4, EVENTS - 1) or kinds[m] == "z" and i == end + 1:
                            silu(m)
                    if i == EVENTS - 1:
                        dve.wait_ge(scores, p * N + N)
                        split_qk(p, p + 2)


def ssd(nc, proj, y, dt, da, d_rows, ssd_gain, consts):
    with stage(nc) as ctx:
        def sb(n, shape, dt_=F32):
            return ctx.enter_context(nc.sbuf_tensor(f"ssd_{n}", shape, dt_))

        def ps(n, shape):
            return ctx.enter_context(nc.psum_tensor(f"ssd_{n}", shape, F32))

        def sem(n):
            return nc.alloc_semaphore(f"ssd_{n}")

        R = HPG
        xT, zT, yT = sb("xT", [P, GB, S]), sb("zT", [P, GB, S]), sb("yT", [P, GB, S])
        bcT = sb("bcT", [P, 2, S])
        bch, bcl = sb("bch", [P, 2, S], F32R), sb("bcl", [P, 2, S], F32R)
        drow, gain = sb("drow", [P, GROUPS * GB]), sb("gain", [P, GROUPS * GB])
        a_cs, to_end = (sb(n, [P, TB, SSD_HEADS]) for n in ("acs", "toend"))
        bth, btl = sb("bth", [P, 2, P], F32R), sb("btl", [P, 2, P], F32R)
        xd = sb("xd", [P, R, 64])
        xe = sb("xe", [P, R, 64])
        xdh, xdl, xeh, xel = (sb(n, [P, 2, R * 64], F32R) for n in ("xdh", "xdl", "xeh", "xel"))
        cb = sb("cb", [P, P])
        tri_da = sb("trida", [P, R, P])
        w = sb("w", [P, R, P])
        grown = sb("grown", [P, R, P])
        ce = sb("ce", [P, R, P])
        wh, wl, ceh, cel = (sb(n, [P, 2, R, P], F32R) for n in ("wh", "wl", "ceh", "cel"))
        whole = sb("whole", [P, 2, R])
        state = sb("state", [P, R, 64])
        sth, stl = sb("sth", [P, R * 64], F32R), sb("stl", [P, R * 64], F32R)
        rstd = sb("rstd", [P, S])
        ps_bc, ps_x, ps_a = ps("psbc", [P, 2, P]), ps("psx", [P, R, 64]), ps("psa", [P, R, P])
        ps_y, ps_s, ps_cs = ps("psy", [P, GB, 2, P]), ps("pss", [P, R, 64]), ps("pscs", [P, 2, TB * SSD_HEADS])

        small_loaded, cs_done, cs_exp, cs_read, cs_diff = (sem(n) for n in ("small", "cs", "csexp", "csread", "csdiff"))
        loaded, z_loaded, stored = sem("loaded"), sem("zloaded"), sem("stored")
        bc_hi, bc_split, skip_done = sem("bchi"), sem("bcsplit"), sem("skip")
        tri_done, bc_turned, x_turned, a_done = (sem(n) for n in ("tri", "bcturned", "xturned", "adone"))
        xd_done, xe_done, cb_done, seg_raw, seg_done = (sem(n) for n in ("xd", "xe", "cb", "segraw", "seg"))
        bt_hi, bt_split, xd_hi, xd_split, xe_hi, xe_split = (
            sem(n) for n in ("bthi", "btsplit", "xdhi", "xdsplit", "xehi", "xesplit"))
        decayed, w_done, w_hi, w_split = (sem(n) for n in ("decayed", "wdone", "whi", "wsplit"))
        grown_done, ce_done, ce_hi, ce_split = (sem(n) for n in ("grown", "cedone", "cehi", "cesplit"))
        y_mm, s_mm, y_done, state_scaled, state_done, st_hi, st_split = (
            sem(n) for n in ("ymm", "smm", "ydone", "scaled", "state", "sthi", "stsplit"))
        whole_kept = sem("whole")
        gated, squared, norm_mm, rooted, inverted, normed = (
            sem(n) for n in ("gated", "squared", "normmm", "rooted", "inverted", "normed"))

        block = ctx.enter_context(nc.Block())

        @block.sync
        def _(sp):
            sp.dma_start(drow[:], d_rows).then_inc(small_loaded, 16)
            sp.dma_start(gain[:], ssd_gain).then_inc(small_loaded, 16)
            with sp.Fori(0, GROUPS) as g:
                sp.wait_ge(ce_done, g * TB)
                sp.wait_ge(x_turned, g * TB)
                sp.wait_ge(bc_turned, g * TB)
                for n, b in enumerate((B0, C0)):
                    sp.dma_start(bcT[:, n], proj[bass.ds(g + b, 1)].rearrange("a p n -> (a p) n")).then_inc(loaded, 16)
                sp.wait_ge(skip_done, g * GB)
                sp.dma_start(xT[:], proj[bass.ds(g * GB + X0, GB)].rearrange("k p n -> p k n")).then_inc(loaded, 16)
                sp.wait_ge(norm_mm, g)
                sp.dma_start(zT[:], proj[bass.ds(g * GB + Z0, GB)].rearrange("k p n -> p k n")).then_inc(z_loaded, 16)
                sp.wait_ge(normed, g * GB + GB)
                sp.dma_start(y[bass.ds(g * GB + Y_SSD, GB)].rearrange("k p n -> p k n"), yT[:]).then_inc(stored, 16)
            sp.wait_ge(stored, 16 * GROUPS)

        @block.tensor
        def _(pe):
            da_all = da[:].rearrange("p c h -> p (c h)")
            nc.tensor.matmul(ps_cs[:, 0], consts["tri"][:], da_all, start=True, stop=True)
            nc.tensor.matmul(ps_cs[:, 1], consts["ones"][:], da_all, start=True, stop=True).then_inc(cs_done, 1)

            with pe.Fori(0, GROUPS) as g:
                def front(c):
                    n = g * TB + c
                    cols = slice(c * P, (c + 1) * P)
                    if c == 0:
                        pe.wait_ge(bc_split, g * 2 + 2)
                        pe.wait_ge(loaded, g * 48 + 48)
                    pe.wait_ge(bt_split, n)
                    pe.wait_ge(cb_done, n)
                    nc.tensor.transpose(ps_bc[:, 0], bcT[:, 0, cols], consts["ident"][:])
                    for j, (l, r) in enumerate(split3((bch, bch), (bcl, bcl))):
                        last = nc.tensor.matmul(ps_bc[:, 1], l[:, 0, cols], r[:, 1, cols], start=(j == 0), stop=(j == 2))
                    last.then_inc(bc_turned, 1)
                    pe.wait_ge(xd_done, n)
                    for b in range(GB):
                        last = nc.tensor.transpose(ps_x[:, 2 * b:2 * b + 2].rearrange("p r d -> p (r d)"),
                                                   xT[:, b, cols], consts["ident"][:])
                    last.then_inc(x_turned, 1)
                    pe.wait_ge(tri_done, n + 1)
                    pe.wait_ge(seg_raw, n)
                    pe.wait_ge(grown_done, n)
                    if c == 0:
                        pe.wait_ge(rooted, g)
                    for h in range(2):
                        last = nc.tensor.matmul(ps_a[:, 4 * h:4 * h + 4], consts["ones"][:],
                                                tri_da[:, 4 * h:4 * h + 4], start=True, stop=True)
                    last.then_inc(a_done, 1)

                def back(c):
                    n = g * TB + c
                    b = c % 2
                    pe.wait_ge(xd_split, n + 1)
                    pe.wait_ge(w_split, n + 1)
                    if c:
                        pe.wait_ge(ce_split, n + 1)
                        pe.wait_ge(st_split, n)
                    pe.wait_ge(y_done, n * 2)
                    for q in range(GB):
                        heads = slice(q * P, (q + 1) * P)
                        for j, (l, r) in enumerate(split3((xdh, wh), (xdl, wl))):
                            last = nc.tensor.matmul(ps_y[:, q], l[:, b, heads], r[:, b, 2 * q:2 * q + 2],
                                                    start=(j == 0), stop=(c == 0 and j == 2))
                        for j, (l, r) in enumerate(split3((sth, ceh), (stl, cel)) if c else ()):
                            last = nc.tensor.matmul(ps_y[:, q], l[:, heads], r[:, b, 2 * q:2 * q + 2],
                                                    start=False, stop=(j == 2))
                    last.then_inc(y_mm, 1)
                    pe.wait_ge(xe_split, n + 1)
                    pe.wait_ge(bt_split, n + 1)
                    pe.wait_ge(state_done, n)
                    for j, (l, r) in enumerate(split3((bth, xeh), (btl, xel))):
                        last = nc.tensor.matmul(ps_s[:], l[:, b], r[:, b], start=(j == 0), stop=(j == 2))
                    last.then_inc(s_mm, 1)

                for c in range(TB + 1):
                    if c < TB:
                        front(c)
                    if c:
                        back(c - 1)
                pe.wait_ge(squared, g + 1)
                for h in range(2):
                    for b in range(GB):
                        last = nc.tensor.matmul(ps_a[:, 4 * h:4 * h + 4], consts["ones"][:],
                                                zT[:, b, h * HALF:(h + 1) * HALF], start=(b == 0), stop=(b == GB - 1))
                last.then_inc(norm_mm, 1)

        @block.scalar
        def _(act):
            act.wait_ge(cs_diff, 1)
            nc.scalar.activation(to_end[:], to_end[:], ACT.Exp).then_inc(cs_exp, 1)
            with act.Fori(0, GROUPS) as g:
                act.wait_ge(loaded, g * 48 + 48)
                act.wait_ge(s_mm, g * TB)
                act.wait_ge(bc_split, g * 2)
                for i in range(2):
                    nc.scalar.activation(bch[:, i], bcT[:, i], ACT.Copy).then_inc(bc_hi, 1)
                for c in range(TB + 1):
                    n = g * TB + c
                    b = c % 2
                    if c < TB:
                        if c >= 2:
                            act.wait_ge(s_mm, n - 1)
                        act.wait_ge(bc_turned, n + 1)
                        nc.scalar.activation(bth[:, b], ps_bc[:, 0], ACT.Copy).then_inc(bt_hi, 1)
                        act.wait_ge(xd_done, n + 1)
                        nc.scalar.activation(xdh[:, b], xd[:].rearrange("p r d -> p (r d)"), ACT.Copy).then_inc(xd_hi, 1)
                        act.wait_ge(a_done, n + 1)
                        act.wait_ge(ce_done, n)
                        act.wait_ge(whole_kept, n)
                        nc.scalar.activation(grown[:], ps_a[:], ACT.Exp).then_inc(grown_done, 1)
                        act.wait_ge(seg_done, n + 1)
                        nc.scalar.activation(w[:], w[:], ACT.Exp).then_inc(decayed, 1)
                        act.wait_ge(xe_done, n + 1)
                        nc.scalar.activation(xeh[:, b], xe[:].rearrange("p r d -> p (r d)"), ACT.Copy).then_inc(xe_hi, 1)
                        act.wait_ge(w_done, n + 1)
                        nc.scalar.activation(wh[:, b], w[:], ACT.Copy).then_inc(w_hi, 1)
                        act.wait_ge(ce_done, n + 1)
                        nc.scalar.activation(ceh[:, b], ce[:], ACT.Copy).then_inc(ce_hi, 1)
                    if c:
                        act.wait_ge(state_done, n)
                        act.wait_ge(y_mm, n)
                        nc.scalar.activation(sth[:], state[:].rearrange("p r d -> p (r d)"), ACT.Copy).then_inc(st_hi, 1)
                act.wait_ge(gated, g + 1)
                nc.scalar.activation(zT[:], yT[:], ACT.Square).then_inc(squared, 1)
                act.wait_ge(norm_mm, g + 1)
                act.wait_ge(normed, g * GB)
                nc.scalar.activation(rstd[:], ps_a[:].rearrange("p r l -> p (r l)"), ACT.Sqrt,
                                     scale=1.0 / (GB * P), bias=consts["eps"][:]).then_inc(rooted, 1)

        @block.gpsimd
        def _(pool):
            with pool.Fori(0, GROUPS) as g:
                def decays(c):
                    pool.wait_ge(a_done, g * TB + c)
                    nc.gpsimd.tensor_tensor(
                        tri_da[:], consts["tri"][:, None, :].broadcast_to([P, R, P]),
                        da[:, c, bass.ds(g * R, R)][:, :, None].broadcast_to([P, R, P]), ALU.mult).then_inc(tri_done, 1)

                decays(0)
                for c in range(TB):
                    n = g * TB + c
                    pool.wait_ge(xd_done, n + 1)
                    pool.wait_ge(xe_split, n)
                    if c == 0:
                        pool.wait_ge(cs_exp, 1)
                    nc.gpsimd.tensor_tensor(
                        xe[:], xd[:], to_end[:, c, bass.ds(g * R, R)][:, :, None].broadcast_to([P, R, 64]),
                        ALU.mult).then_inc(xe_done, 1)
                    if c < TB - 1:
                        decays(c + 1)
                    pool.wait_ge(decayed, n + 1)
                    pool.wait_ge(cb_done, n + 1)
                    nc.gpsimd.tensor_tensor(w[:], w[:], cb[:, None, :].broadcast_to([P, R, P]),
                                            ALU.mult).then_inc(w_done, 1)
                    pool.wait_ge(grown_done, n + 1)
                    pool.wait_ge(ce_split, n)
                    nc.gpsimd.tensor_tensor(
                        ce[:], grown[:], bcT[:, 1, c * P:(c + 1) * P][:, None, :].broadcast_to([P, R, P]),
                        ALU.mult).then_inc(ce_done, 1)

        @block.vector
        def _(dve):
            dve.wait_ge(small_loaded, 32)
            dve.wait_ge(cs_done, 1)
            flat = "p c h -> p (c h)"
            nc.vector.tensor_copy(a_cs[:].rearrange(flat), ps_cs[:, 0]).then_inc(cs_read, 1)
            dve.wait_ge(cs_read, 1)
            nc.vector.tensor_tensor(to_end[:].rearrange(flat), ps_cs[:, 1], a_cs[:].rearrange(flat),
                                    ALU.subtract).then_inc(cs_diff, 1)
            with dve.Fori(0, GROUPS) as g:
                dve.wait_ge(loaded, g * 48 + 48)
                for i in range(2):
                    dve.wait_ge(bc_hi, g * 2 + i + 1)
                    nc.vector.tensor_tensor(bcl[:, i], bcT[:, i], bch[:, i].bitcast(F32), ALU.subtract).then_inc(bc_split, 1)
                dve.wait_ge(stored, g * 16)
                for b in range(GB):
                    nc.vector.tensor_scalar(yT[:, b], xT[:, b], drow[:, bass.ds(g * GB + b, 1)], None,
                                            ALU.mult).then_inc(skip_done, 1)
                for c in range(TB + 1):
                    n = g * TB + c
                    b = c % 2
                    if c < TB:
                        heads = bass.ds(g * R, R)
                        if c >= 2:
                            dve.wait_ge(s_mm, n - 1)
                        dve.wait_ge(x_turned, n + 1)
                        dve.wait_ge(xd_hi, n)
                        dve.wait_ge(xe_done, n)
                        dve.wait_ge(xd_split, n)
                        nc.vector.tensor_tensor(xd[:], ps_x[:], dt[:, c, heads][:, :, None].broadcast_to([P, R, 64]),
                                                ALU.mult).then_inc(xd_done, 1)
                        dve.wait_ge(bc_turned, n + 1)
                        dve.wait_ge(bt_hi, n + 1)
                        dve.wait_ge(w_done, n)
                        nc.vector.tensor_tensor(cb[:], ps_bc[:, 1], consts["tri"][:], ALU.mult).then_inc(cb_done, 1)
                        dve.wait_ge(bt_hi, n + 1)
                        nc.vector.tensor_tensor(btl[:, b], ps_bc[:, 0], bth[:, b].bitcast(F32),
                                                ALU.subtract).then_inc(bt_split, 1)
                        dve.wait_ge(grown_done, n + 1)
                        nc.vector.tensor_copy(whole[:, b], grown[:, :, P - 1]).then_inc(whole_kept, 1)
                        dve.wait_ge(w_split, n)
                        nc.vector.tensor_tensor(w[:], ps_a[:], a_cs[:, c, heads][:, :, None].broadcast_to([P, R, P]),
                                                ALU.subtract).then_inc(seg_raw, 1)
                        dve.wait_ge(seg_raw, n + 1)
                        nc.vector.tensor_scalar(w[:], w[:], 0.0, None, ALU.min).then_inc(seg_done, 1)
                        dve.wait_ge(xd_hi, n + 1)
                        nc.vector.tensor_tensor(xdl[:, b], xd[:].rearrange("p r d -> p (r d)"), xdh[:, b].bitcast(F32),
                                                ALU.subtract).then_inc(xd_split, 1)
                        dve.wait_ge(xe_hi, n + 1)
                        nc.vector.tensor_tensor(xel[:, b], xe[:].rearrange("p r d -> p (r d)"), xeh[:, b].bitcast(F32),
                                                ALU.subtract).then_inc(xe_split, 1)
                        dve.wait_ge(w_hi, n + 1)
                        nc.vector.tensor_tensor(wl[:, b], w[:], wh[:, b].bitcast(F32), ALU.subtract).then_inc(w_split, 1)
                        dve.wait_ge(ce_hi, n + 1)
                        nc.vector.tensor_tensor(cel[:, b], ce[:], ceh[:, b].bitcast(F32),
                                                ALU.subtract).then_inc(ce_split, 1)
                    if c:
                        m = n - 1
                        dve.wait_ge(y_mm, m + 1)
                        cols = slice((c - 1) * P, c * P)
                        for h in range(2):
                            rows = slice(64 * h, 64 * h + 64)
                            nc.vector.tensor_tensor(yT[rows, :, cols], ps_y[rows, :, h], yT[rows, :, cols],
                                                    ALU.add).then_inc(y_done, 1)
                        dve.wait_ge(s_mm, m + 1)
                        if c > 1:
                            nc.vector.tensor_tensor(state[:], state[:],
                                                    whole[:, 1 - b, :, None].broadcast_to([P, R, 64]),
                                                    ALU.mult).then_inc(state_scaled, 1)
                            dve.wait_ge(state_scaled, g * (TB - 1) + c - 1)
                            nc.vector.tensor_tensor(state[:], ps_s[:], state[:], ALU.add).then_inc(state_done, 1)
                        else:
                            nc.vector.tensor_copy(state[:], ps_s[:]).then_inc(state_done, 1)
                        dve.wait_ge(st_hi, m + 1)
                        nc.vector.tensor_tensor(stl[:], state[:].rearrange("p r d -> p (r d)"), sth[:].bitcast(F32),
                                                ALU.subtract).then_inc(st_split, 1)
                dve.wait_ge(z_loaded, g * 16 + 16)
                dve.wait_ge(y_done, (g * TB + TB) * 2)
                nc.vector.tensor_tensor(yT[:], yT[:], zT[:], ALU.mult).then_inc(gated, 1)
                dve.wait_ge(rooted, g + 1)
                nc.vector.reciprocal(rstd[:], rstd[:]).then_inc(inverted, 1)
                dve.wait_ge(inverted, g + 1)
                for b in range(GB):
                    nc.vector.scalar_tensor_tensor(yT[:, b], yT[:, b], gain[:, bass.ds(g * GB + b, 1)], rstd[:],
                                                   ALU.mult, ALU.mult).then_inc(normed, 1)


def memory_keys_values(nc, w_kv, kv, xh, xl, consts):
    with stage(nc) as ctx:
        ring = Ring(nc, ctx, "kv", consts)
        n_blocks = 2 * KB
        out_tile = ctx.enter_context(nc.sbuf_tensor("kv_out", [P, 2, M], F32))
        ps = ctx.enter_context(nc.psum_tensor("kv_ps", [P, 2, HALF], F32))
        evacuated = [nc.alloc_semaphore(f"kv_evac{s}") for s in range(2)]
        stored = [nc.alloc_semaphore(f"kv_stored{s}") for s in range(2)]
        block = ctx.enter_context(nc.Block())

        @block.sync
        def _(sp):
            for s in range(2):
                load_weights(sp, ring, w_kv, 0, s, s)
            with sp.Fori(0, n_blocks // 2 - 1) as i:
                for s in range(2):
                    load_weights(sp, ring, w_kv, i + 1, s, i * 2 + s + 2)
                    sp.wait_ge(evacuated[s], i + 1)
                    sp.dma_start(kv[bass.ds(i * 2 + s, 1)].rearrange("a p n -> (a p) n"),
                                 out_tile[:, s]).then_inc(stored[s], 16)
            for s in range(2):
                sp.wait_ge(evacuated[s], n_blocks // 2)
                sp.dma_start(kv[n_blocks - 2 + s], out_tile[:, s]).then_inc(stored[s], 16)
            for s in range(2):
                sp.wait_ge(stored[s], 16 * n_blocks // 2)

        @block.gpsimd
        def _(pool):
            with pool.Fori(0, n_blocks // 2) as i:
                for s in range(2):
                    split_weights(nc, pool, ring, i, s)

        @block.tensor
        def _(pe):
            with pe.Fori(0, n_blocks // 2) as i:
                for s in range(2):
                    pe.wait_ge(ring.split[s], i + 1)
                    pe.wait_ge(evacuated[s], i)
                    product(nc, ring, s, xh, xl, ps[:, s], M).then_inc(ring.used[s], 1)

        @block.scalar
        def _(act):
            with act.Fori(0, n_blocks // 2) as i:
                for s in range(2):
                    act.wait_ge(ring.used[s], i + 1)
                    act.wait_ge(stored[s], i * 16)
                    nc.scalar.activation(out_tile[:, s], ps[:, s, 0:M], ACT.Copy).then_inc(evacuated[s], 1)


def project_gates(nc, w_kv, kv, xh, xl, consts):
    with stage(nc) as ctx:
        ring = Ring(nc, ctx, "gt", consts)
        n_blocks = 24
        out_tile = ctx.enter_context(nc.sbuf_tensor("gt_out", [P, 2, S], F32))
        ps = ctx.enter_context(nc.psum_tensor("gt_ps", [P, 2, S], F32))
        evacuated = [nc.alloc_semaphore(f"gt_evac{s}") for s in range(2)]
        stored = [nc.alloc_semaphore(f"gt_stored{s}") for s in range(2)]
        block = ctx.enter_context(nc.Block())

        @block.sync
        def _(sp):
            for s in range(2):
                load_weights(sp, ring, w_kv, 0, s, s + G0)
            with sp.Fori(0, n_blocks // 2 - 1) as i:
                for s in range(2):
                    load_weights(sp, ring, w_kv, i + 1, s, i * 2 + s + 2 + G0)
                    sp.wait_ge(evacuated[s], i + 1)
                    sp.dma_start(kv[bass.ds(i * 2 + s + G0, 1)].rearrange("a p n -> (a p) n"),
                                 out_tile[:, s]).then_inc(stored[s], 16)
            for s in range(2):
                sp.wait_ge(evacuated[s], n_blocks // 2)
                sp.dma_start(kv[G0 + n_blocks - 2 + s], out_tile[:, s]).then_inc(stored[s], 16)
            for s in range(2):
                sp.wait_ge(stored[s], 16 * n_blocks // 2)

        @block.gpsimd
        def _(pool):
            with pool.Fori(0, n_blocks // 2) as i:
                for s in range(2):
                    split_weights(nc, pool, ring, i, s)

        @block.tensor
        def _(pe):
            with pe.Fori(0, n_blocks // 2) as i:
                for s in range(2):
                    pe.wait_ge(ring.split[s], i + 1)
                    pe.wait_ge(evacuated[s], i)
                    product(nc, ring, s, xh, xl, ps[:, s], S).then_inc(ring.used[s], 1)

        @block.scalar
        def _(act):
            with act.Fori(0, n_blocks // 2) as i:
                for s in range(2):
                    act.wait_ge(ring.used[s], i + 1)
                    act.wait_ge(stored[s], i * 16)
                    nc.scalar.activation(out_tile[:, s], ps[:, s], ACT.Sigmoid).then_inc(evacuated[s], 1)


def memory_attention(nc, proj, kv, y, consts):
    with stage(nc) as ctx:
        def sb(n, shape, dt=F32):
            return ctx.enter_context(nc.sbuf_tensor(f"ma_{n}", shape, dt))

        def sem(n):
            return nc.alloc_semaphore(f"ma_{n}")

        DB = 2
        qT, kT, vT = sb("qT", [P, DB, S]), sb("kT", [P, DB, M]), sb("vT", [P, DB, M])
        qh, ql = sb("qh", [P, DB, S], F32R), sb("ql", [P, DB, S], F32R)
        kh, kl = sb("kh", [P, DB, M], F32R), sb("kl", [P, DB, M], F32R)
        vh, vl = sb("vh", [P, MB, M], F32R), sb("vl", [P, MB, M], F32R)
        top, less, total, share = (sb(n, [P, 2]) for n in ("top", "less", "total", "share"))
        e, prob = sb("e", [P, 2, M]), sb("prob", [P, 2, M])
        pth, ptl = sb("pth", [P, MB, S], F32R), sb("ptl", [P, MB, S], F32R)
        y_tile = sb("y", [P, DB, S])
        ps_s = ctx.enter_context(nc.psum_tensor("ma_pss", [P, 2, HALF], F32))
        ps_t = ctx.enter_context(nc.psum_tensor("ma_pst", [P, 2, HALF], F32))
        ps_v = ctx.enter_context(nc.psum_tensor("ma_psv", [P, MB, M], F32))
        ps_y = ctx.enter_context(nc.psum_tensor("ma_psy", [P, 2, HALF], F32))
        loaded, k_hi, q_hi, k_split, q_split = (sem(n) for n in ("ld", "khi", "qhi", "ksplit", "qsplit"))
        v_turned, v_hi, v_split = sem("vturned"), sem("vhi"), sem("vsplit")
        scores, topped, lessened, e_done, inverted, prob_done = (
            sem(n) for n in ("scores", "topped", "less", "e", "inverted", "prob"))
        turned, pt_hi, pt_split, y_mm, y_out, stored = (
            sem(n) for n in ("turned", "pthi", "ptsplit", "ymm", "yout", "stored"))
        block = ctx.enter_context(nc.Block())

        @block.sync
        def _(sp):
            with sp.Fori(0, MEM_HEADS) as h:
                sp.wait_ge(q_split, h)
                sp.wait_ge(k_split, h)
                sp.wait_ge(v_turned, h)
                for dst, src, b in ((kT, kv, 0), (vT, kv, KB), (qT, proj, MQ0)):
                    sp.dma_start(dst[:], src[bass.ds(h * DB + b, DB)].rearrange("k p n -> p k n")).then_inc(loaded, 16)
                sp.wait_ge(y_out, h * 4 + 4)
                sp.dma_start(y[bass.ds(h * DB + Y_MEM, DB)].rearrange("k p n -> p k n"), y_tile[:]).then_inc(stored, 16)
            sp.wait_ge(stored, 16 * MEM_HEADS)

        @block.tensor
        def _(pe):
            with pe.Fori(0, MEM_HEADS) as h:
                pe.wait_ge(loaded, h * 48 + 48)
                for m in range(MB):
                    for d in range(DB):
                        last = nc.tensor.transpose(ps_v[:, m, d * P:(d + 1) * P], vT[:, d, m * P:(m + 1) * P],
                                                   consts["ident"][:])
                last.then_inc(v_turned, 1)
                pe.wait_ge(q_split, h + 1)
                pe.wait_ge(k_split, h + 1)
                for t in range(TB + 1):
                    n = h * TB + t
                    if t < TB:
                        pe.wait_ge(e_done, n - 1 if t >= 2 else h * TB)
                        for d in range(DB):
                            for j, (l, r) in enumerate(split3((qh, kh), (ql, kl))):
                                last = nc.tensor.matmul(ps_s[:, t % 2, 0:M], l[:, d, t * P:(t + 1) * P], r[:, d],
                                                        start=(d == 0 and j == 0), stop=(d == DB - 1 and j == 2))
                        last.then_inc(scores, 1)
                    if t:
                        pe.wait_ge(prob_done, n)
                        pe.wait_ge(pt_split, n - 2 if t >= 3 else h * TB)
                        for m in range(MB):
                            last = nc.tensor.transpose(ps_t[:, (t - 1) % 2, m * P:(m + 1) * P],
                                                       prob[:, (t - 1) % 2, m * P:(m + 1) * P], consts["ident"][:])
                        last.then_inc(turned, 1)
                pe.wait_ge(pt_split, h * TB + TB)
                pe.wait_ge(v_split, h + 1)
                for u in range(4):
                    d, half = u // 2, u % 2
                    pe.wait_ge(y_out, h * 4 + (u - 1 if u >= 2 else 0))
                    for m in range(MB):
                        for j, (l, r) in enumerate(split3((vh, pth), (vl, ptl))):
                            last = nc.tensor.matmul(ps_y[:, u % 2], l[:, m, d * P:(d + 1) * P],
                                                    r[:, m, half * HALF:(half + 1) * HALF],
                                                    start=(m == 0 and j == 0), stop=(m == MB - 1 and j == 2))
                    last.then_inc(y_mm, 1)

        @block.scalar
        def _(act):
            with act.Fori(0, MEM_HEADS) as h:
                act.wait_ge(loaded, h * 48 + 48)
                act.wait_ge(y_mm, h * 4)
                act.wait_ge(scores, h * TB)
                nc.scalar.activation(qh[:], qT[:], ACT.Copy).then_inc(q_hi, 1)
                nc.scalar.activation(kh[:], kT[:], ACT.Copy).then_inc(k_hi, 1)
                act.wait_ge(v_turned, h + 1)
                nc.scalar.activation(vh[:], ps_v[:], ACT.Copy).then_inc(v_hi, 1)
                for t in range(TB + 1):
                    n = h * TB + t
                    if t < TB:
                        act.wait_ge(lessened, n + 1)
                        act.wait_ge(prob_done, n - 1 if t >= 2 else h * TB)
                        nc.scalar.activation(e[:, t % 2], ps_s[:, t % 2, 0:M], ACT.Exp, scale=MEM_SCALE,
                                             bias=less[:, t % 2:t % 2 + 1],
                                             accum_out=total[:, t % 2:t % 2 + 1]).then_inc(e_done, 1)
                    if t:
                        act.wait_ge(turned, n)
                        nc.scalar.activation(pth[:, :, (t - 1) * P:t * P],
                                             ps_t[:, (t - 1) % 2, 0:M].rearrange("p (m t) -> p m t", m=MB),
                                             ACT.Copy).then_inc(pt_hi, 1)
                for u in range(4):
                    d, half = u // 2, u % 2
                    act.wait_ge(y_mm, h * 4 + u + 1)
                    act.wait_ge(stored, h * 16)
                    nc.scalar.activation(y_tile[:, d, half * HALF:(half + 1) * HALF], ps_y[:, u % 2],
                                         ACT.Copy).then_inc(y_out, 1)

        @block.vector
        def _(dve):
            with dve.Fori(0, MEM_HEADS) as h:
                dve.wait_ge(q_hi, h + 1)
                nc.vector.tensor_tensor(ql[:], qT[:], qh[:].bitcast(F32), ALU.subtract).then_inc(q_split, 1)
                dve.wait_ge(k_hi, h + 1)
                nc.vector.tensor_tensor(kl[:], kT[:], kh[:].bitcast(F32), ALU.subtract).then_inc(k_split, 1)
                dve.wait_ge(v_hi, h + 1)
                nc.vector.tensor_tensor(vl[:], ps_v[:], vh[:].bitcast(F32), ALU.subtract).then_inc(v_split, 1)
                for t in range(TB + 1):
                    n = h * TB + t
                    s = slice(t % 2, t % 2 + 1)
                    if t < TB:
                        dve.wait_ge(scores, n + 1)
                        nc.vector.tensor_reduce(top[:, s], ps_s[:, t % 2, 0:M], AX_X, ALU.max).then_inc(topped, 1)
                        dve.wait_ge(topped, n + 1)
                        dve.wait_ge(e_done, n - 1 if t >= 2 else h * TB)
                        nc.vector.tensor_scalar(less[:, s], top[:, s], -MEM_SCALE, None, ALU.mult).then_inc(lessened, 1)
                        dve.wait_ge(e_done, n + 1)
                        nc.vector.reciprocal(share[:, s], total[:, s]).then_inc(inverted, 1)
                        dve.wait_ge(inverted, n + 1)
                        dve.wait_ge(turned, n - 1 if t >= 2 else h * TB)
                        nc.vector.tensor_scalar(prob[:, t % 2], e[:, t % 2], share[:, s], None,
                                                ALU.mult).then_inc(prob_done, 1)
                    if t:
                        dve.wait_ge(pt_hi, n)
                        cols = slice((t - 1) * P, t * P)
                        nc.vector.tensor_tensor(ptl[:, :, cols],
                                                ps_t[:, (t - 1) % 2, 0:M].rearrange("p (m t) -> p m t", m=MB),
                                                pth[:, :, cols].bitcast(F32), ALU.subtract).then_inc(pt_split, 1)


def merge_branches(nc, w_out, proj, y, merged, consts):
    gates_of = (0, 1, 1, 2)
    with stage(nc) as ctx:
        def sb(n, shape, dt=F32):
            return ctx.enter_context(nc.sbuf_tensor(f"mg_{n}", shape, dt))

        def sem(n):
            return nc.alloc_semaphore(f"mg_{n}")

        ring = Ring(nc, ctx, "mg", consts)
        raw = sb("raw", [P, 2, S])
        yh, yl = sb("yh", [P, KB, S], F32R), sb("yl", [P, KB, S], F32R)
        gate, gated = sb("gate", [P, 2, S]), sb("gated", [P, 2, S])
        ps = ctx.enter_context(nc.psum_tensor("mg_ps", [P, 2, S], F32))
        y_loaded = [sem(f"yld{s}") for s in range(2)]
        gate_loaded = [sem(f"gld{s}") for s in range(2)]
        y_hi, y_split, gated_done, summed = sem("yhi"), sem("ysplit"), sem("gated"), sem("summed")
        multiplied = [sem(f"mult{s}") for s in range(2)]
        cleared = sem("cleared")
        block = ctx.enter_context(nc.Block())
        NP = KB // 2

        @block.sync
        def _(sp):
            for part in range(4):
                for k in range(KB):
                    sp.wait_ge(y_split, part * KB + (k - 1 if k >= 2 else 0))
                    sp.dma_start(raw[:, k % 2], y[part * KB + k]).then_inc(y_loaded[k % 2], 16)
                with sp.Fori(0, NP) as i:
                    for s in range(2):
                        load_weights(sp, ring, w_out, i + part * NP, s, i * 2 + s + part * KB)
                        sp.wait_ge(multiplied[s], i + part * NP)
                        sp.dma_start(gate[:, s], proj[bass.ds(i * 2 + s + G0 + gates_of[part] * KB, 1)]
                                     .rearrange("a p n -> (a p) n")).then_inc(gate_loaded[s], 16)

        @block.gpsimd
        def _(pool):
            with pool.Fori(0, 4 * NP) as i:
                for s in range(2):
                    split_weights(nc, pool, ring, i, s)

        @block.scalar
        def _(act):
            for part in range(4):
                for k in range(KB):
                    act.wait_ge(y_loaded[k % 2], 16 * (part * NP + k // 2 + 1))
                    if k == 0 and part:
                        for s in range(2):
                            act.wait_ge(ring.used[s], part * NP)
                    nc.scalar.activation(yh[:, k], raw[:, k % 2], ACT.Copy).then_inc(y_hi, 1)

        @block.tensor
        def _(pe):
            for part in range(4):
                pe.wait_ge(y_split, part * KB + KB)
                with pe.Fori(part * NP, part * NP + NP) as i:
                    for s in range(2):
                        pe.wait_ge(ring.split[s], i + 1)
                        pe.wait_ge(multiplied[s], i)
                        product(nc, ring, s, yh, yl, ps[:, s], S).then_inc(ring.used[s], 1)

        @block.vector
        def _(dve):
            nc.vector.memset(merged[:], 0.0).then_inc(cleared, 1)
            dve.wait_ge(cleared, 1)
            for part in range(4):
                for k in range(KB):
                    n = part * KB + k
                    dve.wait_ge(y_hi, n + 1)
                    nc.vector.tensor_tensor(yl[:, k], raw[:, k % 2], yh[:, k].bitcast(F32),
                                            ALU.subtract).then_inc(y_split, 1)
                with dve.Fori(part * NP, part * NP + NP) as i:
                    for s in range(2):
                        dve.wait_ge(ring.used[s], i + 1)
                        dve.wait_ge(gate_loaded[s], i * 16 + 16)
                        dve.wait_ge(summed, i * 2 + s)
                        nc.vector.tensor_tensor(gated[:, s], ps[:, s], gate[:, s], ALU.mult).then_inc(multiplied[s], 1)
                        dve.wait_ge(multiplied[s], i + 1)
                        row = merged[:, bass.ds(i * 2 + s - part * KB, 1)].rearrange("p a n -> p (a n)")
                        nc.vector.tensor_tensor(row, row, gated[:, s], ALU.add).then_inc(summed, 1)


def split_blocks(nc, name, x, xh, xl):
    with stage(nc) as ctx:
        hi_done = nc.alloc_semaphore(f"{name}_hi")
        block = ctx.enter_context(nc.Block())

        @block.scalar
        def _(act):
            for k in range(KB):
                nc.scalar.activation(xh[:, k], x[:, k], ACT.Copy).then_inc(hi_done, 1)

        @block.vector
        def _(dve):
            for k in range(KB):
                dve.wait_ge(hi_done, k + 1)
                nc.vector.tensor_tensor(xl[:, k], x[:, k], xh[:, k].bitcast(F32), ALU.subtract)


def output_projection(nc, w_o, xh, xl, mix, consts):
    with stage(nc) as ctx:
        ring = Ring(nc, ctx, "wo", consts)
        ps = ctx.enter_context(nc.psum_tensor("wo_ps", [P, 2, S], F32))
        evacuated = [nc.alloc_semaphore(f"wo_evac{s}") for s in range(2)]
        block = ctx.enter_context(nc.Block())

        @block.sync
        def _(sp):
            with sp.Fori(0, KB // 2) as i:
                for s in range(2):
                    load_weights(sp, ring, w_o, i, s, i * 2 + s)

        @block.gpsimd
        def _(pool):
            with pool.Fori(0, KB // 2) as i:
                for s in range(2):
                    split_weights(nc, pool, ring, i, s)

        @block.tensor
        def _(pe):
            with pe.Fori(0, KB // 2) as i:
                for s in range(2):
                    pe.wait_ge(ring.split[s], i + 1)
                    pe.wait_ge(evacuated[s], i)
                    product(nc, ring, s, xh, xl, ps[:, s], S).then_inc(ring.used[s], 1)

        @block.scalar
        def _(act):
            with act.Fori(0, KB // 2) as i:
                for s in range(2):
                    act.wait_ge(ring.used[s], i + 1)
                    nc.scalar.activation(mix[:, bass.ds(i * 2 + s, 1)].rearrange("p a n -> p (a n)"), ps[:, s],
                                         ACT.Copy).then_inc(evacuated[s], 1)


def add_normed(nc, name, xT, gain_row, base, dst, consts):
    with stage(nc) as ctx:
        def sb(n, shape, dt=F32):
            return ctx.enter_context(nc.sbuf_tensor(f"{name}_{n}", shape, dt))

        def sem(n):
            return nc.alloc_semaphore(f"{name}_{n}")

        gain, tile, square, scaled = sb("gain", [P, D]), sb("tile", [P, 2, D]), sb("sq", [P, D]), sb("scaled", [P, 2, D])
        sums, root, rstd = sb("sums", [P, TB]), sb("root", [P, TB]), sb("rstd", [P, TB])
        ps = ctx.enter_context(nc.psum_tensor(f"{name}_ps", [P, 2, D], F32))
        gain_loaded = sem("gain")
        loaded, stored = [sem(f"ld{s}") for s in range(2)], [sem(f"st{s}") for s in range(2)]
        turned, summed, rooted, inverted, scaled_done, added = (
            sem(n) for n in ("turned", "summed", "rooted", "inverted", "scaled_done", "added"))
        block = ctx.enter_context(nc.Block())

        @block.sync
        def _(sp):
            sp.dma_start(gain[:], gain_row).then_inc(gain_loaded, 16)
            for t in range(TB + 1):
                if t < TB:
                    if t >= 2:
                        sp.wait_ge(stored[t % 2], 16 * (t // 2))
                    sp.dma_start(tile[:, t % 2], base[t * P:(t + 1) * P, :]).then_inc(loaded[t % 2], 16)
                if t:
                    sp.wait_ge(added, t)
                    sp.dma_start(dst[(t - 1) * P:t * P, :], tile[:, (t - 1) % 2]).then_inc(stored[(t - 1) % 2], 16)
            for s in range(2):
                sp.wait_ge(stored[s], 16 * TB // 2)

        @block.tensor
        def _(pe):
            for t in range(TB):
                if t >= 2:
                    pe.wait_ge(scaled_done, t - 1)
                for k in range(KB):
                    last = nc.tensor.transpose(ps[:, t % 2, k * P:(k + 1) * P], xT[:, k, t * P:(t + 1) * P],
                                               consts["ident"][:])
                last.then_inc(turned, 1)

        @block.scalar
        def _(act):
            for t in range(TB):
                act.wait_ge(turned, t + 1)
                nc.scalar.activation(square[:], ps[:, t % 2], ACT.Square, accum_out=sums[:, t:t + 1]).then_inc(summed, 1)
                act.wait_ge(summed, t + 1)
                nc.scalar.activation(root[:, t:t + 1], sums[:, t:t + 1], ACT.Sqrt, scale=1.0 / D,
                                     bias=consts["eps"][:]).then_inc(rooted, 1)

        @block.vector
        def _(dve):
            dve.wait_ge(gain_loaded, 16)
            for t in range(TB):
                dve.wait_ge(rooted, t + 1)
                nc.vector.reciprocal(rstd[:, t:t + 1], root[:, t:t + 1]).then_inc(inverted, 1)
                dve.wait_ge(inverted, t + 1)
                nc.vector.scalar_tensor_tensor(scaled[:, t % 2], ps[:, t % 2], rstd[:, t:t + 1], gain[:],
                                               ALU.mult, ALU.mult).then_inc(scaled_done, 1)
                dve.wait_ge(scaled_done, t + 1)
                dve.wait_ge(loaded[t % 2], 16 * (t // 2 + 1))
                nc.vector.tensor_tensor(tile[:, t % 2], tile[:, t % 2], scaled[:, t % 2], ALU.add).then_inc(added, 1)


def mlp(nc, w_up, w_down, xh, xl, out, consts):
    with stage(nc) as ctx:
        def sb(n, shape, dt=F32):
            return ctx.enter_context(nc.sbuf_tensor(f"ff_{n}", shape, dt))

        def sem(n):
            return nc.alloc_semaphore(f"ff_{n}")

        ring = Ring(nc, ctx, "ff", consts)
        fh, fl = sb("fh", [P, KB, S], F32R), sb("fl", [P, KB, S], F32R)
        positive, square = sb("pos", [P, 2, S]), sb("sq", [P, 2, S])
        ps = ctx.enter_context(nc.psum_tensor("ff_ps", [P, 2, S], F32))
        pos_done, sq_done, f_hi, f_split = ([sem(f"{n}{s}") for s in range(2)] for n in ("posdone", "sqdone", "fhi", "fsplit"))
        added = [sem(f"added{s}") for s in range(2)]
        cleared = sem("cleared")
        NP = KB // 2
        block = ctx.enter_context(nc.Block())

        @block.sync
        def _(sp):
            with sp.Fori(0, FF_CHUNKS) as f:
                with sp.Fori(0, NP) as i:
                    for s in range(2):
                        load_weights(sp, ring, w_up, f * 2 * NP + i, s, f * KB + i * 2 + s)
                with sp.Fori(0, NP) as i:
                    for s in range(2):
                        load_weights(sp, ring, w_down, f * 2 * NP + NP + i, s, f * KB + i * 2 + s)

        @block.gpsimd
        def _(pool):
            with pool.Fori(0, FF_CHUNKS * 2 * NP) as i:
                for s in range(2):
                    split_weights(nc, pool, ring, i, s)

        @block.tensor
        def _(pe):
            with pe.Fori(0, FF_CHUNKS) as f:
                with pe.Fori(0, NP) as i:
                    for s in range(2):
                        pe.wait_ge(ring.split[s], f * 2 * NP + i + 1)
                        pe.wait_ge(pos_done[s], f * NP + i)
                        pe.wait_ge(added[s], f * NP)
                        product(nc, ring, s, xh, xl, ps[:, s], S).then_inc(ring.used[s], 1)
                with pe.Fori(0, NP) as i:
                    for s in range(2):
                        for r in range(2):
                            pe.wait_ge(f_split[r], f * NP + NP)
                        pe.wait_ge(ring.split[s], f * 2 * NP + NP + i + 1)
                        pe.wait_ge(added[s], f * NP + i)
                        product(nc, ring, s, fh, fl, ps[:, s], S).then_inc(ring.used[s], 1)

        @block.scalar
        def _(act):
            with act.Fori(0, FF_CHUNKS) as f:
                with act.Fori(0, NP) as i:
                    for s in range(2):
                        act.wait_ge(ring.used[s], f * 2 * NP + i + 1)
                        act.wait_ge(sq_done[s], f * NP + i)
                        nc.scalar.activation(positive[:, s], ps[:, s], ACT.Relu).then_inc(pos_done[s], 1)
                        act.wait_ge(sq_done[s], f * NP + i + 1)
                        nc.scalar.activation(fh[:, bass.ds(i * 2 + s, 1)].rearrange("p a n -> p (a n)"),
                                             square[:, s], ACT.Copy).then_inc(f_hi[s], 1)

        @block.vector
        def _(dve):
            nc.vector.memset(out[:], 0.0).then_inc(cleared, 1)
            dve.wait_ge(cleared, 1)
            with dve.Fori(0, FF_CHUNKS) as f:
                with dve.Fori(0, NP) as i:
                    for s in range(2):
                        dve.wait_ge(pos_done[s], f * NP + i + 1)
                        dve.wait_ge(f_split[s], f * NP + i)
                        nc.vector.tensor_tensor(square[:, s], positive[:, s], positive[:, s],
                                                ALU.mult).then_inc(sq_done[s], 1)
                        dve.wait_ge(f_hi[s], f * NP + i + 1)
                        one = bass.ds(i * 2 + s, 1)
                        nc.vector.tensor_tensor(fl[:, one].rearrange("p a n -> p (a n)"), square[:, s],
                                                fh[:, one].rearrange("p a n -> p (a n)").bitcast(F32),
                                                ALU.subtract).then_inc(f_split[s], 1)
                with dve.Fori(0, NP) as i:
                    for s in range(2):
                        dve.wait_ge(ring.used[s], f * 2 * NP + NP + i + 1)
                        row = out[:, bass.ds(i * 2 + s, 1)].rearrange("p a n -> p (a n)")
                        nc.vector.tensor_tensor(row, ps[:, s], row, ALU.add).then_inc(added[s], 1)


def set_constants(nc, consts):
    with stage(nc) as ctx:
        set_, shaped = (nc.alloc_semaphore("const_set")), (nc.alloc_semaphore("const_shaped"))
        block = ctx.enter_context(nc.Block())

        @block.gpsimd
        def _(pool):
            for name, value in (("ident", 0.0), ("tri", 1.0), ("before", 1.0), ("ones", 1.0), ("one", 1.0), ("eps", EPS)):
                nc.gpsimd.memset(consts[name][:], value).then_inc(set_, 1)
            pool.wait_ge(set_, 6)
            ident, tri, before = consts["ident"][:], consts["tri"][:], consts["before"][:]
            nc.gpsimd.affine_select(out=ident, in_=ident, pattern=[[-1, P]], compare_op=ALU.not_equal, fill=1.0,
                                    base=0, channel_multiplier=1).then_inc(shaped, 1)
            nc.gpsimd.affine_select(out=tri, in_=tri, pattern=[[1, P]], compare_op=ALU.is_ge, fill=0.0,
                                    base=0, channel_multiplier=-1).then_inc(shaped, 1)
            nc.gpsimd.affine_select(out=before, in_=before, pattern=[[-1, P]], compare_op=ALU.is_gt, fill=0.0,
                                    base=0, channel_multiplier=1).then_inc(shaped, 1)


def layer(nc, a, out, scratch):
    proj, y, kv, h = (scratch[n] for n in ("proj", "y", "kv", "h"))
    with ExitStack() as ctx:
        def sb(c, n, shape, dt=F32):
            return c.enter_context(nc.sbuf_tensor(n, shape, dt))

        consts = {n: sb(ctx, n, [P, P]) for n in ("ident", "tri", "before", "ones")}
        consts |= {n: sb(ctx, n, [P, 1]) for n in ("one", "eps")}
        set_constants(nc, consts)
        dt, da = sb(ctx, "dt", [P, TB, SSD_HEADS]), sb(ctx, "da", [P, TB, SSD_HEADS])
        with ExitStack() as c:
            xh, xl = sb(c, "memh", [P, KB, M], F32R), sb(c, "meml", [P, KB, M], F32R)
            norm_to_feature_major(nc, "nm", a["mem"], M, a["norm_mem"], xh, xl, consts)
            memory_keys_values(nc, a["w_mem_kv"], kv, xh, xl, consts)
        with ExitStack() as c:
            xh, xl = sb(c, "uh", [P, KB, S], F32R), sb(c, "ul", [P, KB, S], F32R)
            norm_to_feature_major(nc, "nu", a["x"], S, a["norm_mix_pre"], xh, xl, consts)
            input_projection(nc, a["w_in"], a["w_dt"], proj,
                             a["dt_bias"].broadcast_to([P, 32]), a["a_log"].broadcast_to([P, 32]), dt, da, xh, xl, consts)
            stick_breaking(nc, a["w_in"], a["conv_w"], a["conv_b"], proj, y, xh, xl, consts)
            project_gates(nc, a["w_in"], proj, xh, xl, consts)
        ssd(nc, proj, y, dt, da, a["d_skip"], a["ssd_norm"], consts)
        memory_attention(nc, proj, kv, y, consts)
        with ExitStack() as c:
            merged = sb(c, "merged", [P, KB, S])
            merge_branches(nc, a["w_branch"], proj, y, merged, consts)
            xh, xl = sb(c, "mh", [P, KB, S], F32R), sb(c, "ml", [P, KB, S], F32R)
            split_blocks(nc, "ms", merged, xh, xl)
            output_projection(nc, a["w_o"], xh, xl, merged, consts)
            add_normed(nc, "h1", merged, a["norm_mix_post"].broadcast_to([P, D]), a["x"], h, consts)
        with ExitStack() as c:
            xh, xl = sb(c, "vh", [P, KB, S], F32R), sb(c, "vl", [P, KB, S], F32R)
            norm_to_feature_major(nc, "nh", h, S, a["norm_mlp_pre"], xh, xl, consts)
            ff = sb(c, "ff", [P, KB, S])
            mlp(nc, a["w_up"], a["w_down"], xh, xl, ff, consts)
            add_normed(nc, "h2", ff, a["norm_mlp_post"].broadcast_to([P, D]), h, out, consts)


def lay_out(inputs):
    import numpy as np
    x = {k: np.asarray(v) for k, v in inputs.items()}
    n_qkv_z_xbc, n_dt = Q0 * P + MQ0 * P, SSD_HEADS
    w_in = x["w_in"][0]

    def tiles(w):
        r, c = w.shape[0] // D, w.shape[1] // P
        return np.ascontiguousarray(w.reshape(r, KB, P, c, P).transpose(0, 3, 2, 1, 4).reshape(r * c, P, D))

    def columns(v):
        return np.ascontiguousarray(v.reshape(-1, P).T)

    return {
        "x": x["x"][0], "mem": x["mem"][0],
        "w_in": tiles(np.concatenate([w_in[:, :n_qkv_z_xbc], w_in[:, n_qkv_z_xbc + n_dt:]], axis=1)),
        "w_dt": np.ascontiguousarray(w_in[:, n_qkv_z_xbc:n_qkv_z_xbc + n_dt].reshape(KB, P, n_dt).transpose(1, 0, 2)),
        "conv_w": np.ascontiguousarray(x["conv_w"][0].reshape(CONV, -1, P).transpose(2, 1, 0)),
        "conv_b": columns(x["conv_b"][0]),
        "dt_bias": x["dt_bias"], "a_log": x["a_log"],
        "d_skip": np.ascontiguousarray(np.repeat(x["d_skip"][0], 64).reshape(-1, P).T),
        "ssd_norm": columns(x["ssd_norm"][0]),
        "norm_mix_pre": columns(x["norm_mix_pre"][0]), "norm_mem": columns(x["norm_mem"][0]),
        "norm_mlp_pre": columns(x["norm_mlp_pre"][0]),
        "norm_mix_post": x["norm_mix_post"], "norm_mlp_post": x["norm_mlp_post"],
        "w_mem_kv": tiles(x["w_mem_kv"][0]),
        "w_branch": tiles(np.concatenate([x["w_sb_out"][0], x["w_ssd_out"][0], x["w_mem_out"][0]], axis=0)),
        "w_o": tiles(x["w_o"][0]), "w_up": tiles(x["w_up"][0]), "w_down": tiles(x["w_down"][0]),
    }


def kernel(**inputs):
    import numpy as np
    import concourse.bacc as bacc
    from concourse.bass_utils import run_bass_kernel_spmd

    nc = bacc.Bacc("TRN2", target_bir_lowering=False, num_devices=1)
    arrays = {f"in_{k}": v for k, v in lay_out(inputs).items()}
    a = {k[3:]: nc.dram_tensor(k, v.shape, mybir.dt.from_np(v.dtype), kind="ExternalInput").ap()
         for k, v in arrays.items()}
    out = nc.dram_tensor("out", (S, D), F32, kind="ExternalOutput").ap()
    scratch = {n: nc.dram_tensor(f"scratch_{n}", shape, F32, kind=KIND).ap()
               for n, shape in (("proj", (N_IN, P, S)), ("y", (N_Y, P, S)), ("kv", (2 * KB, P, M)), ("h", (S, D)))}
    layer(nc, a, out, scratch)
    r = run_bass_kernel_spmd(nc, [arrays], core_ids=[0])
    return r.results[0]["out"].reshape(1, S, D)


KIND = "Internal"
```

```python
from contextlib import ExitStack, contextmanager

import concourse.bass as bass
from concourse import mybir

F32 = mybir.dt.float32
F32R = mybir.dt.float32r
ALU = mybir.AluOpType
ACT = mybir.ActivationFunctionType
AX_X = mybir.AxisListType.X

P = 128
D = 1024
KB = D // P
S = 1024
TB = S // P
HALF = 512
M = 256
MB = M // P
EPS = 1e-6

SB_PAIRS = 8
SSD_HEADS, GROUPS, HPG = 32, 4, 8
GB = 4
MEM_HEADS = 4
MEM_SCALE = 256.0 ** -0.5
CONV = 4

Q0, K0, V0, Z0, X0, B0, C0, MQ0, G0, N_IN = 0, 8, 16, 24, 40, 56, 60, 64, 72, 96
Y_SB, Y_SSD, Y_MEM, N_Y = 0, 8, 24, 32
FF_CHUNKS = 4


@contextmanager
def stage(nc):
    with nc.cleanup_on_exit(), ExitStack() as ctx:
        yield ctx


def split3(hi, lo):
    (ah, bh), (al, bl) = hi, lo
    return ((ah, bh), (ah, bl), (al, bh))


def norm_to_feature_major(nc, name, src, tokens, gain, xh, xl, consts):
    n_pairs = tokens // P // 2
    with stage(nc) as ctx:
        def sb(n, shape, dt=F32):
            return ctx.enter_context(nc.sbuf_tensor(f"{name}_{n}", shape, dt))

        def sem(n):
            return nc.alloc_semaphore(f"{name}_{n}")

        x_tile, u, square = sb("x", [P, 2, D]), sb("u", [P, 2, D]), sb("sq", [P, D])
        scaled = sb("scaled", [P, 2, D])
        sums, root, rstd = sb("sums", [P, 2]), sb("root", [P, 2]), sb("rstd", [P, 2])
        gains = sb("gain", [P, KB])
        turned = ctx.enter_context(nc.psum_tensor(f"{name}_ps", [P, 2, D], F32))
        gain_loaded = sem("gain_loaded")
        loaded = [sem(f"loaded{s}") for s in range(2)]
        summed, rooted, inverted = sem("summed"), sem("rooted"), sem("inverted")
        normed = [sem(f"normed{s}") for s in range(2)]
        turned_done = [sem(f"turned{s}") for s in range(2)]
        gained = [sem(f"gained{s}") for s in range(2)]
        hi_done = [sem(f"hi{s}") for s in range(2)]
        lo_done = [sem(f"lo{s}") for s in range(2)]

        block = ctx.enter_context(nc.Block())

        @block.sync
        def _(sp):
            sp.dma_start(gains[:], gain).then_inc(gain_loaded, 16)
            with sp.Fori(0, n_pairs) as i:
                for s in range(2):
                    sp.wait_ge(normed[s], i)
                    sp.dma_start(x_tile[:, s], src[bass.ds(i * 256 + s * P, P), :]).then_inc(loaded[s], 16)

        @block.scalar
        def _(act):
            with act.Fori(0, n_pairs) as i:
                for s in range(2):
                    act.wait_ge(loaded[s], i * 16 + 16)
                    nc.scalar.activation(square[:], x_tile[:, s], ACT.Square,
                                         accum_out=sums[:, s:s + 1]).then_inc(summed, 1)
                    act.wait_ge(summed, i * 2 + s + 1)
                    act.wait_ge(normed[s], i)
                    nc.scalar.activation(root[:, s:s + 1], sums[:, s:s + 1], ACT.Sqrt, scale=1.0 / D,
                                         bias=consts["eps"][:]).then_inc(rooted, 1)
                for s in range(2):
                    act.wait_ge(gained[s], i + 1)
                    act.wait_ge(lo_done[s], i)
                    nc.scalar.activation(xh[:, :, bass.ds(i * 256 + s * P, P)],
                                         scaled[:, s].rearrange("p (k t) -> p k t", k=KB),
                                         ACT.Copy).then_inc(hi_done[s], 1)

        @block.vector
        def _(dve):
            dve.wait_ge(gain_loaded, 16)
            with dve.Fori(0, n_pairs) as i:
                for s in range(2):
                    dve.wait_ge(rooted, i * 2 + s + 1)
                    nc.vector.reciprocal(rstd[:, s:s + 1], root[:, s:s + 1]).then_inc(inverted, 1)
                    dve.wait_ge(inverted, i * 2 + s + 1)
                    dve.wait_ge(turned_done[s], i)
                    nc.vector.tensor_scalar(u[:, s], x_tile[:, s], rstd[:, s:s + 1], None,
                                            ALU.mult).then_inc(normed[s], 1)
                for s in range(2):
                    dve.wait_ge(turned_done[s], i + 1)
                    dve.wait_ge(lo_done[s], i)
                    nc.vector.tensor_tensor(
                        scaled[:, s].rearrange("p (k t) -> p k t", k=KB),
                        turned[:, s].rearrange("p (k t) -> p k t", k=KB),
                        gains[:, :, None].broadcast_to([P, KB, P]), ALU.mult).then_inc(gained[s], 1)
                for s in range(2):
                    dve.wait_ge(hi_done[s], i + 1)
                    dve.wait_ge(gained[s], i + 1)
                    hi = xh[:, :, bass.ds(i * 256 + s * P, P)].bitcast(F32)
                    nc.vector.tensor_tensor(xl[:, :, bass.ds(i * 256 + s * P, P)],
                                            scaled[:, s].rearrange("p (k t) -> p k t", k=KB), hi,
                                            ALU.subtract).then_inc(lo_done[s], 1)

        @block.tensor
        def _(pe):
            with pe.Fori(0, n_pairs) as i:
                for s in range(2):
                    pe.wait_ge(normed[s], i + 1)
                    pe.wait_ge(gained[s], i)
                    for k in range(KB):
                        last = nc.tensor.transpose(turned[:, s, k * P:(k + 1) * P], u[:, s, k * P:(k + 1) * P],
                                                   consts["ident"][:])
                    last.then_inc(turned_done[s], 1)


class Ring:

    def __init__(self, nc, ctx, name, consts):
        self.ones = consts["one"]
        self.raw = ctx.enter_context(nc.sbuf_tensor(f"{name}_w", [P, 2, D], F32))
        self.hi = ctx.enter_context(nc.sbuf_tensor(f"{name}_wh", [P, 2, KB, P], F32R))
        self.lo = ctx.enter_context(nc.sbuf_tensor(f"{name}_wl", [P, 2, KB, P], F32R))
        s = [nc.alloc_semaphore(f"{name}_{n}{i}") for n in ("loaded", "hi", "split", "used")
             for i in range(2)]
        self.loaded, self.hi_done, self.split, self.used = s[0:2], s[2:4], s[4:6], s[6:8]


def load_weights(sp, ring, w, i, s, row):
    sp.wait_ge(ring.split[s], i)
    sp.dma_start(ring.raw[:, s], w[bass.ds(row, 1)].rearrange("a p n -> (a p) n")).then_inc(ring.loaded[s], 16)


def round_weights(nc, pool, ring, i, s):
    pool.wait_ge(ring.loaded[s], i * 16 + 16)
    pool.wait_ge(ring.used[s], i)
    nc.gpsimd.tensor_tensor(ring.hi[:, s].rearrange("p k n -> p (k n)"), ring.raw[:, s],
                            ring.ones[:].broadcast_to([P, D]), ALU.mult).then_inc(ring.hi_done[s], 1)


def rest_of_weights(nc, pool, ring, i, s):
    flat = "p k n -> p (k n)"
    pool.wait_ge(ring.hi_done[s], i + 1)
    nc.gpsimd.tensor_tensor(ring.lo[:, s].rearrange(flat), ring.raw[:, s],
                            ring.hi[:, s].rearrange(flat).bitcast(F32), ALU.subtract).then_inc(ring.split[s], 1)


def split_weights(nc, pool, ring, i, s):
    round_weights(nc, pool, ring, i, s)
    rest_of_weights(nc, pool, ring, i, s)


def product(nc, ring, s, xh, xl, out, tokens):
    n = min(tokens, HALF)
    for h in range(tokens // n):
        for k in range(KB):
            for j, (w, x) in enumerate(split3((ring.hi, xh), (ring.lo, xl))):
                last = nc.tensor.matmul(out[:, h * n:(h + 1) * n], w[:, s, k], x[:, k, h * n:(h + 1) * n],
                                        start=(k == 0 and j == 0), stop=(k == KB - 1 and j == 2))
    return last


def input_projection(nc, w_in, w_dt, proj, dt_bias, a_log, dt_out, da_out, xh, xl, consts):
    with stage(nc) as ctx:
        def sb(n, shape, dt=F32):
            return ctx.enter_context(nc.sbuf_tensor(f"in_{n}", shape, dt))

        def sem(n):
            return nc.alloc_semaphore(f"in_{n}")

        ring = Ring(nc, ctx, "in", consts)
        out_tile = sb("out", [P, 2, S])
        wd, wdh, wdl = sb("wd", [P, KB, 32]), sb("wdh", [P, KB, 32], F32R), sb("wdl", [P, KB, 32], F32R)
        bias_row, a_row = sb("bias", [P, 32]), sb("a", [P, 32])
        raw, capped, soft = (sb(n, [P, TB, 32]) for n in ("dtraw", "dtcap", "dtsoft"))
        ps = ctx.enter_context(nc.psum_tensor("in_ps", [P, 2, S], F32))
        ps_dt = ctx.enter_context(nc.psum_tensor("in_psdt", [P, TB, 32], F32))
        ps_dtT = ctx.enter_context(nc.psum_tensor("in_psdtT", [32, S], F32))
        dtT = sb("dtT", [32, S])
        dtT_done, dtT_out = sem("dtTdone"), sem("dtTout")
        small_loaded, wd_hi, wd_split, dt_done = sem("small"), sem("wdhi"), sem("wdsplit"), sem("dtdone")
        dt_dve, dt_act = sem("dtdve"), sem("dtact")
        evacuated = [sem(f"evac{s}") for s in range(2)]
        stored = [sem(f"stored{s}") for s in range(2)]
        N_QKV = Z0

        block = ctx.enter_context(nc.Block())

        @block.sync
        def _(sp):
            for dst, src in ((wd, w_dt), (bias_row, dt_bias), (a_row, a_log)):
                sp.dma_start(dst[:], src).then_inc(small_loaded, 16)
            for s in range(2):
                load_weights(sp, ring, w_in, 0, s, s)
            with sp.Fori(0, N_QKV // 2 - 1) as i:
                for s in range(2):
                    load_weights(sp, ring, w_in, i + 1, s, i * 2 + s + 2)
                    sp.wait_ge(evacuated[s], i + 1)
                    sp.dma_start(proj[bass.ds(i * 2 + s, 1)].rearrange("a p n -> (a p) n"),
                                 out_tile[:, s]).then_inc(stored[s], 16)
            for s in range(2):
                sp.wait_ge(evacuated[s], N_QKV // 2)
                sp.dma_start(proj[N_QKV - 2 + s], out_tile[:, s]).then_inc(stored[s], 16)
            for s in range(2):
                sp.wait_ge(stored[s], 16 * N_QKV // 2)

        @block.gpsimd
        def _(pool):
            pool.wait_ge(small_loaded, 48)
            nc.gpsimd.tensor_copy(wdh[:], wd[:]).then_inc(wd_hi, 1)
            pool.wait_ge(wd_hi, 1)
            nc.gpsimd.tensor_tensor(wdl[:], wd[:], wdh[:].bitcast(F32), ALU.subtract).then_inc(wd_split, 1)
            with pool.Fori(0, N_QKV // 2) as i:
                for s in range(2):
                    split_weights(nc, pool, ring, i, s)

        @block.tensor
        def _(pe):
            pe.wait_ge(wd_split, 1)
            for h in range(2):
                for k in range(KB):
                    for j, (w, x) in enumerate(split3((wdh, xh), (wdl, xl))):
                        last = nc.tensor.matmul(ps_dtT[:, h * HALF:(h + 1) * HALF], w[:, k], x[:, k, h * HALF:(h + 1) * HALF],
                                                start=(k == 0 and j == 0), stop=(k == KB - 1 and j == 2))
            last.then_inc(dtT_done, 1)
            pe.wait_ge(dtT_out, 1)
            for t in range(TB):
                last = nc.tensor.transpose(ps_dt[:, t], dtT[:, t * P:(t + 1) * P], consts["ident"][0:32, 0:32])
            last.then_inc(dt_done, 1)
            with pe.Fori(0, N_QKV // 2) as i:
                for s in range(2):
                    pe.wait_ge(ring.split[s], i + 1)
                    pe.wait_ge(evacuated[s], i)
                    product(nc, ring, s, xh, xl, ps[:, s], S).then_inc(ring.used[s], 1)

        @block.scalar
        def _(act):
            act.wait_ge(dt_dve, 2)
            nc.scalar.activation(soft[:], capped[:], ACT.Exp).then_inc(dt_act, 1)
            act.wait_ge(dt_act, 1)
            nc.scalar.activation(soft[:], soft[:], ACT.Ln, bias=consts["one"][:]).then_inc(dt_act, 1)
            nc.scalar.activation(a_row[:], a_row[:], ACT.Exp).then_inc(dt_act, 1)
            with act.Fori(0, N_QKV // 2) as i:
                for s in range(2):
                    act.wait_ge(ring.used[s], i + 1)
                    act.wait_ge(stored[s], i * 16)
                    nc.scalar.activation(out_tile[:, s], ps[:, s], ACT.Copy).then_inc(evacuated[s], 1)

        @block.vector
        def _(dve):
            dve.wait_ge(dtT_done, 1)
            nc.vector.tensor_copy(dtT[:], ps_dtT[:]).then_inc(dtT_out, 1)
            dve.wait_ge(small_loaded, 48)
            dve.wait_ge(dt_done, 1)
            nc.vector.tensor_tensor(raw[:], ps_dt[:], bias_row[:, None, :].broadcast_to([P, TB, 32]),
                                    ALU.add).then_inc(dt_dve, 1)
            dve.wait_ge(dt_dve, 1)
            nc.vector.tensor_scalar(capped[:], raw[:], 40.0, None, ALU.min).then_inc(dt_dve, 1)
            dve.wait_ge(dt_act, 3)
            nc.vector.tensor_tensor(dt_out[:], soft[:], raw[:], ALU.max).then_inc(dt_dve, 1)
            nc.vector.tensor_scalar(a_row[:], a_row[:], -1.0, None, ALU.mult).then_inc(dt_dve, 1)
            dve.wait_ge(dt_dve, 4)
            nc.vector.tensor_tensor(da_out[:], dt_out[:], a_row[:, None, :].broadcast_to([P, TB, 32]),
                                    ALU.mult).then_inc(dt_dve, 1)


def stick_breaking(nc, w_in, conv_w, conv_b, proj, y, uh, ul, consts):
    with stage(nc) as ctx:
        def sb(n, shape, dt=F32):
            return ctx.enter_context(nc.sbuf_tensor(f"sb_{n}", shape, dt))

        def sem(n):
            return nc.alloc_semaphore(f"sb_{n}")

        qkv = sb("qkv", [P, 3, S])
        qkh, qkl = sb("qkh", [P, 2, S], F32R), sb("qkl", [P, 2, S], F32R)
        vh, vl = sb("vh", [P, TB, P], F32R), sb("vl", [P, TB, P], F32R)
        beta, keep = sb("beta", [P, 2, S]), sb("keep", [P, S])
        rest = sb("rest", [P, 2, S + 1])
        wth, wtl = sb("wth", [P, TB, HALF], F32R), sb("wtl", [P, TB, HALF], F32R)
        y_tile = sb("y", [P, S])
        ps_z = ctx.enter_context(nc.psum_tensor("sb_psz", [P, S], F32))
        ps_t = ctx.enter_context(nc.psum_tensor("sb_pst", [P, 2, HALF], F32))
        ps_y = ctx.enter_context(nc.psum_tensor("sb_psy", [P, HALF], F32))

        loaded, v_loaded, qk_hi, qk_split = (sem(n) for n in ("ld", "vld", "qkhi", "qksplit"))
        ones_set = sem("ones")
        scores, beta_done, masked, keep_done, scanned, weighted = (
            sem(n) for n in ("scores", "beta", "masked", "keep", "scanned", "weighted"))
        turned, hi_done, lo_done = sem("turned"), sem("hi"), sem("lo")
        y_done, y_out, stored = sem("ydone"), sem("yout"), sem("stored")

        ring = Ring(nc, ctx, "sb", consts)
        kinds = "xzxzxq"
        PER = len(kinds)
        n_conv = MQ0 - X0
        out_tile = sb("out", [P, 2, S])
        padded = sb("padded", [P, CONV - 1 + S])
        sigm = sb("sigm", [P, 2, S])
        cw, cb = sb("cw", [P, n_conv, CONV]), sb("cb", [P, n_conv])
        ps_g = ctx.enter_context(nc.psum_tensor("sb_psg", [P, 2, HALF], F32))
        small_loaded, zeroed = sem("small"), sem("zeroed")
        half_done, half_out = sem("halfdone"), [sem(f"halfout{h}") for h in range(2)]
        conv_step, sigm_done = sem("convstep"), sem("sigm")
        silu_done = [sem(f"silu{s}") for s in range(2)]
        g_stored = [sem(f"gstored{s}") for s in range(2)]

        steps = [(a, t) for a in range(2) for t in range(TB)]
        N = len(steps)
        units = [("v", 0, 4 * u, 4) for u in range(2)]
        for n, (a, t) in enumerate(steps):
            units += [("w", n, j, min(4, t + 1 - j)) for j in range(0, t + 1, 4)]
        U = len(units)
        LAG = 2
        EVENTS = N + LAG
        PASSES = KB * 3
        PER_EVENT = PER * 2 * PASSES // (EVENTS - 2)

        def event_of(m, h):
            return 2 + (m * 2 * PASSES + h * PASSES + PASSES - 1) // PER_EVENT

        def units_of(n):
            return [u for u, x in enumerate(units) if x[:2] == ("w", n)]

        def turned_by(n):
            return units_of(n)[-1] + 1

        def row_of(p, m):
            return {"x": p * 3 + X0 + m // 2, "z": p * 2 + Z0 + m // 2, "q": p + MQ0}[kinds[m]]

        block = ctx.enter_context(nc.Block())

        @block.sync
        def _(sp):
            def load_qk(p):
                for n, b in enumerate((Q0, K0)):
                    sp.dma_start(qkv[:, n], proj[bass.ds(p + b, 1)].rearrange("a p n -> (a p) n")).then_inc(loaded, 16)

            def load_v(p):
                sp.dma_start(qkv[:, 2], proj[bass.ds(p + V0, 1)].rearrange("a p n -> (a p) n")).then_inc(v_loaded, 16)

            load_qk(0)
            load_v(0)
            load_weights(sp, ring, w_in, 0, 0, row_of(0, 0))
            for dst, src in ((cw, conv_w), (cb, conv_b)):
                sp.dma_start(dst[:], src).then_inc(small_loaded, 16)
            with sp.Fori(0, SB_PAIRS) as p:
                after = p + 1

                def load(m):
                    load_weights(sp, ring, w_in, p * 3 + m // 2, m % 2, row_of(p, m))

                def store(m):
                    if kinds[m] == "q":
                        sp.wait_ge(half_out[1], p * PER + m + 1)
                    else:
                        sp.wait_ge(silu_done[m % 2], p * (3 if kinds[m] == "x" else 2) + m // 2 + 1)
                    sp.dma_start(proj[bass.ds(row_of(p, m), 1)].rearrange("a p n -> (a p) n"),
                                 out_tile[:, m % 2]).then_inc(g_stored[m % 2], 16)

                load(1)
                sp.wait_ge(qk_split, p * 2 + 2)
                load_qk(after)
                sp.wait_ge(turned, p * U + 2)
                load_v(after)
                load(2)
                load(3)
                load(4)
                store(0)
                store(1)
                load(5)
                store(2)
                load_weights(sp, ring, w_in, p * 3 + 3, 0, row_of(after, 0))
                store(3)
                store(4)
                store(5)
                sp.wait_ge(y_out, p * 4 + 4)
                sp.dma_start(y[bass.ds(p + Y_SB, 1)].rearrange("a p n -> (a p) n"), y_tile[:]).then_inc(stored, 16)
            sp.wait_ge(stored, 16 * SB_PAIRS)
            for s in range(2):
                sp.wait_ge(g_stored[s], 16 * 3 * SB_PAIRS)
            sp.wait_ge(loaded, 32 * (SB_PAIRS + 1))
            sp.wait_ge(v_loaded, 16 * (SB_PAIRS + 1))
            sp.wait_ge(ring.loaded[0], 16 * (3 * SB_PAIRS + 1))

        @block.tensor
        def _(pe):
            with pe.Fori(0, SB_PAIRS) as p:
                def turn(u):
                    kind, n, j0, cnt = units[u]
                    if u >= 2:
                        pe.wait_ge(lo_done, p * U + u - 1)
                    for j in range(j0, j0 + cnt):
                        src = qkv[:, 2, j * P:(j + 1) * P] if kind == "v" else beta[:, n % 2, j * P:(j + 1) * P]
                        last = nc.tensor.transpose(ps_t[:, u % 2, (j - j0) * P:(j - j0 + 1) * P], src,
                                                   consts["ident"][:])
                    last.then_inc(turned, 1)

                def project(first, end):
                    for x in range(first, end):
                        m, h, k, j = x // (2 * PASSES), x // PASSES % 2, x % PASSES // 3, x % 3
                        s = m % 2
                        if k == 0 and j == 0:
                            if h == 0:
                                pe.wait_ge(ring.split[s], p * 3 + m // 2 + 1)
                            pe.wait_ge(half_out[h], p * PER + m)
                        l, r = split3((ring.hi, uh), (ring.lo, ul))[j]
                        last = nc.tensor.matmul(ps_g[:, h], l[:, s, k], r[:, k, h * HALF:(h + 1) * HALF],
                                                start=(k == 0 and j == 0), stop=(k == KB - 1 and j == 2))
                        if k == KB - 1 and j == 2:
                            last.then_inc(ring.used[s] if h else half_done, 1)

                pe.wait_ge(v_loaded, p * 16 + 16)
                turn(0)
                turn(1)
                for i in range(EVENTS):
                    if i < N:
                        a, t = steps[i]
                        rows = slice(64 * a, 64 * a + 64)
                        if i == 0:
                            pe.wait_ge(qk_split, p * 2 + 2)
                        pe.wait_ge(beta_done, p * N + i)
                        cols = (t + 1) * P
                        for c in range(0, cols, HALF):
                            e = min(cols, c + HALF)
                            for j, (l, r) in enumerate(split3((qkh, qkh), (qkl, qkl))):
                                last = nc.tensor.matmul(ps_z[:, c:e], l[rows, 0, t * P:(t + 1) * P],
                                                        r[rows, 1, c:e], start=(j == 0), stop=(j == 2))
                        last.then_inc(scores, 1)
                    n = i - LAG
                    if n >= 0:
                        a, t = steps[n]
                        pe.wait_ge(weighted, p * N + n + 1)
                        for u in units_of(n):
                            turn(u)
                    if i >= 2:
                        project((i - 2) * PER_EVENT, (i - 1) * PER_EVENT)
                    if n >= 0 and t % 4 == 3:
                        pe.wait_ge(lo_done, p * U + turned_by(n))
                        pe.wait_ge(y_out, p * 4 + n // 4)
                        for j in range(t + 1):
                            lo_col = max(0, j - (t - 3)) * P
                            for m, (l, r) in enumerate(split3((vh, wth), (vl, wtl))):
                                last = nc.tensor.matmul(ps_y[:, lo_col:], l[:, j], r[:, j, lo_col:],
                                                        start=(j == 0 and m == 0), stop=(j == t and m == 2))
                        last.then_inc(y_done, 1)

        def moved(u, dst, v_dst):
            kind, n, j0, cnt = units[u]
            ps = ps_t[:, u % 2, 0:cnt * P].rearrange("p (j t) -> p j t", j=cnt)
            if kind == "v":
                return v_dst[:, j0:j0 + cnt], ps
            t = steps[n][1]
            return dst[:, j0:j0 + cnt, (t % 4) * P:(t % 4 + 1) * P], ps

        @block.scalar
        def _(act):
            act.wait_ge(zeroed, 1)
            with act.Fori(0, SB_PAIRS) as p:
                def hi(u):
                    kind, n, j0, _ = units[u]
                    act.wait_ge(turned, p * U + u + 1)
                    if u == 0:
                        act.wait_ge(y_done, p * 4)
                    if kind == "w" and n % 4 == 0 and j0 == 0:
                        act.wait_ge(y_done, p * 4 + n // 4)
                    out, src = moved(u, wth, vh)
                    nc.scalar.activation(out, src, ACT.Copy).then_inc(hi_done, 1)

                def evacuate(m, h):
                    s, cols = m % 2, slice(h * HALF, (h + 1) * HALF)
                    if h:
                        act.wait_ge(ring.used[s], p * 3 + m // 2 + 1)
                    else:
                        act.wait_ge(half_done, p * PER + m + 1)
                        if kinds[m] != "x":
                            act.wait_ge(g_stored[s], (p * 3 + m // 2) * 16)
                        if kinds[m] == "x":
                            act.wait_ge(conv_step, (p * 3 + m // 2) * CONV)
                        if kinds[m] == "z":
                            act.wait_ge(silu_done[1], p * 2 + m // 2)
                    if kinds[m] == "x":
                        nc.scalar.activation(padded[:, CONV - 1 + h * HALF:CONV - 1 + (h + 1) * HALF], ps_g[:, h],
                                             ACT.Copy).then_inc(half_out[h], 1)
                    elif kinds[m] == "q":
                        nc.scalar.activation(out_tile[:, s, cols], ps_g[:, h], ACT.Copy).then_inc(half_out[h], 1)
                    else:
                        nc.scalar.activation(out_tile[:, s, cols], ps_g[:, h], ACT.Copy)
                        nc.scalar.activation(sigm[:, 1, cols], ps_g[:, h], ACT.Sigmoid).then_inc(half_out[h], 1)

                def sigmoid_of_conv(m):
                    act.wait_ge(conv_step, (p * 3 + m // 2 + 1) * CONV)
                    act.wait_ge(silu_done[0], p * 3 + m // 2)
                    nc.scalar.activation(sigm[:, 0], out_tile[:, 0], ACT.Sigmoid).then_inc(sigm_done, 1)

                hi(0)
                hi(1)
                for i in range(EVENTS):
                    if i < N:
                        t = steps[i][1]
                        act.wait_ge(scores, p * N + i + 1)
                        act.wait_ge(turned, p * U + (turned_by(i - 2) if i >= 2 else 0))
                        nc.scalar.activation(beta[:, i % 2, 0:(t + 1) * P], ps_z[:, 0:(t + 1) * P],
                                             ACT.Sigmoid, scale=0.125).then_inc(beta_done, 1)
                    n = i - LAG
                    if n >= 0:
                        for u in units_of(n):
                            hi(u)
                    for m in (0, 2, 4):
                        if i == min(event_of(m, 1) + 3, EVENTS - 1):
                            sigmoid_of_conv(m)
                    for m in range(PER):
                        for h in range(2):
                            if event_of(m, h) == i:
                                evacuate(m, h)
                    if n >= 0 and n % 4 == 3:
                        g = n // 4
                        rows = slice(64 * (g // 2), 64 * (g // 2) + 64)
                        act.wait_ge(y_done, p * 4 + g + 1)
                        if g == 0:
                            act.wait_ge(stored, p * 16)
                        nc.scalar.activation(y_tile[rows, (g % 2) * HALF:(g % 2 + 1) * HALF], ps_y[rows, :],
                                             ACT.Copy).then_inc(y_out, 1)

        @block.gpsimd
        def _(pool):
            with pool.Fori(0, SB_PAIRS) as p:
                def weigh(n):
                    cols = (steps[n][1] + 1) * P
                    pool.wait_ge(scanned, p * N + n + 1)
                    nc.gpsimd.tensor_tensor(beta[:, n % 2, 0:cols], beta[:, n % 2, 0:cols],
                                            rest[:, n % 2, S - cols + 1:S + 1], ALU.mult).then_inc(weighted, 1)

                for i in range(N + 1):
                    if i < N:
                        t = steps[i][1]
                        diag = beta[:, i % 2, t * P:(t + 1) * P]
                        pool.wait_ge(beta_done, p * N + i + 1)
                        nc.gpsimd.tensor_tensor(diag, diag, consts["before"][:], ALU.mult).then_inc(masked, 1)
                    if i:
                        weigh(i - 1)
                    for m in range(PER):
                        at = 2 + m * 2 * PASSES // PER_EVENT
                        if i == max(0, at - 2):
                            round_weights(nc, pool, ring, p * 3 + m // 2, m % 2)
                        if i == max(0, at - 2) + 1:
                            rest_of_weights(nc, pool, ring, p * 3 + m // 2, m % 2)

        @block.vector
        def _(dve):
            def split_qk(p, n_pairs):
                dve.wait_ge(loaded, n_pairs * 32)
                for n in range(2):
                    nc.vector.tensor_copy(qkh[:, n], qkv[:, n]).then_inc(qk_hi, 1)
                for n in range(2):
                    dve.wait_ge(qk_hi, n_pairs * 2 - 1 + n)
                    nc.vector.tensor_tensor(qkl[:, n], qkv[:, n], qkh[:, n].bitcast(F32),
                                            ALU.subtract).then_inc(qk_split, 1)

            nc.vector.memset(rest[:, :, S:S + 1], 1.0).then_inc(ones_set, 1)
            nc.vector.memset(padded[:, 0:CONV - 1], 0.0).then_inc(zeroed, 1)
            dve.wait_ge(ones_set, 1)
            dve.wait_ge(small_loaded, 32)
            split_qk(None, 1)
            with dve.Fori(0, SB_PAIRS) as p:
                def lo(u):
                    dve.wait_ge(hi_done, p * U + u + 1)
                    out, src = moved(u, wtl, vl)
                    hi = moved(u, wth, vh)[0].bitcast(F32)
                    nc.vector.tensor_tensor(out, src, hi, ALU.subtract).then_inc(lo_done, 1)

                def convolve(m, taps):
                    n = p * 3 + m // 2
                    for tap in taps:
                        if tap == 0:
                            dve.wait_ge(half_out[1], p * PER + m + 1)
                            dve.wait_ge(g_stored[0], n * 16)
                            nc.vector.tensor_scalar(out_tile[:, 0], padded[:, 0:S], cw[:, bass.ds(n, 1), 0],
                                                    cb[:, bass.ds(n, 1)], ALU.mult, ALU.add).then_inc(conv_step, 1)
                        else:
                            dve.wait_ge(conv_step, n * CONV + tap)
                            nc.vector.scalar_tensor_tensor(
                                out_tile[:, 0], padded[:, tap:tap + S], cw[:, bass.ds(n, 1), tap],
                                out_tile[:, 0], ALU.mult, ALU.add).then_inc(conv_step, 1)

                def silu(m):
                    s = m % 2
                    if kinds[m] == "x":
                        dve.wait_ge(sigm_done, p * 3 + m // 2 + 1)
                    else:
                        dve.wait_ge(half_out[1], p * PER + m + 1)
                    nc.vector.tensor_tensor(out_tile[:, s], out_tile[:, s], sigm[:, s], ALU.mult).then_inc(silu_done[s], 1)

                lo(0)
                lo(1)
                for i in range(EVENTS):
                    if i < N:
                        t = steps[i][1]
                        cols = (t + 1) * P
                        dve.wait_ge(masked, p * N + i + 1)
                        dve.wait_ge(scanned, p * N + i)
                        nc.vector.tensor_scalar(keep[:, 0:cols], beta[:, i % 2, 0:cols], -1.0, 1.0,
                                                ALU.mult, ALU.add).then_inc(keep_done, 1)
                        dve.wait_ge(keep_done, p * N + i + 1)
                        dve.wait_ge(weighted, p * N + (i - 1 if i >= 2 else 0))
                        down = keep[:, 0:cols][:, ::-1]
                        nc.vector.tensor_tensor_scan(rest[:, i % 2, S - cols:S][:, ::-1], down, down, 1.0,
                                                     ALU.mult, ALU.bypass).then_inc(scanned, 1)
                    n = i - LAG
                    if n >= 0:
                        for u in units_of(n):
                            lo(u)
                    for m in range(PER):
                        end = event_of(m, 1)
                        if kinds[m] == "x" and i == end + 1:
                            convolve(m, range(2) if end + 2 < EVENTS else range(CONV))
                        if kinds[m] == "x" and i == end + 2:
                            convolve(m, range(2, CONV))
                        if kinds[m] == "x" and i == min(end + 4, EVENTS - 1) or kinds[m] == "z" and i == end + 1:
                            silu(m)
                    if i == EVENTS - 1:
                        dve.wait_ge(scores, p * N + N)
                        split_qk(p, p + 2)


def ssd(nc, w_in, proj, y, dt, da, d_rows, uh, ul, consts):
    with stage(nc) as ctx:
        def sb(n, shape, dt_=F32):
            return ctx.enter_context(nc.sbuf_tensor(f"ssd_{n}", shape, dt_))

        def ps(n, shape):
            return ctx.enter_context(nc.psum_tensor(f"ssd_{n}", shape, F32))

        def sem(n):
            return nc.alloc_semaphore(f"ssd_{n}")

        R = HPG
        xT, yT, bcT = sb("xT", [P, 2, GB, P]), sb("yT", [P, 2, GB, P]), sb("bcT", [P, 2, 2, P])
        bch, bcl = sb("bch", [P, 2, P], F32R), sb("bcl", [P, 2, P], F32R)
        drow, d_group = sb("drow", [P, GROUPS * GB]), sb("dgroup", [P, GB])
        d_ready = sem("dready")
        a_cs, to_end = (sb(n, [P, TB, SSD_HEADS]) for n in ("acs", "toend"))
        bth, btl = sb("bth", [P, 2, P], F32R), sb("btl", [P, 2, P], F32R)
        xd = sb("xd", [P, R, 64])
        xe = sb("xe", [P, R, 64])
        xdh, xdl, xeh, xel = (sb(n, [P, 2, R * 64], F32R) for n in ("xdh", "xdl", "xeh", "xel"))
        cb = sb("cb", [P, P])
        tri_da = sb("trida", [P, R, P])
        w = sb("w", [P, R, P])
        grown = sb("grown", [P, R, P])
        ce = sb("ce", [P, R, P])
        wh, wl, ceh, cel = (sb(n, [P, 2, R, P], F32R) for n in ("wh", "wl", "ceh", "cel"))
        whole = sb("whole", [P, 2, R])
        state = sb("state", [P, R, 64])
        sth, stl = sb("sth", [P, R * 64], F32R), sb("stl", [P, R * 64], F32R)
        ps_bc, ps_x, ps_a = ps("psbc", [P, 2, P]), ps("psx", [P, R, 64]), ps("psa", [P, R, P])
        ps_y, ps_s, ps_g = ps("psy", [P, GB, 2, P]), ps("pss", [P, R, 64]), ps("psg", [P, HALF])
        ps_cs = ps_s[:].rearrange("p (a r) d -> p a (r d)", a=2)

        small_loaded, cs_done, cs_exp, cs_read, cs_diff = (sem(n) for n in ("small", "cs", "csexp", "csread", "csdiff"))
        chunk_loaded, stored = ([sem(f"{n}{s}") for s in range(2)] for n in ("loaded", "stored"))
        bc_hi, bc_split, skip_done = sem("bchi"), sem("bcsplit"), sem("skip")
        ring = Ring(nc, ctx, "sg", consts)
        out_tile = sb("out", [P, 2, S])
        half_done, half_out = sem("halfdone"), sem("halfout")
        g_stored = [sem(f"gstored{s}") for s in range(2)]
        PER = 6
        after_front = (0, 1, 2, 4, 5, 7, 8, 10)
        after_back = {2: 3, 4: 6, 6: 9, 8: 11}
        split_step = (7, 1, 2, 3, 5, 6)
        load_step = (5, 6, 0, 1, 2, 3)
        store_step = (2, 3, 5, 6, 7, 8)
        tri_done, bc_turned, x_turned, a_done = (sem(n) for n in ("tri", "bcturned", "xturned", "adone"))
        xd_done, xe_done, cb_done, seg_raw, seg_done = (sem(n) for n in ("xd", "xe", "cb", "segraw", "seg"))
        bt_hi, bt_split, xd_hi, xd_split, xe_hi, xe_split = (
            sem(n) for n in ("bthi", "btsplit", "xdhi", "xdsplit", "xehi", "xesplit"))
        decayed, w_done, w_hi, w_split = (sem(n) for n in ("decayed", "wdone", "whi", "wsplit"))
        grown_done, ce_done, ce_hi, ce_split = (sem(n) for n in ("grown", "cedone", "cehi", "cesplit"))
        y_mm, s_mm, y_done, state_scaled, state_done, st_hi, st_split = (
            sem(n) for n in ("ymm", "smm", "ydone", "scaled", "state", "sthi", "stsplit"))
        whole_kept = sem("whole")
        block = ctx.enter_context(nc.Block())

        @block.sync
        def _(sp):
            sp.dma_start(drow[:], d_rows).then_inc(small_loaded, 16)
            def load_chunk(g, c):
                cols = slice(c * P, (c + 1) * P)
                loaded = chunk_loaded[c % 2]
                for n, b in enumerate((B0, C0)):
                    sp.dma_start(bcT[:, c % 2, n], proj[bass.ds(g + b, 1)].rearrange("a p n -> (a p) n")[:, cols]
                                 ).then_inc(loaded, 16)
                sp.dma_start(xT[:, c % 2], proj[bass.ds(g * GB + X0, GB)].rearrange("k p n -> p k n")[:, :, cols]
                             ).then_inc(loaded, 16)

            for c in range(2):
                load_chunk(0, c)
                load_weights(sp, ring, w_in, 0, c, G0 + GROUPS * c)
            with sp.Fori(0, GROUPS) as g:
                for c in range(TB + 1):
                    n = g * TB + c
                    for m in range(PER):
                        if store_step[m] == c:
                            sp.wait_ge(half_out, g * 2 * PER + 2 * m + 2)
                            sp.dma_start(proj[bass.ds(g + G0 + GROUPS * m, 1)].rearrange("a p n -> (a p) n"),
                                         out_tile[:, m % 2]).then_inc(g_stored[m % 2], 16)
                    for m in range(PER):
                        if load_step[m] == c:
                            later = int(m < 2)
                            load_weights(sp, ring, w_in, g * 3 + m // 2 + 3 * later, m % 2,
                                         g + later + G0 + GROUPS * m)
                    if c < TB:
                        sp.wait_ge(ce_done, n + 1)
                        sp.wait_ge(bc_turned, n + 1)
                        sp.wait_ge(x_turned, n + 1)
                        sp.wait_ge(skip_done, n + 1)
                        load_chunk(g + (c + 2) // TB, (c + 2) % TB)
                    if c:
                        sp.wait_ge(y_done, n * 2)
                        cols = slice((c - 1) * P, c * P)
                        sp.dma_start(y[bass.ds(g * GB + Y_SSD, GB)].rearrange("k p n -> p k n")[:, :, cols],
                                     yT[:, (c - 1) % 2]).then_inc(stored[(c - 1) % 2], 16)
            for s in range(2):
                sp.wait_ge(chunk_loaded[s], 48 * (GROUPS * TB // 2 + 1))
                sp.wait_ge(stored[s], 16 * GROUPS * TB // 2)
                sp.wait_ge(g_stored[s], 16 * 3 * GROUPS)
                sp.wait_ge(ring.loaded[s], 16 * (3 * GROUPS + 1))

        @block.tensor
        def _(pe):
            da_all = da[:].rearrange("p c h -> p (c h)")
            nc.tensor.matmul(ps_cs[:, 0], consts["tri"][:], da_all, start=True, stop=True)
            nc.tensor.matmul(ps_cs[:, 1], consts["ones"][:], da_all, start=True, stop=True).then_inc(cs_done, 1)

            with pe.Fori(0, GROUPS) as g:
                def front(c):
                    n = g * TB + c
                    pe.wait_ge(bc_split, n + 1)
                    pe.wait_ge(chunk_loaded[c % 2], (g * TB // 2 + c // 2) * 48 + 48)
                    pe.wait_ge(bt_split, n)
                    pe.wait_ge(cb_done, n)
                    nc.tensor.transpose(ps_bc[:, 0], bcT[:, c % 2, 0], consts["ident"][:])
                    for j, (l, r) in enumerate(split3((bch, bch), (bcl, bcl))):
                        last = nc.tensor.matmul(ps_bc[:, 1], l[:, 0], r[:, 1], start=(j == 0), stop=(j == 2))
                    last.then_inc(bc_turned, 1)
                    pe.wait_ge(xd_done, n)
                    for b in range(GB):
                        last = nc.tensor.transpose(ps_x[:, 2 * b:2 * b + 2].rearrange("p r d -> p (r d)"),
                                                   xT[:, c % 2, b], consts["ident"][:])
                    last.then_inc(x_turned, 1)
                    pe.wait_ge(tri_done, n + 1)
                    pe.wait_ge(seg_raw, n)
                    pe.wait_ge(grown_done, n)
                    for h in range(2):
                        last = nc.tensor.matmul(ps_a[:, 4 * h:4 * h + 4], consts["ones"][:],
                                                tri_da[:, 4 * h:4 * h + 4], start=True, stop=True)
                    last.then_inc(a_done, 1)

                def back(c):
                    n = g * TB + c
                    b = c % 2
                    pe.wait_ge(xd_split, n + 1)
                    pe.wait_ge(w_split, n + 1)
                    if c:
                        pe.wait_ge(ce_split, n + 1)
                        pe.wait_ge(st_split, n)
                    pe.wait_ge(y_done, n * 2)
                    for q in range(GB):
                        heads = slice(q * P, (q + 1) * P)
                        for j, (l, r) in enumerate(split3((xdh, wh), (xdl, wl))):
                            last = nc.tensor.matmul(ps_y[:, q], l[:, b, heads], r[:, b, 2 * q:2 * q + 2],
                                                    start=(j == 0), stop=(c == 0 and j == 2))
                        for j, (l, r) in enumerate(split3((sth, ceh), (stl, cel)) if c else ()):
                            last = nc.tensor.matmul(ps_y[:, q], l[:, heads], r[:, b, 2 * q:2 * q + 2],
                                                    start=False, stop=(j == 2))
                    last.then_inc(y_mm, 1)
                    pe.wait_ge(xe_split, n + 1)
                    pe.wait_ge(bt_split, n + 1)
                    pe.wait_ge(state_done, n)
                    for j, (l, r) in enumerate(split3((bth, xeh), (btl, xel))):
                        last = nc.tensor.matmul(ps_s[:], l[:, b], r[:, b], start=(j == 0), stop=(j == 2))
                    last.then_inc(s_mm, 1)

                def project(q):
                    m, h = q // 2, q % 2
                    if h == 0:
                        pe.wait_ge(ring.split[m % 2], g * 3 + m // 2 + 1)
                    pe.wait_ge(half_out, g * 2 * PER + q)
                    for k in range(KB):
                        for j, (l, r) in enumerate(split3((ring.hi, uh), (ring.lo, ul))):
                            last = nc.tensor.matmul(ps_g[:], l[:, m % 2, k], r[:, k, h * HALF:(h + 1) * HALF],
                                                    start=(k == 0 and j == 0), stop=(k == KB - 1 and j == 2))
                    last.then_inc(ring.used[m % 2] if h else half_done, 1)

                for c in range(TB + 1):
                    if c < TB:
                        front(c)
                        project(after_front[c])
                    if c:
                        back(c - 1)
                    if c in after_back:
                        project(after_back[c])

        @block.scalar
        def _(act):
            act.wait_ge(cs_diff, 1)
            nc.scalar.activation(to_end[:], to_end[:], ACT.Exp).then_inc(cs_exp, 1)

            def round_bc(n, c, loaded):
                act.wait_ge(chunk_loaded[c % 2], loaded)
                nc.scalar.activation(bch[:], bcT[:, c % 2], ACT.Copy).then_inc(bc_hi, 1)

            def round_gate_weights(m, i):
                act.wait_ge(ring.loaded[m % 2], i * 16 + 16)
                act.wait_ge(ring.used[m % 2], i)
                nc.scalar.activation(ring.hi[:, m % 2].rearrange("p k n -> p (k n)"), ring.raw[:, m % 2],
                                     ACT.Copy).then_inc(ring.hi_done[m % 2], 1)

            round_bc(0, 0, 48)
            round_gate_weights(0, 0)
            with act.Fori(0, GROUPS) as g:
                def evacuate(q):
                    m, h = q // 2, q % 2
                    if h:
                        act.wait_ge(ring.used[m % 2], g * 3 + m // 2 + 1)
                    else:
                        act.wait_ge(half_done, g * PER + m + 1)
                        act.wait_ge(g_stored[m % 2], (g * 3 + m // 2) * 16)
                    nc.scalar.activation(out_tile[:, m % 2, h * HALF:(h + 1) * HALF], ps_g[:],
                                         ACT.Copy).then_inc(half_out, 1)

                flat = "p r d -> p (r d)"
                for c in range(TB + 1):
                    n = g * TB + c
                    if c < TB:
                        b = c % 2
                        free = n - 1 if c >= 2 else g * TB
                        act.wait_ge(a_done, n + 1)
                        act.wait_ge(ce_done, n)
                        act.wait_ge(whole_kept, n)
                        nc.scalar.activation(grown[:], ps_a[:], ACT.Exp).then_inc(grown_done, 1)
                        act.wait_ge(seg_done, n + 1)
                        nc.scalar.activation(w[:], w[:], ACT.Exp).then_inc(decayed, 1)
                        act.wait_ge(y_mm, free)
                        act.wait_ge(xd_done, n + 1)
                        nc.scalar.activation(xdh[:, b], xd[:].rearrange(flat), ACT.Copy).then_inc(xd_hi, 1)
                        act.wait_ge(s_mm, free)
                        act.wait_ge(bc_turned, n + 1)
                        act.wait_ge(cb_done, n + 1)
                        nc.scalar.activation(bth[:, b], ps_bc[:, 0], ACT.Copy).then_inc(bt_hi, 1)
                        act.wait_ge(xe_done, n + 1)
                        nc.scalar.activation(xeh[:, b], xe[:].rearrange(flat), ACT.Copy).then_inc(xe_hi, 1)
                        round_bc(n + 1, (c + 1) % TB, (g * TB // 2 + (c + 1) // 2) * 48 + 48)
                        act.wait_ge(ce_done, n + 1)
                        nc.scalar.activation(ceh[:, b], ce[:], ACT.Copy).then_inc(ce_hi, 1)
                        act.wait_ge(w_done, n + 1)
                        nc.scalar.activation(wh[:, b], w[:], ACT.Copy).then_inc(w_hi, 1)
                        for m in range(PER):
                            if split_step[m] == c:
                                round_gate_weights(m, g * 3 + (m // 2 if m else 3))
                        evacuate(after_front[c])
                    if c:
                        act.wait_ge(state_done, n)
                        act.wait_ge(y_mm, n)
                        nc.scalar.activation(sth[:], state[:].rearrange(flat), ACT.Copy).then_inc(st_hi, 1)
                    if c in after_back:
                        evacuate(after_back[c])

        @block.gpsimd
        def _(pool):
            rest_of_weights(nc, pool, ring, 0, 0)
            with pool.Fori(0, GROUPS) as g:
                def decays(c):
                    pool.wait_ge(a_done, g * TB + c)
                    nc.gpsimd.tensor_tensor(
                        tri_da[:], consts["tri"][:, None, :].broadcast_to([P, R, P]),
                        da[:, c, bass.ds(g * R, R)][:, :, None].broadcast_to([P, R, P]), ALU.mult).then_inc(tri_done, 1)

                decays(0)
                for c in range(TB):
                    n = g * TB + c
                    pool.wait_ge(xd_done, n + 1)
                    pool.wait_ge(xe_split, n)
                    if c == 0:
                        pool.wait_ge(cs_exp, 1)
                    nc.gpsimd.tensor_tensor(
                        xe[:], xd[:], to_end[:, c, bass.ds(g * R, R)][:, :, None].broadcast_to([P, R, 64]),
                        ALU.mult).then_inc(xe_done, 1)
                    pool.wait_ge(grown_done, n + 1)
                    pool.wait_ge(ce_split, n)
                    nc.gpsimd.tensor_tensor(
                        ce[:], grown[:], bcT[:, c % 2, 1][:, None, :].broadcast_to([P, R, P]),
                        ALU.mult).then_inc(ce_done, 1)
                    pool.wait_ge(decayed, n + 1)
                    pool.wait_ge(cb_done, n + 1)
                    nc.gpsimd.tensor_tensor(w[:], w[:], cb[:, None, :].broadcast_to([P, R, P]),
                                            ALU.mult).then_inc(w_done, 1)
                    if c < TB - 1:
                        decays(c + 1)
                    if c >= 2:
                        pool.wait_ge(y_done, n * 2 - 2)
                    if c == 0:
                        pool.wait_ge(d_ready, g + 1)
                    pool.wait_ge(stored[c % 2], (g * TB // 2 + c // 2) * 16)
                    nc.gpsimd.tensor_tensor(
                        yT[:, c % 2], xT[:, c % 2], d_group[:, :, None].broadcast_to([P, GB, P]),
                        ALU.mult).then_inc(skip_done, 1)
                    for m in range(PER):
                        if split_step[m] == c:
                            rest_of_weights(nc, pool, ring, g * 3 + (m // 2 if m else 3), m % 2)

        @block.vector
        def _(dve):
            dve.wait_ge(small_loaded, 16)
            dve.wait_ge(cs_done, 1)
            flat = "p c h -> p (c h)"
            nc.vector.tensor_copy(a_cs[:].rearrange(flat), ps_cs[:, 0]).then_inc(cs_read, 1)
            dve.wait_ge(cs_read, 1)
            nc.vector.tensor_tensor(to_end[:].rearrange(flat), ps_cs[:, 1], a_cs[:].rearrange(flat),
                                    ALU.subtract).then_inc(cs_diff, 1)

            def rest_of_bc(n, c):
                dve.wait_ge(bc_hi, n + 1)
                nc.vector.tensor_tensor(bcl[:], bcT[:, c % 2], bch[:].bitcast(F32),
                                        ALU.subtract).then_inc(bc_split, 1)

            rest_of_bc(0, 0)
            with dve.Fori(0, GROUPS) as g:
                dve.wait_ge(skip_done, g * TB)
                nc.vector.tensor_tensor(d_group[:], drow[:, bass.ds(g * GB, GB)],
                                        consts["one"][:].broadcast_to([P, GB]), ALU.mult).then_inc(d_ready, 1)
                for c in range(TB + 1):
                    n = g * TB + c
                    b = c % 2
                    if c < TB:
                        heads = bass.ds(g * R, R)
                        dve.wait_ge(x_turned, n + 1)
                        dve.wait_ge(xd_hi, n)
                        dve.wait_ge(xe_done, n)
                        dve.wait_ge(xd_split, n)
                        nc.vector.tensor_tensor(xd[:], ps_x[:], dt[:, c, heads][:, :, None].broadcast_to([P, R, 64]),
                                                ALU.mult).then_inc(xd_done, 1)
                        dve.wait_ge(bc_turned, n + 1)
                        dve.wait_ge(w_done, n)
                        nc.vector.tensor_tensor(cb[:], ps_bc[:, 1], consts["tri"][:], ALU.mult).then_inc(cb_done, 1)
                        dve.wait_ge(grown_done, n + 1)
                        nc.vector.tensor_copy(whole[:, b], grown[:, :, P - 1]).then_inc(whole_kept, 1)
                        dve.wait_ge(w_split, n)
                        nc.vector.tensor_tensor(w[:], ps_a[:], a_cs[:, c, heads][:, :, None].broadcast_to([P, R, P]),
                                                ALU.subtract).then_inc(seg_raw, 1)
                        dve.wait_ge(seg_raw, n + 1)
                        nc.vector.tensor_scalar(w[:], w[:], 0.0, None, ALU.min).then_inc(seg_done, 1)
                        dve.wait_ge(xd_hi, n + 1)
                        nc.vector.tensor_tensor(xdl[:, b], xd[:].rearrange("p r d -> p (r d)"), xdh[:, b].bitcast(F32),
                                                ALU.subtract).then_inc(xd_split, 1)
                        dve.wait_ge(bt_hi, n + 1)
                        nc.vector.tensor_tensor(btl[:, b], ps_bc[:, 0], bth[:, b].bitcast(F32),
                                                ALU.subtract).then_inc(bt_split, 1)
                        dve.wait_ge(xe_hi, n + 1)
                        nc.vector.tensor_tensor(xel[:, b], xe[:].rearrange("p r d -> p (r d)"), xeh[:, b].bitcast(F32),
                                                ALU.subtract).then_inc(xe_split, 1)
                        rest_of_bc(n + 1, (c + 1) % TB)
                        dve.wait_ge(ce_hi, n + 1)
                        nc.vector.tensor_tensor(cel[:, b], ce[:], ceh[:, b].bitcast(F32),
                                                ALU.subtract).then_inc(ce_split, 1)
                        dve.wait_ge(w_hi, n + 1)
                        nc.vector.tensor_tensor(wl[:, b], w[:], wh[:, b].bitcast(F32),
                                                ALU.subtract).then_inc(w_split, 1)
                    if c:
                        m = n - 1
                        dve.wait_ge(y_mm, m + 1)
                        dve.wait_ge(skip_done, m + 1)
                        for h in range(2):
                            rows = slice(64 * h, 64 * h + 64)
                            nc.vector.tensor_tensor(yT[rows, 1 - b], ps_y[rows, :, h], yT[rows, 1 - b],
                                                    ALU.add).then_inc(y_done, 1)
                        dve.wait_ge(s_mm, m + 1)
                        if c > 1:
                            nc.vector.tensor_tensor(state[:], state[:],
                                                    whole[:, 1 - b, :, None].broadcast_to([P, R, 64]),
                                                    ALU.mult).then_inc(state_scaled, 1)
                            dve.wait_ge(state_scaled, g * (TB - 1) + c - 1)
                            nc.vector.tensor_tensor(state[:], ps_s[:], state[:], ALU.add).then_inc(state_done, 1)
                        else:
                            nc.vector.tensor_copy(state[:], ps_s[:]).then_inc(state_done, 1)
                        dve.wait_ge(st_hi, m + 1)
                        nc.vector.tensor_tensor(stl[:], state[:].rearrange("p r d -> p (r d)"), sth[:].bitcast(F32),
                                                ALU.subtract).then_inc(st_split, 1)


def memory_keys_values(nc, w_kv, kv, xh, xl, consts):
    with stage(nc) as ctx:
        ring = Ring(nc, ctx, "kv", consts)
        n_blocks = 2 * KB
        out_tile = ctx.enter_context(nc.sbuf_tensor("kv_out", [P, 2, M], F32))
        ps = ctx.enter_context(nc.psum_tensor("kv_ps", [P, 2, HALF], F32))
        evacuated = [nc.alloc_semaphore(f"kv_evac{s}") for s in range(2)]
        stored = [nc.alloc_semaphore(f"kv_stored{s}") for s in range(2)]
        block = ctx.enter_context(nc.Block())

        @block.sync
        def _(sp):
            for s in range(2):
                load_weights(sp, ring, w_kv, 0, s, s)
            with sp.Fori(0, n_blocks // 2 - 1) as i:
                for s in range(2):
                    load_weights(sp, ring, w_kv, i + 1, s, i * 2 + s + 2)
                    sp.wait_ge(evacuated[s], i + 1)
                    sp.dma_start(kv[bass.ds(i * 2 + s, 1)].rearrange("a p n -> (a p) n"),
                                 out_tile[:, s]).then_inc(stored[s], 16)
            for s in range(2):
                sp.wait_ge(evacuated[s], n_blocks // 2)
                sp.dma_start(kv[n_blocks - 2 + s], out_tile[:, s]).then_inc(stored[s], 16)
            for s in range(2):
                sp.wait_ge(stored[s], 16 * n_blocks // 2)

        @block.gpsimd
        def _(pool):
            with pool.Fori(0, n_blocks // 2) as i:
                for s in range(2):
                    rest_of_weights(nc, pool, ring, i, s)

        @block.tensor
        def _(pe):
            with pe.Fori(0, n_blocks // 2) as i:
                for s in range(2):
                    pe.wait_ge(ring.split[s], i + 1)
                    pe.wait_ge(evacuated[s], i)
                    product(nc, ring, s, xh, xl, ps[:, s], M).then_inc(ring.used[s], 1)

        @block.scalar
        def _(act):
            def round_on_act(i, s):
                act.wait_ge(ring.loaded[s], i * 16 + 16)
                act.wait_ge(ring.used[s], i)
                nc.scalar.activation(ring.hi[:, s].rearrange("p k n -> p (k n)"), ring.raw[:, s],
                                     ACT.Copy).then_inc(ring.hi_done[s], 1)

            def evacuate(i, s):
                act.wait_ge(ring.used[s], i + 1)
                act.wait_ge(stored[s], i * 16)
                nc.scalar.activation(out_tile[:, s], ps[:, s, 0:M], ACT.Copy).then_inc(evacuated[s], 1)

            for s in range(2):
                round_on_act(0, s)
            with act.Fori(0, n_blocks // 2 - 1) as i:
                for s in range(2):
                    evacuate(i, s)
                    round_on_act(i + 1, s)
            for s in range(2):
                evacuate(n_blocks // 2 - 1, s)


def memory_attention(nc, proj, kv, y, ssd_gain, consts):
    with stage(nc) as ctx:
        def sb(n, shape, dt=F32):
            return ctx.enter_context(nc.sbuf_tensor(f"ma_{n}", shape, dt))

        def sem(n):
            return nc.alloc_semaphore(f"ma_{n}")

        DB = 2
        qT, kT, vT = sb("qT", [P, DB, S]), sb("kT", [P, DB, M]), sb("vT", [P, DB, M])
        qh, ql = sb("qh", [P, DB, S], F32R), sb("ql", [P, DB, S], F32R)
        kh, kl = sb("kh", [P, DB, M], F32R), sb("kl", [P, DB, M], F32R)
        vh, vl = sb("vh", [P, MB, M], F32R), sb("vl", [P, MB, M], F32R)
        top, less, total, share = (sb(n, [P, 2]) for n in ("top", "less", "total", "share"))
        e, prob = sb("e", [P, 2, M]), sb("prob", [P, 2, M])
        pth, ptl = sb("pth", [P, MB, S], F32R), sb("ptl", [P, MB, S], F32R)
        y_tile = sb("y", [P, DB, S])
        ps_s = ctx.enter_context(nc.psum_tensor("ma_pss", [P, 2, HALF], F32))
        ps_t = ctx.enter_context(nc.psum_tensor("ma_pst", [P, 2, HALF], F32))
        ps_v = ctx.enter_context(nc.psum_tensor("ma_psv", [P, MB, M], F32))
        ps_y = ctx.enter_context(nc.psum_tensor("ma_psy", [P, 2, HALF], F32))
        ps_n = ctx.enter_context(nc.psum_tensor("ma_psn", [P, HALF], F32))
        loaded, k_hi, q_hi, k_split, q_split = (sem(n) for n in ("ld", "khi", "qhi", "ksplit", "qsplit"))
        v_turned, v_hi, v_split = sem("vturned"), sem("vhi"), sem("vsplit")
        scores, topped, lessened, e_done, inverted, prob_done = (
            sem(n) for n in ("scores", "topped", "less", "e", "inverted", "prob"))
        turned, pt_hi, pt_split, y_mm, y_out, stored = (
            sem(n) for n in ("turned", "pthi", "ptsplit", "ymm", "yout", "stored"))

        gy, gz = sb("gy", [P, 2, GB, S]), sb("gz", [P, GB, S])
        gain, rstd = sb("gain", [P, GROUPS * GB]), sb("rstd", [P, S])
        gain_loaded = sem("gain")
        g_loaded, g_stored = ([sem(f"{n}{s}") for s in range(2)] for n in ("gld", "gst"))
        gated, squared, summed, rooted, g_inverted, normed = (
            sem(n) for n in ("gated", "squared", "summed", "rooted", "ginverted", "normed"))
        LAG = 2
        STEPS = TB + LAG
        block = ctx.enter_context(nc.Block())

        def done(h, t, k):
            return h * TB + max(t - k + 1, 0)

        @block.sync
        def _(sp):
            sp.dma_start(gain[:], ssd_gain).then_inc(gain_loaded, 16)

            def load_head(h):
                if h:
                    sp.wait_ge(q_split, h)
                    sp.wait_ge(k_split, h)
                    sp.wait_ge(v_turned, h)
                for dst, src, b in ((kT, kv, 0), (vT, kv, KB), (qT, proj, MQ0)):
                    sp.dma_start(dst[:], src[h * DB + b:h * DB + b + DB].rearrange("k p n -> p k n")).then_inc(loaded, 16)

            def load_group(g):
                if g:
                    sp.wait_ge(summed, 2 * g)
                if g >= 2:
                    sp.wait_ge(g_stored[g % 2], 16 * (g // 2))
                sp.dma_start(gy[:, g % 2], y[Y_SSD + g * GB:Y_SSD + (g + 1) * GB].rearrange("k p n -> p k n")
                             ).then_inc(g_loaded[g % 2], 16)
                sp.dma_start(gz[:], proj[Z0 + g * GB:Z0 + (g + 1) * GB].rearrange("k p n -> p k n")
                             ).then_inc(g_loaded[g % 2], 16)

            load_head(0)
            load_group(0)
            for h in range(MEM_HEADS):
                if h + 1 < MEM_HEADS:
                    load_head(h + 1)
                    load_group(h + 1)
                sp.wait_ge(y_out, h * 4 + 4)
                sp.dma_start(y[h * DB + Y_MEM:h * DB + Y_MEM + DB].rearrange("k p n -> p k n"), y_tile[:]).then_inc(stored, 16)
                sp.wait_ge(normed, h * 2 * GB + 2 * GB)
                sp.dma_start(y[Y_SSD + h * GB:Y_SSD + (h + 1) * GB].rearrange("k p n -> p k n"),
                             gy[:, h % 2]).then_inc(g_stored[h % 2], 16)
            sp.wait_ge(stored, 16 * MEM_HEADS)
            for s in range(2):
                sp.wait_ge(g_stored[s], 16 * GROUPS // 2)

        @block.tensor
        def _(pe):
            def sum_squares(h, half):
                pe.wait_ge(squared, h * GB + GB)
                pe.wait_ge(rooted, h * 2 + half)
                for b in range(GB):
                    last = nc.tensor.matmul(ps_n[:], consts["ones"][:], gz[:, b, half * HALF:(half + 1) * HALF],
                                            start=(b == 0), stop=(b == GB - 1))
                last.then_inc(summed, 1)

            with pe.Fori(0, MEM_HEADS) as h:
                pe.wait_ge(loaded, h * 48 + 48)
                for m in range(MB):
                    for d in range(DB):
                        last = nc.tensor.transpose(ps_v[:, m, d * P:(d + 1) * P], vT[:, d, m * P:(m + 1) * P],
                                                   consts["ident"][:])
                last.then_inc(v_turned, 1)
                pe.wait_ge(q_split, h + 1)
                pe.wait_ge(k_split, h + 1)
                for t in range(STEPS):
                    if t < TB:
                        pe.wait_ge(e_done, done(h, t, 2))
                        for d in range(DB):
                            for j, (l, r) in enumerate(split3((qh, kh), (ql, kl))):
                                last = nc.tensor.matmul(ps_s[:, t % 2, 0:M], l[:, d, t * P:(t + 1) * P], r[:, d],
                                                        start=(d == 0 and j == 0), stop=(d == DB - 1 and j == 2))
                        last.then_inc(scores, 1)
                    if t >= LAG:
                        u = t - LAG
                        pe.wait_ge(prob_done, done(h, t, LAG))
                        pe.wait_ge(pt_split, done(h, u, 2))
                        for m in range(MB):
                            last = nc.tensor.transpose(ps_t[:, u % 2, m * P:(m + 1) * P],
                                                       prob[:, u % 2, m * P:(m + 1) * P], consts["ident"][:])
                        last.then_inc(turned, 1)
                    if t >= 6 and t < 8:
                        sum_squares(h, t - 6)
                pe.wait_ge(pt_split, h * TB + TB)
                pe.wait_ge(v_split, h + 1)
                for u in range(4):
                    d, half = u // 2, u % 2
                    pe.wait_ge(y_out, h * 4 + (u - 1 if u >= 2 else 0))
                    for m in range(MB):
                        for j, (l, r) in enumerate(split3((vh, pth), (vl, ptl))):
                            last = nc.tensor.matmul(ps_y[:, u % 2], l[:, m, d * P:(d + 1) * P],
                                                    r[:, m, half * HALF:(half + 1) * HALF],
                                                    start=(m == 0 and j == 0), stop=(m == MB - 1 and j == 2))
                    last.then_inc(y_mm, 1)

        @block.scalar
        def _(act):
            def take_root(h, half):
                act.wait_ge(summed, h * 2 + half + 1)
                act.wait_ge(normed, h * 2 * GB)
                nc.scalar.activation(rstd[:, half * HALF:(half + 1) * HALF], ps_n[:], ACT.Sqrt, scale=1.0 / (GB * P),
                                     bias=consts["eps"][:]).then_inc(rooted, 1)

            with act.Fori(0, MEM_HEADS // 2) as i:
                for s in range(2):
                    h = i * 2 + s
                    act.wait_ge(loaded, h * 48 + 48)
                    act.wait_ge(y_mm, h * 4)
                    act.wait_ge(scores, h * TB)
                    nc.scalar.activation(qh[:], qT[:], ACT.Copy).then_inc(q_hi, 1)
                    nc.scalar.activation(kh[:], kT[:], ACT.Copy).then_inc(k_hi, 1)
                    act.wait_ge(v_turned, h + 1)
                    nc.scalar.activation(vh[:], ps_v[:], ACT.Copy).then_inc(v_hi, 1)
                    for t in range(STEPS):
                        if t < TB:
                            act.wait_ge(lessened, h * TB + t + 1)
                            act.wait_ge(prob_done, done(h, t, 2))
                            nc.scalar.activation(e[:, t % 2], ps_s[:, t % 2, 0:M], ACT.Exp, scale=MEM_SCALE,
                                                 bias=less[:, t % 2:t % 2 + 1],
                                                 accum_out=total[:, t % 2:t % 2 + 1]).then_inc(e_done, 1)
                        if t >= LAG:
                            u = t - LAG
                            act.wait_ge(turned, h * TB + u + 1)
                            nc.scalar.activation(pth[:, :, u * P:(u + 1) * P],
                                                 ps_t[:, u % 2, 0:M].rearrange("p (m t) -> p m t", m=MB),
                                                 ACT.Copy).then_inc(pt_hi, 1)
                        if t >= 2 and t < 2 + GB:
                            b = t - 2
                            act.wait_ge(gated, h * GB + b + 1)
                            nc.scalar.activation(gz[:, b], gy[:, s, b], ACT.Square).then_inc(squared, 1)
                        if t in (7, 8):
                            take_root(h, t - 7)
                    for u in range(4):
                        d, half = u // 2, u % 2
                        act.wait_ge(y_mm, h * 4 + u + 1)
                        act.wait_ge(stored, h * 16)
                        nc.scalar.activation(y_tile[:, d, half * HALF:(half + 1) * HALF], ps_y[:, u % 2],
                                             ACT.Copy).then_inc(y_out, 1)

        @block.vector
        def _(dve):
            def norm(h, s, half):
                cols = slice(half * HALF, (half + 1) * HALF)
                dve.wait_ge(rooted, h * 2 + half + 1)
                nc.vector.reciprocal(rstd[:, cols], rstd[:, cols]).then_inc(g_inverted, 1)
                dve.wait_ge(g_inverted, h * 2 + half + 1)
                for b in range(GB):
                    nc.vector.scalar_tensor_tensor(gy[:, s, b, cols], gy[:, s, b, cols], gain[:, bass.ds(h * GB + b, 1)],
                                                   rstd[:, cols], ALU.mult, ALU.mult).then_inc(normed, 1)

            dve.wait_ge(gain_loaded, 16)
            with dve.Fori(0, MEM_HEADS // 2) as i:
                for s in range(2):
                    h = i * 2 + s
                    dve.wait_ge(q_hi, h + 1)
                    nc.vector.tensor_tensor(ql[:], qT[:], qh[:].bitcast(F32), ALU.subtract).then_inc(q_split, 1)
                    dve.wait_ge(k_hi, h + 1)
                    nc.vector.tensor_tensor(kl[:], kT[:], kh[:].bitcast(F32), ALU.subtract).then_inc(k_split, 1)
                    dve.wait_ge(v_hi, h + 1)
                    nc.vector.tensor_tensor(vl[:], ps_v[:], vh[:].bitcast(F32), ALU.subtract).then_inc(v_split, 1)
                    for t in range(STEPS):
                        if t < TB:
                            n = h * TB + t
                            c = slice(t % 2, t % 2 + 1)
                            dve.wait_ge(scores, n + 1)
                            nc.vector.tensor_reduce(top[:, c], ps_s[:, t % 2, 0:M], AX_X, ALU.max).then_inc(topped, 1)
                            dve.wait_ge(topped, n + 1)
                            dve.wait_ge(e_done, done(h, t, 2))
                            nc.vector.tensor_scalar(less[:, c], top[:, c], -MEM_SCALE, None, ALU.mult).then_inc(lessened, 1)
                        if t and t <= TB:
                            n = h * TB + t - 1
                            b = (t - 1) % 2
                            c = slice(b, b + 1)
                            dve.wait_ge(e_done, n + 1)
                            nc.vector.reciprocal(share[:, c], total[:, c]).then_inc(inverted, 1)
                            dve.wait_ge(inverted, n + 1)
                            dve.wait_ge(turned, done(h, t - 1, 2))
                            nc.vector.tensor_scalar(prob[:, b], e[:, b], share[:, c], None, ALU.mult).then_inc(prob_done, 1)
                        if t >= LAG:
                            u = t - LAG
                            dve.wait_ge(pt_hi, h * TB + u + 1)
                            cols = slice(u * P, (u + 1) * P)
                            nc.vector.tensor_tensor(ptl[:, :, cols],
                                                    ps_t[:, u % 2, 0:M].rearrange("p (m t) -> p m t", m=MB),
                                                    pth[:, :, cols].bitcast(F32), ALU.subtract).then_inc(pt_split, 1)
                        if t >= 1 and t < 1 + GB:
                            b = t - 1
                            dve.wait_ge(g_loaded[s], i * 32 + 32)
                            nc.vector.tensor_tensor(gy[:, s, b], gy[:, s, b], gz[:, b], ALU.mult).then_inc(gated, 1)
                        if t == 8:
                            norm(h, s, 0)
                    norm(h, s, 1)


def merge_branches(nc, w_out, proj, y, merged, consts):
    gates_of = (0, 1, 1, 2)
    with stage(nc) as ctx:
        def sb(n, shape, dt=F32):
            return ctx.enter_context(nc.sbuf_tensor(f"mg_{n}", shape, dt))

        def sem(n):
            return nc.alloc_semaphore(f"mg_{n}")

        ring = Ring(nc, ctx, "mg", consts)
        raw = sb("raw", [P, KB, S])
        yh, yl = sb("yh", [P, KB, S], F32R), sb("yl", [P, KB, S], F32R)
        gate, gated = sb("gate", [P, 2, S]), sb("gated", [P, 2, S])
        ps = ctx.enter_context(nc.psum_tensor("mg_ps", [P, 2, S], F32))
        y_loaded = [sem(f"yld{k}") for k in range(KB)]
        block_used = sem("bused")
        gate_loaded = [sem(f"gld{s}") for s in range(2)]
        gate_done = [sem(f"gdone{s}") for s in range(2)]
        y_hi, y_split, gated_done, summed = sem("yhi"), sem("ysplit"), sem("gated"), sem("summed")
        multiplied = [sem(f"mult{s}") for s in range(2)]
        cleared = sem("cleared")
        block = ctx.enter_context(nc.Block())
        NP = KB // 2

        @block.sync
        def _(sp):
            def pair_of_blocks(part, i):
                for s in range(2):
                    load_weights(sp, ring, w_out, i + part * NP, s, i * 2 + s + part * KB)
                    sp.wait_ge(multiplied[s], i + part * NP)
                    sp.dma_start(gate[:, s], proj[bass.ds(i * 2 + s + G0 + gates_of[part] * KB, 1)]
                                 .rearrange("a p n -> (a p) n")).then_inc(gate_loaded[s], 16)

            def load_y(part):
                for k in range(KB):
                    if part:
                        sp.wait_ge(y_split, (part - 1) * KB + k + 1)
                    sp.dma_start(raw[:, k], y[part * KB + k]).then_inc(y_loaded[k], 16)

            for part in range(4):
                if part == 0:
                    load_y(0)
                pair_of_blocks(part, 0)
                if part < 3:
                    load_y(part + 1)
                with sp.Fori(1, NP) as i:
                    pair_of_blocks(part, i)

        @block.gpsimd
        def _(pool):
            with pool.Fori(0, 4 * NP) as i:
                for s in range(2):
                    split_weights(nc, pool, ring, i, s)

        @block.scalar
        def _(act):
            for part in range(4):
                for k in range(KB):
                    act.wait_ge(y_loaded[k], 16 * (part + 1))
                    if part and k < KB - 1:
                        act.wait_ge(block_used, (part * KB - 1) * (KB - 1) + k + 1)
                    elif part:
                        act.wait_ge(ring.used[1], part * NP)
                    nc.scalar.activation(yh[:, k], raw[:, k], ACT.Copy).then_inc(y_hi, 1)
                with act.Fori(part * NP, part * NP + NP) as i:
                    for s in range(2):
                        act.wait_ge(gate_loaded[s], i * 16 + 16)
                        nc.scalar.activation(gate[:, s], gate[:, s], ACT.Sigmoid).then_inc(gate_done[s], 1)

        @block.tensor
        def _(pe):
            for part in range(4):
                with pe.Fori(part * NP, part * NP + NP) as i:
                    for s in range(2):
                        pe.wait_ge(ring.split[s], i + 1)
                        pe.wait_ge(multiplied[s], i)
                        for h in range(2):
                            cols = slice(h * HALF, (h + 1) * HALF)
                            for k in range(KB):
                                if h == 0:
                                    pe.wait_ge(y_split, part * KB + k + 1)
                                for j, (w, x) in enumerate(split3((ring.hi, yh), (ring.lo, yl))):
                                    last = nc.tensor.matmul(ps[:, s, cols], w[:, s, k], x[:, k, cols],
                                                            start=(k == 0 and j == 0), stop=(k == KB - 1 and j == 2))
                                if h == 1 and k < KB - 1:
                                    last.then_inc(block_used, 1)
                        last.then_inc(ring.used[s], 1)

        @block.vector
        def _(dve):
            nc.vector.memset(merged[:], 0.0).then_inc(cleared, 1)
            dve.wait_ge(cleared, 1)
            for part in range(4):
                for k in range(KB):
                    n = part * KB + k
                    dve.wait_ge(y_hi, n + 1)
                    nc.vector.tensor_tensor(yl[:, k], raw[:, k], yh[:, k].bitcast(F32),
                                            ALU.subtract).then_inc(y_split, 1)
                with dve.Fori(part * NP, part * NP + NP) as i:
                    for s in range(2):
                        dve.wait_ge(ring.used[s], i + 1)
                        dve.wait_ge(gate_done[s], i + 1)
                        dve.wait_ge(summed, i * 2 + s)
                        nc.vector.tensor_tensor(gated[:, s], ps[:, s], gate[:, s], ALU.mult).then_inc(multiplied[s], 1)
                        dve.wait_ge(multiplied[s], i + 1)
                        row = merged[:, bass.ds(i * 2 + s - part * KB, 1)].rearrange("p a n -> p (a n)")
                        nc.vector.tensor_tensor(row, row, gated[:, s], ALU.add).then_inc(summed, 1)


def split_blocks(nc, name, x, xh, xl):
    with stage(nc) as ctx:
        hi_done = nc.alloc_semaphore(f"{name}_hi")
        block = ctx.enter_context(nc.Block())

        @block.scalar
        def _(act):
            for k in range(KB):
                nc.scalar.activation(xh[:, k], x[:, k], ACT.Copy).then_inc(hi_done, 1)

        @block.vector
        def _(dve):
            for k in range(KB):
                dve.wait_ge(hi_done, k + 1)
                nc.vector.tensor_tensor(xl[:, k], x[:, k], xh[:, k].bitcast(F32), ALU.subtract)


def output_projection(nc, w_o, xh, xl, mix, consts):
    with stage(nc) as ctx:
        ring = Ring(nc, ctx, "wo", consts)
        ps = ctx.enter_context(nc.psum_tensor("wo_ps", [P, 2, S], F32))
        evacuated = [nc.alloc_semaphore(f"wo_evac{s}") for s in range(2)]
        block = ctx.enter_context(nc.Block())

        @block.sync
        def _(sp):
            with sp.Fori(0, KB // 2) as i:
                for s in range(2):
                    load_weights(sp, ring, w_o, i, s, i * 2 + s)

        @block.gpsimd
        def _(pool):
            with pool.Fori(0, KB // 2) as i:
                for s in range(2):
                    split_weights(nc, pool, ring, i, s)

        @block.tensor
        def _(pe):
            with pe.Fori(0, KB // 2) as i:
                for s in range(2):
                    pe.wait_ge(ring.split[s], i + 1)
                    pe.wait_ge(evacuated[s], i)
                    product(nc, ring, s, xh, xl, ps[:, s], S).then_inc(ring.used[s], 1)

        @block.scalar
        def _(act):
            with act.Fori(0, KB // 2) as i:
                for s in range(2):
                    act.wait_ge(ring.used[s], i + 1)
                    nc.scalar.activation(mix[:, bass.ds(i * 2 + s, 1)].rearrange("p a n -> p (a n)"), ps[:, s],
                                         ACT.Copy).then_inc(evacuated[s], 1)


def add_normed(nc, name, xT, gain_row, base, dst, consts):
    with stage(nc) as ctx:
        def sb(n, shape, dt=F32):
            return ctx.enter_context(nc.sbuf_tensor(f"{name}_{n}", shape, dt))

        def sem(n):
            return nc.alloc_semaphore(f"{name}_{n}")

        gain, tile, square, scaled = sb("gain", [P, D]), sb("tile", [P, TB, D]), sb("sq", [P, D]), sb("scaled", [P, 2, D])
        sums, root, rstd = sb("sums", [P, TB]), sb("root", [P, TB]), sb("rstd", [P, TB])
        ps = ctx.enter_context(nc.psum_tensor(f"{name}_ps", [P, 2, D], F32))
        gain_loaded = sem("gain")
        loaded, stored = [sem(f"ld{t}") for t in range(TB)], sem("st")
        turned, summed, rooted, inverted, scaled_done, added = (
            sem(n) for n in ("turned", "summed", "rooted", "inverted", "scaled_done", "added"))
        block = ctx.enter_context(nc.Block())

        @block.sync
        def _(sp):
            sp.dma_start(gain[:], gain_row).then_inc(gain_loaded, 16)
            for t in range(TB):
                sp.dma_start(tile[:, t], base[t * P:(t + 1) * P, :]).then_inc(loaded[t], 16)
            for t in range(TB):
                sp.wait_ge(added, t + 1)
                sp.dma_start(dst[t * P:(t + 1) * P, :], tile[:, t]).then_inc(stored, 16)
            sp.wait_ge(stored, 16 * TB)

        @block.tensor
        def _(pe):
            for t in range(TB):
                if t >= 2:
                    pe.wait_ge(scaled_done, t - 1)
                for k in range(KB):
                    last = nc.tensor.transpose(ps[:, t % 2, k * P:(k + 1) * P], xT[:, k, t * P:(t + 1) * P],
                                               consts["ident"][:])
                last.then_inc(turned, 1)

        @block.scalar
        def _(act):
            for t in range(TB):
                act.wait_ge(turned, t + 1)
                nc.scalar.activation(square[:], ps[:, t % 2], ACT.Square, accum_out=sums[:, t:t + 1]).then_inc(summed, 1)
                act.wait_ge(summed, t + 1)
                nc.scalar.activation(root[:, t:t + 1], sums[:, t:t + 1], ACT.Sqrt, scale=1.0 / D,
                                     bias=consts["eps"][:]).then_inc(rooted, 1)

        @block.vector
        def _(dve):
            dve.wait_ge(gain_loaded, 16)
            for t in range(TB):
                dve.wait_ge(rooted, t + 1)
                nc.vector.reciprocal(rstd[:, t:t + 1], root[:, t:t + 1]).then_inc(inverted, 1)
                dve.wait_ge(inverted, t + 1)
                nc.vector.scalar_tensor_tensor(scaled[:, t % 2], ps[:, t % 2], rstd[:, t:t + 1], gain[:],
                                               ALU.mult, ALU.mult).then_inc(scaled_done, 1)
                dve.wait_ge(scaled_done, t + 1)
                dve.wait_ge(loaded[t], 16)
                nc.vector.tensor_tensor(tile[:, t], tile[:, t], scaled[:, t % 2], ALU.add).then_inc(added, 1)


def mlp(nc, w_up, w_down, xh, xl, out, consts):
    with stage(nc) as ctx:
        def sb(n, shape, dt=F32):
            return ctx.enter_context(nc.sbuf_tensor(f"ff_{n}", shape, dt))

        def sem(n):
            return nc.alloc_semaphore(f"ff_{n}")

        ring = Ring(nc, ctx, "ff", consts)
        fh, fl = sb("fh", [P, KB, S], F32R), sb("fl", [P, KB, S], F32R)
        positive, square = sb("pos", [P, 2, S]), sb("sq", [P, 2, S])
        ps = ctx.enter_context(nc.psum_tensor("ff_ps", [P, 2, S], F32))
        pos_done, sq_done, f_hi, f_split = ([sem(f"{n}{s}") for s in range(2)] for n in ("posdone", "sqdone", "fhi", "fsplit"))
        added = [sem(f"added{s}") for s in range(2)]
        cleared = sem("cleared")
        NP = KB // 2
        block = ctx.enter_context(nc.Block())

        @block.sync
        def _(sp):
            with sp.Fori(0, FF_CHUNKS) as f:
                with sp.Fori(0, NP) as i:
                    for s in range(2):
                        load_weights(sp, ring, w_up, f * 2 * NP + i, s, f * KB + i * 2 + s)
                with sp.Fori(0, NP) as i:
                    for s in range(2):
                        load_weights(sp, ring, w_down, f * 2 * NP + NP + i, s, f * KB + i * 2 + s)

        @block.gpsimd
        def _(pool):
            with pool.Fori(0, FF_CHUNKS * 2 * NP) as i:
                for s in range(2):
                    split_weights(nc, pool, ring, i, s)

        @block.tensor
        def _(pe):
            with pe.Fori(0, FF_CHUNKS) as f:
                with pe.Fori(0, NP) as i:
                    for s in range(2):
                        pe.wait_ge(ring.split[s], f * 2 * NP + i + 1)
                        pe.wait_ge(pos_done[s], f * NP + i)
                        pe.wait_ge(added[s], f * NP)
                        product(nc, ring, s, xh, xl, ps[:, s], S).then_inc(ring.used[s], 1)
                with pe.Fori(0, NP) as i:
                    for s in range(2):
                        for r in range(2):
                            pe.wait_ge(f_split[r], f * NP + NP)
                        pe.wait_ge(ring.split[s], f * 2 * NP + NP + i + 1)
                        pe.wait_ge(added[s], f * NP + i)
                        product(nc, ring, s, fh, fl, ps[:, s], S).then_inc(ring.used[s], 1)

        @block.scalar
        def _(act):
            with act.Fori(0, FF_CHUNKS) as f:
                with act.Fori(0, NP) as i:
                    for s in range(2):
                        act.wait_ge(ring.used[s], f * 2 * NP + i + 1)
                        act.wait_ge(sq_done[s], f * NP + i)
                        nc.scalar.activation(positive[:, s], ps[:, s], ACT.Relu).then_inc(pos_done[s], 1)
                        act.wait_ge(sq_done[s], f * NP + i + 1)
                        nc.scalar.activation(fh[:, bass.ds(i * 2 + s, 1)].rearrange("p a n -> p (a n)"),
                                             square[:, s], ACT.Copy).then_inc(f_hi[s], 1)

        @block.vector
        def _(dve):
            nc.vector.memset(out[:], 0.0).then_inc(cleared, 1)
            dve.wait_ge(cleared, 1)
            with dve.Fori(0, FF_CHUNKS) as f:
                with dve.Fori(0, NP) as i:
                    for s in range(2):
                        dve.wait_ge(pos_done[s], f * NP + i + 1)
                        dve.wait_ge(f_split[s], f * NP + i)
                        nc.vector.tensor_tensor(square[:, s], positive[:, s], positive[:, s],
                                                ALU.mult).then_inc(sq_done[s], 1)
                        dve.wait_ge(f_hi[s], f * NP + i + 1)
                        one = bass.ds(i * 2 + s, 1)
                        nc.vector.tensor_tensor(fl[:, one].rearrange("p a n -> p (a n)"), square[:, s],
                                                fh[:, one].rearrange("p a n -> p (a n)").bitcast(F32),
                                                ALU.subtract).then_inc(f_split[s], 1)
                with dve.Fori(0, NP) as i:
                    for s in range(2):
                        dve.wait_ge(ring.used[s], f * 2 * NP + NP + i + 1)
                        row = out[:, bass.ds(i * 2 + s, 1)].rearrange("p a n -> p (a n)")
                        nc.vector.tensor_tensor(row, ps[:, s], row, ALU.add).then_inc(added[s], 1)


def set_constants(nc, consts):
    with stage(nc) as ctx:
        set_, shaped = (nc.alloc_semaphore("const_set")), (nc.alloc_semaphore("const_shaped"))
        block = ctx.enter_context(nc.Block())

        @block.gpsimd
        def _(pool):
            for name, value in (("ident", 0.0), ("tri", 1.0), ("before", 1.0), ("ones", 1.0), ("one", 1.0), ("eps", EPS)):
                nc.gpsimd.memset(consts[name][:], value).then_inc(set_, 1)
            pool.wait_ge(set_, 6)
            ident, tri, before = consts["ident"][:], consts["tri"][:], consts["before"][:]
            nc.gpsimd.affine_select(out=ident, in_=ident, pattern=[[-1, P]], compare_op=ALU.not_equal, fill=1.0,
                                    base=0, channel_multiplier=1).then_inc(shaped, 1)
            nc.gpsimd.affine_select(out=tri, in_=tri, pattern=[[1, P]], compare_op=ALU.is_ge, fill=0.0,
                                    base=0, channel_multiplier=-1).then_inc(shaped, 1)
            nc.gpsimd.affine_select(out=before, in_=before, pattern=[[-1, P]], compare_op=ALU.is_gt, fill=0.0,
                                    base=0, channel_multiplier=1).then_inc(shaped, 1)


def layer(nc, a, out, scratch):
    proj, y, kv, h = (scratch[n] for n in ("proj", "y", "kv", "h"))
    with ExitStack() as ctx:
        def sb(c, n, shape, dt=F32):
            return c.enter_context(nc.sbuf_tensor(n, shape, dt))

        consts = {n: sb(ctx, n, [P, P]) for n in ("ident", "tri", "before", "ones")}
        consts |= {n: sb(ctx, n, [P, 1]) for n in ("one", "eps")}
        set_constants(nc, consts)
        dt, da = sb(ctx, "dt", [P, TB, SSD_HEADS]), sb(ctx, "da", [P, TB, SSD_HEADS])
        with ExitStack() as c:
            xh, xl = sb(c, "memh", [P, KB, M], F32R), sb(c, "meml", [P, KB, M], F32R)
            norm_to_feature_major(nc, "nm", a["mem"], M, a["norm_mem"], xh, xl, consts)
            memory_keys_values(nc, a["w_mem_kv"], kv, xh, xl, consts)
        with ExitStack() as c:
            xh, xl = sb(c, "uh", [P, KB, S], F32R), sb(c, "ul", [P, KB, S], F32R)
            norm_to_feature_major(nc, "nu", a["x"], S, a["norm_mix_pre"], xh, xl, consts)
            input_projection(nc, a["w_in"], a["w_dt"], proj,
                             a["dt_bias"].broadcast_to([P, 32]), a["a_log"].broadcast_to([P, 32]), dt, da, xh, xl, consts)
            stick_breaking(nc, a["w_in"], a["conv_w"], a["conv_b"], proj, y, xh, xl, consts)
            ssd(nc, a["w_in"], proj, y, dt, da, a["d_skip"], xh, xl, consts)
        memory_attention(nc, proj, kv, y, a["ssd_norm"], consts)
        with ExitStack() as c:
            merged = sb(c, "merged", [P, KB, S])
            merge_branches(nc, a["w_branch"], proj, y, merged, consts)
            xh, xl = sb(c, "mh", [P, KB, S], F32R), sb(c, "ml", [P, KB, S], F32R)
            split_blocks(nc, "ms", merged, xh, xl)
            output_projection(nc, a["w_o"], xh, xl, merged, consts)
            add_normed(nc, "h1", merged, a["norm_mix_post"].broadcast_to([P, D]), a["x"], h, consts)
        with ExitStack() as c:
            xh, xl = sb(c, "vh", [P, KB, S], F32R), sb(c, "vl", [P, KB, S], F32R)
            norm_to_feature_major(nc, "nh", h, S, a["norm_mlp_pre"], xh, xl, consts)
            ff = sb(c, "ff", [P, KB, S])
            mlp(nc, a["w_up"], a["w_down"], xh, xl, ff, consts)
            add_normed(nc, "h2", ff, a["norm_mlp_post"].broadcast_to([P, D]), h, out, consts)


def lay_out(inputs):
    import numpy as np
    x = {k: np.asarray(v) for k, v in inputs.items()}
    n_qkv_z_xbc, n_dt = Q0 * P + MQ0 * P, SSD_HEADS
    w_in = x["w_in"][0]

    def tiles(w):
        r, c = w.shape[0] // D, w.shape[1] // P
        return np.ascontiguousarray(w.reshape(r, KB, P, c, P).transpose(0, 3, 2, 1, 4).reshape(r * c, P, D))

    def columns(v):
        return np.ascontiguousarray(v.reshape(-1, P).T)

    return {
        "x": x["x"][0], "mem": x["mem"][0],
        "w_in": tiles(np.concatenate([w_in[:, :n_qkv_z_xbc], w_in[:, n_qkv_z_xbc + n_dt:]], axis=1)),
        "w_dt": np.ascontiguousarray(w_in[:, n_qkv_z_xbc:n_qkv_z_xbc + n_dt].reshape(KB, P, n_dt).transpose(1, 0, 2)),
        "conv_w": np.ascontiguousarray(x["conv_w"][0].reshape(CONV, -1, P).transpose(2, 1, 0)),
        "conv_b": columns(x["conv_b"][0]),
        "dt_bias": x["dt_bias"], "a_log": x["a_log"],
        "d_skip": np.ascontiguousarray(np.repeat(x["d_skip"][0], 64).reshape(-1, P).T),
        "ssd_norm": columns(x["ssd_norm"][0]),
        "norm_mix_pre": columns(x["norm_mix_pre"][0]), "norm_mem": columns(x["norm_mem"][0]),
        "norm_mlp_pre": columns(x["norm_mlp_pre"][0]),
        "norm_mix_post": x["norm_mix_post"], "norm_mlp_post": x["norm_mlp_post"],
        "w_mem_kv": tiles(x["w_mem_kv"][0]),
        "w_branch": tiles(np.concatenate([x["w_sb_out"][0], x["w_ssd_out"][0], x["w_mem_out"][0]], axis=0)),
        "w_o": tiles(x["w_o"][0]), "w_up": tiles(x["w_up"][0]), "w_down": tiles(x["w_down"][0]),
    }


def kernel(**inputs):
    import numpy as np
    import concourse.bacc as bacc
    from concourse.bass_utils import run_bass_kernel_spmd

    nc = bacc.Bacc("TRN2", target_bir_lowering=False, num_devices=1)
    arrays = {f"in_{k}": v for k, v in lay_out(inputs).items()}
    a = {k[3:]: nc.dram_tensor(k, v.shape, mybir.dt.from_np(v.dtype), kind="ExternalInput").ap()
         for k, v in arrays.items()}
    out = nc.dram_tensor("out", (S, D), F32, kind="ExternalOutput").ap()
    scratch = {n: nc.dram_tensor(f"scratch_{n}", shape, F32, kind=KIND).ap()
               for n, shape in (("proj", (N_IN, P, S)), ("y", (N_Y, P, S)), ("kv", (2 * KB, P, M)), ("h", (S, D)))}
    layer(nc, a, out, scratch)
    r = run_bass_kernel_spmd(nc, [arrays], core_ids=[0])
    return r.results[0]["out"].reshape(1, S, D)


KIND = "Internal"
```
